# Optimizing a Trainium2 kernel written in Bass

```python
import math
import jax, jax.numpy as jnp
from jax import lax
import numpy as np

D_MODEL = 2048
BATCH = 1
SEQ = 1024
DEPTH = 1
DEC_BATCH = 1
DEC_SEQ = 64
PAST_LEN = 128

CHUNK = 64
D_SSM = D_MODEL // 2
D_ATT = D_MODEL // 2
D_INNER = D_SSM + D_ATT
SSM_GROUP = 16
N_GROUPS = D_SSM // SSM_GROUP
STATE_DIM = 64
HEAD_DIM = 128
N_HEADS = D_ATT // HEAD_DIM
Q_BLOCK = 128
D_PROJ = 2 * D_SSM + 4 * D_ATT + N_HEADS
EPS = 1e-6
F_BIAS_INIT = 3.0
DT_MIN = 0.001
DT_MAX = 0.1

kernel_name = "hymba_s5_fox_streaming_encoder"

def _rmsnorm(x, g):
    xf = x.astype(jnp.float32)
    y = xf * lax.rsqrt(jnp.mean(xf * xf, axis=-1, keepdims=True) + EPS)
    return (y * g.astype(jnp.float32)).astype(x.dtype)

def _s5_scan(u, log_dt, a_re, a_im, b_re, b_im, c_re, c_im, d, h0_re, h0_im):
    f32 = jnp.float32
    bsz, L, _ = u.shape
    uf = u.astype(f32).reshape(bsz, L, N_GROUPS, SSM_GROUP)
    dt = jnp.exp(log_dt.astype(f32))[:, None]
    ar = a_re.astype(f32)
    ai = a_im.astype(f32)
    mag = jnp.exp(ar * dt)
    abar_re = mag * jnp.cos(ai * dt)
    abar_im = mag * jnp.sin(ai * dt)
    den = ar * ar + ai * ai
    nr = abar_re - 1.0
    ni = abar_im
    coef_re = (nr * ar + ni * ai) / den
    coef_im = (ni * ar - nr * ai) / den
    bu_re = jnp.einsum('blgc,gpc->blgp', uf, b_re.astype(f32))
    bu_im = jnp.einsum('blgc,gpc->blgp', uf, b_im.astype(f32))
    bb_re = coef_re * bu_re - coef_im * bu_im
    bb_im = coef_re * bu_im + coef_im * bu_re
    if h0_re is not None:
        h0r = h0_re.astype(f32)
        h0i = h0_im.astype(f32)
        bb_re = bb_re.at[:, 0].add(abar_re * h0r - abar_im * h0i)
        bb_im = bb_im.at[:, 0].add(abar_re * h0i + abar_im * h0r)
    a_re_t = jnp.broadcast_to(abar_re, bb_re.shape)
    a_im_t = jnp.broadcast_to(abar_im, bb_im.shape)

    def combine(e1, e2):
        a1r, a1i, b1r, b1i = e1
        a2r, a2i, b2r, b2i = e2
        return (a2r * a1r - a2i * a1i,
                a2r * a1i + a2i * a1r,
                a2r * b1r - a2i * b1i + b2r,
                a2r * b1i + a2i * b1r + b2i)

    _, _, h_re, h_im = lax.associative_scan(combine, (a_re_t, a_im_t, bb_re, bb_im), axis=1)
    y = (jnp.einsum('blgp,gcp->blgc', h_re, c_re.astype(f32))
         - jnp.einsum('blgp,gcp->blgc', h_im, c_im.astype(f32))
         + d.astype(f32) * uf)
    return y.reshape(bsz, L, D_SSM), h_re[:, -1], h_im[:, -1]

def _fox_block(q, cq, qpos, k, v, ck, kpos):
    s = jnp.einsum('bqhd,bkhd->bhqk', q, k).astype(jnp.float32) * (HEAD_DIM ** -0.5)
    s = s + (jnp.transpose(cq, (0, 2, 1))[..., :, None] - jnp.transpose(ck, (0, 2, 1))[..., None, :])
    mask = kpos[None, :] <= qpos[:, None]
    s = jnp.where(mask, s, -jnp.inf)
    p = jax.nn.softmax(s, axis=-1)
    return jnp.einsum('bhqk,bkhd->bqhd', p.astype(v.dtype), v)

def _layer(x, params, past):
    (g, w_in, b_f, qg, kg, log_dt, a_re, a_im, b_re, b_im, c_re, c_im, d,
     w_glu, b_glu, ssm_ng, att_ng, w_out) = params
    bsz, L, _ = x.shape
    h = _rmsnorm(x, g)
    proj = h @ w_in
    splits = [D_SSM, 2 * D_SSM, 2 * D_SSM + D_ATT, 2 * D_SSM + 2 * D_ATT,
              2 * D_SSM + 3 * D_ATT, 2 * D_SSM + 4 * D_ATT]
    u, z_ssm, q, k, v, z_att, f_pre = jnp.split(proj, splits, axis=-1)

    if past is None:
        h0_re, h0_im = None, None
    else:
        h0_re, h0_im = past[3], past[4]
    y_ssm, hT_re, hT_im = _s5_scan(u, log_dt, a_re, a_im, b_re, b_im, c_re, c_im, d, h0_re, h0_im)
    zs = jax.nn.gelu(y_ssm, approximate=False)
    y_ssm = zs * jax.nn.sigmoid(zs @ w_glu.astype(jnp.float32) + b_glu.astype(jnp.float32))
    y_ssm = y_ssm * jax.nn.silu(z_ssm.astype(jnp.float32))
    y_ssm = _rmsnorm(y_ssm, ssm_ng).astype(x.dtype)

    q = _rmsnorm(q.reshape(bsz, L, N_HEADS, HEAD_DIM), qg)
    k = _rmsnorm(k.reshape(bsz, L, N_HEADS, HEAD_DIM), kg)
    v = v.reshape(bsz, L, N_HEADS, HEAD_DIM)
    logf = jax.nn.log_sigmoid(f_pre.astype(jnp.float32) + b_f.astype(jnp.float32))
    if past is None:
        k_all, v_all, logf_all = k, v, logf
        offset = 0
    else:
        k_past, v_past, logf_past = past[0], past[1], past[2]
        k_all = jnp.concatenate([k_past, k.astype(k_past.dtype)], axis=1)
        v_all = jnp.concatenate([v_past, v.astype(v_past.dtype)], axis=1)
        logf_all = jnp.concatenate([logf_past.astype(jnp.float32), logf], axis=1)
        offset = k_past.shape[1]
    c_all = jnp.cumsum(logf_all, axis=1)
    cq = c_all[:, offset:]
    S = k_all.shape[1]
    kpos = jnp.arange(S, dtype=jnp.int32)
    qpos = offset + jnp.arange(L, dtype=jnp.int32)
    q = q.astype(k_all.dtype)
    if L <= Q_BLOCK:
        o = _fox_block(q, cq, qpos, k_all, v_all, c_all, kpos)
    else:
        nblk = L // Q_BLOCK
        qb = jnp.transpose(q.reshape(bsz, nblk, Q_BLOCK, N_HEADS, HEAD_DIM), (1, 0, 2, 3, 4))
        cqb = jnp.transpose(cq.reshape(bsz, nblk, Q_BLOCK, N_HEADS), (1, 0, 2, 3))
        qposb = qpos.reshape(nblk, Q_BLOCK)
        ob = lax.map(lambda a: _fox_block(a[0], a[1], a[2], k_all, v_all, c_all, kpos), (qb, cqb, qposb))
        o = jnp.transpose(ob, (1, 0, 2, 3, 4))
    o = o.reshape(bsz, L, D_ATT).astype(jnp.float32)
    y_att = _rmsnorm(o * jax.nn.silu(z_att.astype(jnp.float32)), att_ng).astype(x.dtype)

    y = jnp.concatenate([y_ssm, y_att], axis=-1)
    x = x + (y @ w_out).astype(x.dtype)
    return x, (k, v, logf, hT_re, hT_im)

def setup_inputs(seed: int = 0) -> dict:
    key = jax.random.key(seed)
    ks = jax.random.split(key, 32)
    f32 = jnp.float32
    nrm = lambda k, shape, scale: jax.random.normal(k, shape, f32) * scale
    x_prompt = nrm(ks[0], (BATCH, SEQ, D_MODEL), 1.0)
    x_sample = nrm(ks[1], (DEC_BATCH, DEC_SEQ, D_MODEL), 1.0)
    cache_k = nrm(ks[2], (DEPTH, DEC_BATCH, PAST_LEN, N_HEADS, HEAD_DIM), 1.0)
    cache_v = nrm(ks[3], (DEPTH, DEC_BATCH, PAST_LEN, N_HEADS, HEAD_DIM), 1.0)
    cache_logf = jax.nn.log_sigmoid(F_BIAS_INIT + nrm(ks[4], (DEPTH, DEC_BATCH, PAST_LEN, N_HEADS), 1.0))
    state_ssm_re = nrm(ks[5], (DEPTH, DEC_BATCH, N_GROUPS, STATE_DIM), 0.1)
    state_ssm_im = nrm(ks[6], (DEPTH, DEC_BATCH, N_GROUPS, STATE_DIM), 0.1)
    norm_gain = 1.0 + nrm(ks[7], (DEPTH, D_MODEL), 0.01)
    w_in = nrm(ks[8], (DEPTH, D_MODEL, D_PROJ), D_MODEL ** -0.5)
    b_f = F_BIAS_INIT + nrm(ks[9], (DEPTH, N_HEADS), 0.1)
    q_norm_gain = 1.0 + nrm(ks[10], (DEPTH, HEAD_DIM), 0.01)
    k_norm_gain = 1.0 + nrm(ks[11], (DEPTH, HEAD_DIM), 0.01)
    ssm_log_dt = jax.random.uniform(ks[12], (DEPTH, N_GROUPS), f32, math.log(DT_MIN), math.log(DT_MAX))
    n_idx = jnp.arange(STATE_DIM, dtype=f32)
    ssm_a_re = -0.5 + nrm(ks[13], (DEPTH, N_GROUPS, STATE_DIM), 0.01)
    ssm_a_im = math.pi * n_idx + nrm(ks[14], (DEPTH, N_GROUPS, STATE_DIM), 0.01)
    ssm_b_re = nrm(ks[15], (DEPTH, N_GROUPS, STATE_DIM, SSM_GROUP), (2 * SSM_GROUP) ** -0.5)
    ssm_b_im = nrm(ks[16], (DEPTH, N_GROUPS, STATE_DIM, SSM_GROUP), (2 * SSM_GROUP) ** -0.5)
    ssm_c_re = nrm(ks[17], (DEPTH, N_GROUPS, SSM_GROUP, STATE_DIM), STATE_DIM ** -0.5)
    ssm_c_im = nrm(ks[18], (DEPTH, N_GROUPS, SSM_GROUP, STATE_DIM), STATE_DIM ** -0.5)
    ssm_d = nrm(ks[19], (DEPTH, N_GROUPS, SSM_GROUP), 1.0)
    w_glu = nrm(ks[20], (DEPTH, D_SSM, D_SSM), D_SSM ** -0.5)
    b_glu = nrm(ks[21], (DEPTH, D_SSM), 0.01)
    ssm_out_norm = 1.0 + nrm(ks[22], (DEPTH, D_SSM), 0.01)
    att_out_norm = 1.0 + nrm(ks[23], (DEPTH, D_ATT), 0.01)
    w_out = nrm(ks[24], (DEPTH, D_INNER, D_MODEL), 0.5 * D_INNER ** -0.5)
    return {"x_prompt": x_prompt, "x_sample": x_sample,
            "cache_k": cache_k, "cache_v": cache_v, "cache_logf": cache_logf,
            "state_ssm_re": state_ssm_re, "state_ssm_im": state_ssm_im,
            "norm_gain": norm_gain, "w_in": w_in, "b_f": b_f,
            "q_norm_gain": q_norm_gain, "k_norm_gain": k_norm_gain,
            "ssm_log_dt": ssm_log_dt, "ssm_a_re": ssm_a_re, "ssm_a_im": ssm_a_im,
            "ssm_b_re": ssm_b_re, "ssm_b_im": ssm_b_im, "ssm_c_re": ssm_c_re, "ssm_c_im": ssm_c_im,
            "ssm_d": ssm_d, "w_glu": w_glu, "b_glu": b_glu,
            "ssm_out_norm": ssm_out_norm, "att_out_norm": att_out_norm, "w_out": w_out}

def reference(x_prompt, x_sample, cache_k, cache_v, cache_logf, state_ssm_re, state_ssm_im,
              norm_gain, w_in, b_f, q_norm_gain, k_norm_gain, ssm_log_dt, ssm_a_re, ssm_a_im,
              ssm_b_re, ssm_b_im, ssm_c_re, ssm_c_im, ssm_d, w_glu, b_glu,
              ssm_out_norm, att_out_norm, w_out):
    xp, xs = x_prompt, x_sample
    kp_l, vp_l, fp_l, hrp_l, hip_l = [], [], [], [], []
    ks_l, vs_l, fs_l, hrs_l, his_l = [], [], [], [], []
    for l in range(DEPTH):
        params = (norm_gain[l], w_in[l], b_f[l], q_norm_gain[l], k_norm_gain[l], ssm_log_dt[l],
                  ssm_a_re[l], ssm_a_im[l], ssm_b_re[l], ssm_b_im[l], ssm_c_re[l], ssm_c_im[l],
                  ssm_d[l], w_glu[l], b_glu[l], ssm_out_norm[l], att_out_norm[l], w_out[l])
        xp, (kp, vp, fp, hrp, hip) = _layer(xp, params, None)
        xs, (kk, vv, ff, hrs, his) = _layer(
            xs, params, (cache_k[l], cache_v[l], cache_logf[l], state_ssm_re[l], state_ssm_im[l]))
        kp_l.append(kp); vp_l.append(vp); fp_l.append(fp); hrp_l.append(hrp); hip_l.append(hip)
        ks_l.append(kk); vs_l.append(vv); fs_l.append(ff); hrs_l.append(hrs); his_l.append(his)
    return (xp, xs,
            jnp.stack(kp_l), jnp.stack(vp_l), jnp.stack(fp_l), jnp.stack(hrp_l), jnp.stack(hip_l),
            jnp.stack(ks_l), jnp.stack(vs_l), jnp.stack(fs_l), jnp.stack(hrs_l), jnp.stack(his_l))


_drawn_inputs = setup_inputs


def setup_inputs(seed=0):
    import zlib

    import numpy as np

    out = dict(_drawn_inputs(seed))
    spreads = {}
    factors = {'norm_gain': 5.621,
     'q_norm_gain': 8.0,
     'k_norm_gain': 5.226,
     'ssm_a_re': 62.222,
     'b_glu': 35.35,
     'ssm_out_norm': 200.0,
     'att_out_norm': 200.0,
     'cache_k': 2.982,
     'cache_v': 2.909,
     'cache_logf': 8.0,
     'ssm_c_re': 3.374,
     'ssm_c_im': 3.34}
    for name, (base, spread) in spreads.items():
        noise = np.random.default_rng([zlib.crc32(name.encode()), seed]).standard_normal(out[name].shape)
        drawn = base * np.exp(spread * noise) if base else spread * noise
        out[name] = __import__('jax').numpy.asarray(drawn.astype(out[name].dtype))
    for name, factor in factors.items():
        out[name] = (out[name] * factor).astype(out[name].dtype)
    return out
```

```python
import math
from contextlib import ExitStack

import concourse.bass as bass
import concourse.mybir as mybir

D_MODEL, SEQ, DEC, PAST = 2048, 1024, 64, 128
D_SSM = D_ATT = 1024
NH, HD = 8, 128
NG, GC, NP = 64, 16, 64
D_PROJ = 2 * D_SSM + 4 * D_ATT + NH
EPS = 1e-6
P = 128
TOK = SEQ + DEC
KT = D_MODEL // P
TT = SEQ // P + 1
L = 8
NB = SEQ // L
NBS = DEC // L
SC = NB + 1 + NBS
HC = SC + 1
RAW, SPL = 4, 4
PIECE = 2
NLV = 7
AR, AI, WR, WI, MG, H0 = 0, 9, 18, 25, 32, 33
NPR = 35
PKW = NPR * 4 + 4 * 4 * GC + 1
CW = 384
COLS = ((0, CW), (CW, CW), (2 * CW, TOK - 2 * CW))
MAGIC = 12582912.0
NEG = -1e30


def build_kernel(nc, x_prompt, x_sample, cache_k, cache_v, cache_logf, state_ssm_re, state_ssm_im,
                 norm_gain, w_in, b_f, q_norm_gain, k_norm_gain, ssm_log_dt, ssm_a_re, ssm_a_im,
                 ssm_b_re, ssm_b_im, ssm_c_re, ssm_c_im, ssm_d, w_glu, b_glu,
                 ssm_out_norm, att_out_norm, w_out,
                 y_prompt, y_sample, k_prompt, v_prompt, logf_prompt, hre_prompt, him_prompt,
                 k_sample, v_sample, logf_sample, hre_sample, him_sample):
    f32, r32, bf16, i32 = mybir.dt.float32, mybir.dt.float32r, mybir.dt.bfloat16, mybir.dt.int32
    ALU, ACT, AX = mybir.AluOpType, mybir.ActivationFunctionType, mybir.AxisListType
    ds = bass.ds
    V, S, G, T = nc.vector, nc.scalar, nc.gpsimd, nc.tensor
    ctx = ExitStack()
    sems, phase = {}, [0]

    def sem(name):
        if name not in sems:
            sems[name] = nc.alloc_semaphore(name=f"{name}_{phase[0]}")
        return sems[name]

    def stand(eng, name):
        eng.sem_inc(sem("stand_" + name), 1)

    def free_semaphores():
        nc.clear_and_free_semaphores(list(sems.values()))
        nc.all_engine_barrier()
        sems.clear()
        phase[0] += 1

    def pool_of(stack):
        def sb(name, shape, dt=f32):
            return stack.enter_context(nc.sbuf_tensor(name, shape, dt))
        return sb

    class Order:

        def __init__(self, eng, name):
            self.eng, self.sem, self.base, self.n = eng, sem(name), 0, 0

        def step(self, ins):
            ins.then_inc(self.sem, 1)
            self.n += 1
            return self.base + self.n

        def then(self, ins):
            self.eng.wait_ge(self.sem, self.step(ins))

        def enter(self, it, per):
            self.start, self.per = self.n, per
            self.base = it * per

        def leave(self, count):
            assert self.n - self.start == self.per, ("steps", self.sem, self.n - self.start, self.per)
            self.base, self.n = 0, self.start + self.per * count

    def scratch(name, shape):
        return nc.dram_tensor(name, shape, f32).ap()

    pk_s = scratch("pk_s", [P, 8 * PKW])
    kpad_s = scratch("kpad_s", [P, 240])
    zg_s = scratch("zg_s", [D_SSM, TOK])
    zs_s = scratch("zs_s", [D_SSM, TOK])
    ya_s = scratch("ya_s", [D_ATT, TOK])
    ys_s = scratch("ys_s", [D_SSM, TOK])
    nc_s = scratch("nc_s", [NH, SEQ + PAST + DEC])
    sqa_s = scratch("sqa_s", [P, TOK])
    sqs_s = scratch("sqs_s", [P, TOK])
    w_in_v = w_in[0].rearrange("(k p) n -> p k n", p=P)
    w_glu_v = w_glu[0].rearrange("(k p) n -> p k n", p=P)
    w_out_v = w_out[0].rearrange("(k p) n -> p k n", p=P)

    with ctx:
        sb = pool_of(ctx)
        ident = sb("ident", [P, P])
        identb = sb("identb", [P, P], bf16)
        maskb = sb("maskb", [P, P], bf16)
        ones = sb("ones", [P, P])
        delta = sb("delta", [P, GC])
        vec = sb("vec", [P, 34])
        epsc = sb("epsc", [P, 1])
        wraw = sb("wraw", [P, RAW, PIECE, P])
        whi = sb("whi", [P, SPL, PIECE, P], r32)
        wlo = sb("wlo", [P, SPL, PIECE, P], r32)
        GB = ctx.enter_context(nc.psum_tensor("GB", [P, 3 * 512], f32))
        TB = ctx.enter_context(nc.psum_tensor("TB", [P, 5 * 512], f32))

        def group(bank, b, p=slice(0, P)):
            return bank[p, 512 * b:512 * b + COLS[b][1]]

        def cols(a, b):
            return a[:, COLS[b][0]:COLS[b][0] + COLS[b][1]]

        def halves(bank, a, p=slice(0, P)):
            return ((bank[p, 0:1024].rearrange("p (b c) -> p b c", b=2)[:, :, 0:CW],
                     a[:, 0:2 * CW].rearrange("p (b c) -> p b c", b=2)), (group(bank, 2, p), cols(a, 2)))

        class Weights:

            def __init__(self, tag, view, xh, xl):
                self.view, self.xh, self.xl, self.tag = view, xh, xl, tag
                self.w_in = [sem(f"{tag}_w_in{i}") for i in range(RAW)]
                self.hi, self.lo, self.mm = sem(f"{tag}_w_hi"), sem(f"{tag}_w_lo"), sem(f"{tag}_w_mm")

            def load(self, eng, m, s, col, k):
                eng.wait_ge(self.lo, m + 1)
                eng.dma_start(wraw[:, s % RAW], self.view[:, k:k + PIECE, ds(col, P)]).then_inc(self.w_in[s % RAW], 16)

            def split_hi(self, m, s, loads):
                S.wait_ge(self.w_in[s % RAW], 16 * loads)
                S.wait_ge(self.mm, m + 1)
                S.copy(whi[:, s % SPL], wraw[:, s % RAW]).then_inc(self.hi, 1)

            def split_lo(self, m, s):
                V.wait_ge(self.hi, m + 1)
                V.tensor_tensor(wlo[:, s % SPL], wraw[:, s % RAW], whi[:, s % SPL].bitcast(f32),
                                ALU.subtract).then_inc(self.lo, 1)

            def multiply(self, m, s, k, first, last, bank=GB):
                T.wait_ge(self.lo, m + 1 + RAW)
                for kk in range(PIECE):
                    for w, x in ((whi, self.xh), (whi, self.xl), (wlo, self.xh)):
                        for b, (c, n) in enumerate(COLS):
                            ins = T.matmul(bank[:, 512 * b:512 * b + n], w[:, s % SPL, kk], x[:, k + kk, c:c + n],
                                           start=first and kk == 0 and w is whi and x is self.xh,
                                           stop=last and kk == PIECE - 1 and w is wlo)
                ins.then_inc(self.mm, 1)

            def multiplied(self, m):
                return m + 1 + SPL

            def credit(self, which):
                if which == "pe":
                    T.sem_inc(self.mm, SPL)
                else:
                    V.sem_inc(self.lo, RAW)

        xs_stack = ctx.enter_context(ExitStack())
        XH = xs_stack.enter_context(nc.sbuf_tensor("XH", [P, KT, TOK], r32))
        XL = xs_stack.enter_context(nc.sbuf_tensor("XL", [P, KT, TOK], r32))
        with ExitStack() as st:
            sbp = pool_of(st)
            xt = sbp("xt", [P, 2, D_MODEL])
            gain = sbp("gain", [P, D_MODEL])
            junk = sbp("junk", [P, 1])
            ssq = sbp("ssq", [P, TT, 3])
            vin = sbp("vin", [34, P])
            pin = sbp("pin", [32, 5, P])
            ldt = sbp("ldt", [32, 2])
            cin = wraw[:].rearrange("p a b c -> p (a b c)").rearrange("p (i n) -> p i n", i=8)
            braw = sbp("braw", [P, 2, 512])
            prm = sbp("prm", [P, 5, 32])
            dtt = sbp("dtt", [P, 32])
            ath = sbp("ath", [P, 2, 32])
            arg = sbp("arg", [P, 14, 32])
            trg = sbp("trg", [P, 2, 14, 32])
            wk = sbp("wk", [P, 2, 14 * 32])
            mag = sbp("mag", [P, 9, 32])
            wki = sbp("wki", [P, 256], i32)
            cf = sbp("cf", [P, 8, 32])
            tmpb = (GB[:, 1024:1536], wk[:].rearrange("p a b -> p (a b)")[:, 0:512])
            pk = sbp("pk", [P, 8, PKW])
            ld_x = [sem("ld_x0"), sem("ld_x1")]
            ld_gain, ld_par, ld_c, st_pk = sem("ld_gain"), sem("ld_par"), sem("ld_c"), sem("st_pk")
            ident_done, par_t, par_ev = sem("ident_done"), sem("par_t"), sem("par_ev")
            sq_done, xs_done, x_t, x_hi, x_lo = (sem(n) for n in ("sq_done", "xs_done", "x_t", "x_hi", "x_lo"))
            sqrt_done, ssq_v, trg_in, trg_sin, c_t, pk_done = (
                sem(n) for n in ("sqrt_done", "ssq_v", "trg_in", "trg_sin", "c_t", "pk_done"))
            rows = [P] * (TT - 1) + [DEC]

            def pkv(row, n=1):
                return pk[:, :, 4 * row:4 * (row + n)].rearrange("p j (n q) -> p n j q", q=4)

            block = ctx.enter_context(ExitStack())
            with nc.Block() as block:
                @block.sync
                def _(sp):
                    def row128(a):
                        return a.rearrange("o (r p) -> (o r) p", p=P)
                    sp.dma_start(xt[:, 0], x_prompt[0, 0:P]).then_inc(ld_x[0], 16)
                    sp.dma_start(gain[:], norm_gain[0:1, :].to_broadcast([P, D_MODEL])).then_inc(ld_gain, 16)
                    for i, a in enumerate((ssm_a_re, ssm_a_im, state_ssm_re, state_ssm_im)):
                        a = a[0, 0] if len(a.shape) == 4 else a[0]
                        i = i if i < 2 else i + 1
                        sp.dma_start(pin[:, i].rearrange("r (g p) -> r g p", g=2),
                                     a.rearrange("(r g) p -> r g p", g=2)).then_inc(ld_par, 16)
                    sp.dma_start(ldt[:], ssm_log_dt[0].rearrange("(r g) -> r g", g=2)).then_inc(ld_par, 16)
                    sp.dma_start(vin[0:8], ssm_d[0].rearrange("(r g) c -> r (g c)", g=8)).then_inc(ld_par, 16)
                    sp.dma_start(vin[8:16], row128(b_glu)).then_inc(ld_par, 16)
                    sp.dma_start(vin[16:24], row128(ssm_out_norm)).then_inc(ld_par, 16)
                    sp.dma_start(vin[24:32], row128(att_out_norm)).then_inc(ld_par, 16)
                    sp.dma_start(vin[32:33], q_norm_gain).then_inc(ld_par, 16)
                    sp.dma_start(vin[33:34], k_norm_gain).then_inc(ld_par, 16)
                    for i, a in enumerate((ssm_c_re, ssm_c_im)):
                        for q in range(4):
                            for g in range(2):
                                src = a[0].rearrange("(q r g) c p -> q g r c p", q=4, g=2)[q, g]
                                sp.dma_start(cin[:, 4 * i + q, g * NP:(g + 1) * NP],
                                             src).then_inc(ld_c, 16)
                    for i, a in enumerate((ssm_b_re, ssm_b_im)):
                        for g in range(2):
                            sp.dma_start(braw[g * NP:(g + 1) * NP, i].rearrange("p (r c) -> p r c", c=GC),
                                         a[0].rearrange("(r g) p c -> g p r c", g=2)[g]).then_inc(ld_c, 16)
                    for m in range(1, TT):
                        if m >= 2:
                            sp.wait_ge(x_t, 4 * (m - 1))
                        src = x_prompt[0, m * P:(m + 1) * P] if m < TT - 1 else x_sample[0]
                        sp.dma_start(xt[0:rows[m], m % 2], src).then_inc(ld_x[m % 2], 16)
                    sp.wait_ge(pk_done, 1)
                    sp.dma_start(pk_s, pk[:].rearrange("p a b -> p (a b)")).then_inc(st_pk, 16)
                    sp.wait_ge(st_pk, 16)

                @block.gpsimd
                def _(pool):
                    o = Order(pool, "pool_order")
                    G.memset(junk[:], 0.0)
                    G.memset(epsc[:], EPS)
                    o.then(G.memset(ident[:], 0.0))
                    o.then(G.affine_select(out=ident[:], in_=ident[:], compare_op=ALU.not_equal, fill=1.0, base=0,
                                           pattern=[[-1, P]], channel_multiplier=1))
                    o.then(G.memset(ones[:], 1.0))
                    o.then(G.memset(identb[:], 0.0))
                    G.affine_select(out=maskb[:], in_=identb[:], compare_op=ALU.is_ge, fill=NEG, base=0,
                                    pattern=[[-1, P]], channel_multiplier=1).then_inc(ident_done, 1)
                    pool.wait_ge(ident_done, 1)
                    G.tensor_copy(identb[:], ident[:]).then_inc(ident_done, 1)

                @block.scalar
                def _(act):
                    act.wait_ge(ident_done, 2)
                    o = Order(act, "act_order")

                    def x_square(m):
                        act.wait_ge(ld_x[m % 2], 16 * (m // 2 + 1))
                        n = rows[m]
                        for h in range(2):
                            last = S.activation(GB[0:n, 0:1024], xt[0:n, m % 2, 1024 * h:1024 * (h + 1)], ACT.Square,
                                                accum_out=ssq[0:n, m, h:h + 1])
                            if h == 0:
                                o.then(last)
                        last.then_inc(sq_done, 1)
                        act.wait_ge(ssq_v, m + 1)
                        S.activation(ssq[0:n, m, 2:3], ssq[0:n, m, 0:1], ACT.Sqrt).then_inc(sqrt_done, 1)

                    def x_split(m):
                        n = rows[m]
                        for b in range(4):
                            act.wait_ge(x_t, 4 * m + b + 1)
                            S.copy(XH[:, 4 * b:4 * b + 4, m * P:m * P + n],
                                   TB[:, b * 512:(b + 1) * 512].rearrange("p (k t) -> p k t", k=4)[:, :, 0:n]
                                   ).then_inc(x_hi, 1)
                    x_square(0)
                    for m in range(TT):
                        if m + 1 < TT:
                            x_square(m + 1)
                        x_split(m)
                        if m == 2:
                            act.wait_ge(trg_in, 1)
                            S.activation(trg[:].rearrange("p a b c -> p (a b c)"),
                                         trg[:].rearrange("p a b c -> p (a b c)"), ACT.Sin).then_inc(trg_sin, 1)

                @block.tensor
                def _(pe):
                    pe.wait_ge(ident_done, 2)
                    pe.wait_ge(ld_par, 16 * 11)
                    dt_bc = sem("dt_bc")
                    pe.wait_ge(dt_bc, 1)
                    T.transpose(TB[:, 4 * 512:4 * 512 + 34], vin[:], ident[0:34, 0:34])
                    for i in range(5):
                        ins = T.transpose(TB[:, 4 * 512 + 64 + 32 * i:4 * 512 + 96 + 32 * i], pin[:, i], ident[0:32, 0:32])
                    ins.then_inc(par_t, 1)

                    def tiles(m):
                        n = rows[m]
                        pe.wait_ge(xs_done, m + 1)
                        for b in range(4):
                            if m:
                                pe.wait_ge(x_lo, 4 * (m - 1) + b + 1)
                            for k in range(4):
                                c = b * 512 + k * P
                                ins = T.transpose(TB[:, c:c + n], xt[0:n, m % 2, (4 * b + k) * P:(4 * b + k + 1) * P],
                                                  ident[0:n, 0:n])
                            ins.then_inc(x_t, 1)
                    for m in range(TT):
                        tiles(m)
                        if m == 0:
                            pe.wait_ge(ld_c, 16 * 20)
                            for i in range(8):
                                if i == 4:
                                    pe.wait_ge(par_ev, 3)
                                elif i == 0:
                                    pe.wait_ge(par_ev, 2)
                                ins = T.transpose(TB[:, 4 * 512 + (i % 4) * P:4 * 512 + (i % 4 + 1) * P], cin[:, i], ident[:])
                                if i % 4 == 3:
                                    ins.then_inc(c_t, 1)

                @block.vector
                def _(dve):
                    o = Order(dve, "dve_order")
                    dt_bc = sem("dt_bc")

                    def x_scale(m):
                        n = rows[m]
                        dve.wait_ge(sq_done, m + 1)
                        o.then(V.tensor_tensor(ssq[0:n, m, 0:1], ssq[0:n, m, 0:1], ssq[0:n, m, 1:2], ALU.add))
                        V.tensor_scalar(ssq[0:n, m, 0:1], ssq[0:n, m, 0:1], 1.0 / D_MODEL, EPS, ALU.mult, ALU.add
                                        ).then_inc(ssq_v, 1)
                        dve.wait_ge(sqrt_done, m + 1)
                        v, y, t = ssq[0:n, m, 0:1], ssq[0:n, m, 1:2], ssq[0:n, m, 2:3]
                        o.then(V.reciprocal(y, t))
                        o.then(V.tensor_tensor(t, y, y, ALU.mult))
                        o.then(V.scalar_tensor_tensor(t, t, -0.5, v, ALU.mult, ALU.mult))
                        o.then(V.scalar_tensor_tensor(y, t, 1.5, y, ALU.add, ALU.mult))
                        if m == 0:
                            dve.wait_ge(ld_gain, 16)
                        V.scalar_tensor_tensor(xt[0:n, m % 2], xt[0:n, m % 2], ssq[0:n, m, 1:2], gain[0:n],
                                               ALU.mult, ALU.mult).then_inc(xs_done, 1)

                    def x_rest(m):
                        n = rows[m]
                        for b in range(4):
                            dve.wait_ge(x_hi, 4 * m + b + 1)
                            tb = TB[:, b * 512:(b + 1) * 512].rearrange("p (k t) -> p k t", k=4)[:, :, 0:n]
                            V.tensor_tensor(XL[:, 4 * b:4 * b + 4, m * P:m * P + n], tb,
                                            XH[:, 4 * b:4 * b + 4, m * P:m * P + n].bitcast(f32),
                                            ALU.subtract).then_inc(x_lo, 1)

                    def exp_poly(out, x, n):
                        t, r = wk[:, 0, 0:n], wk[:, 1, 0:n]
                        o.then(V.tensor_scalar(x, x, -87.0, 88.0, ALU.max, ALU.min))
                        o.then(V.tensor_scalar(t, x, 1.0 / math.log(2.0), MAGIC, ALU.mult, ALU.add))
                        o.then(V.tensor_scalar(t, t, -MAGIC, None, ALU.add))
                        o.then(V.scalar_tensor_tensor(r, t, -0.693359375, x, ALU.mult, ALU.add))
                        o.then(V.scalar_tensor_tensor(r, t, 2.12194440e-4, r, ALU.mult, ALU.add))
                        o.then(V.tensor_scalar(out, r, 1.0 / 5040, None, ALU.mult))
                        for c in (1.0 / 720, 1.0 / 120, 1.0 / 24, 1.0 / 6, 0.5, 1.0):
                            o.then(V.scalar_tensor_tensor(out, out, c, r, ALU.add, ALU.mult))
                        o.then(V.tensor_scalar(out, out, 1.0, None, ALU.add))
                        o.then(V.tensor_scalar(wki[:, 0:n], t, 127.0, 8388608.0, ALU.add, ALU.mult))
                        o.then(V.tensor_tensor(out, out, wki[:, 0:n].bitcast(f32), ALU.mult))

                    dve.wait_ge(ld_par, 16 * 11)
                    V.tensor_copy(pin[:, 2].rearrange("r (g p) -> r g p", g=2),
                                  ldt[:].unsqueeze(2).to_broadcast([32, 2, NP])).then_inc(dt_bc, 1)
                    dve.wait_ge(ident_done, 2)
                    V.tensor_reduce(delta[:], ident[:].rearrange("p (g c) -> p c g", c=GC), AX.X, ALU.add)
                    x_scale(0)
                    dve.wait_ge(par_t, 1)
                    V.tensor_copy(vec[:], TB[:, 4 * 512:4 * 512 + 34]).then_inc(par_ev, 1)
                    V.tensor_copy(prm[:].rearrange("p a b -> p (a b)"), TB[:, 4 * 512 + 64:4 * 512 + 224]).then_inc(par_ev, 1)
                    dve.wait_ge(par_ev, 2)
                    x_scale(1)
                    x_rest(0)
                    dve.wait_ge(c_t, 1)
                    cre = pk[:, :, NPR * 4 + 128:NPR * 4 + 192]
                    cim = pk[:, :, NPR * 4 + 192:NPR * 4 + 256]
                    V.tensor_copy(cre, TB[:, 4 * 512:5 * 512].rearrange("p (j c) -> p j c", j=8)).then_inc(par_ev, 1)
                    dve.wait_ge(c_t, 2)
                    o.then(V.tensor_copy(cim, TB[:, 4 * 512:5 * 512].rearrange("p (j c) -> p j c", j=8)))
                    x_scale(2)
                    x_rest(1)
                    exp_poly(dtt[:], prm[:, 2], 32)
                    o.then(V.tensor_tensor(ath[:], prm[:, 0:2], dtt[:].unsqueeze(1).to_broadcast([P, 2, 32]), ALU.mult))
                    for k in range(14):
                        f = float(k + 1) if k < 8 else float(L << (k - 7))
                        last = o.step(V.tensor_scalar(arg[:, k], ath[:, 1], f, None, ALU.mult))
                    dve.wait_ge(o.sem, last)
                    argf = arg[:].rearrange("p a b -> p (a b)")
                    C1, C2, C3 = 6.28125, 1.9350051879882812e-3, 3.0199159819567e-7
                    for i, quarter in ((0, 0.25), (1, 0.0)):
                        t = wk[:, i]
                        r = trg[:, i].rearrange("p a b -> p (a b)")
                        o.then(V.tensor_scalar(t, argf, 1.0 / (2 * math.pi), quarter, ALU.mult, ALU.add))
                        o.then(V.tensor_scalar(t, t, MAGIC, None, ALU.add))
                        o.then(V.tensor_scalar(t, t, -MAGIC, None, ALU.add))
                        o.then(V.scalar_tensor_tensor(r, t, -C1, argf, ALU.mult, ALU.add))
                        o.then(V.scalar_tensor_tensor(r, t, -C2, r, ALU.mult, ALU.add))
                        o.then(V.scalar_tensor_tensor(r, t, -C3, r, ALU.mult, ALU.add))
                        if quarter:
                            o.then(V.tensor_scalar(r, r, math.pi / 2, None, ALU.add))
                        ins = V.tensor_scalar(r, r, -3.1415925, 3.1415925, ALU.max, ALU.min)
                        if quarter:
                            o.then(ins)
                        else:
                            ins.then_inc(trg_in, 1)
                    dve.wait_ge(trg_in, 1)
                    x_scale(3)
                    x_rest(2)
                    for k in range(8):
                        last = o.step(V.tensor_scalar(mag[:, k + 1], ath[:, 0], float(k + 1), None, ALU.mult))
                    dve.wait_ge(o.sem, last)
                    xm = tmpb[0][:, 0:256]
                    o.then(V.tensor_copy(xm, mag[:, 1:9].rearrange("p a b -> p (a b)")))
                    exp_poly(mag[:, 1:9].rearrange("p a b -> p (a b)"), xm, 256)
                    x_scale(4)
                    x_rest(3)
                    dve.wait_ge(trg_sin, 1)
                    o.then(V.memset(pkv(AR), 1.0))
                    o.then(V.memset(pkv(AI), 0.0))

                    def as_jq(a):
                        return a.rearrange("p n (j q) -> p n j q", q=4)
                    for k in range(8):
                        V.tensor_tensor(pkv(AR + 1 + k), as_jq(mag[:, k + 1:k + 2]), as_jq(trg[:, 0, k:k + 1]), ALU.mult)
                        last = o.step(V.tensor_tensor(pkv(AI + 1 + k), as_jq(mag[:, k + 1:k + 2]),
                                                      as_jq(trg[:, 1, k:k + 1]), ALU.mult))
                    for lv in range(NLV):
                        o.step(V.tensor_copy(pkv(WR + lv), as_jq(trg[:, 0, 7 + lv:8 + lv])))
                        o.step(V.tensor_scalar(pkv(WI + lv), as_jq(trg[:, 1, 7 + lv:8 + lv]), -1.0, None, ALU.mult))
                    o.step(V.tensor_copy(pkv(MG), as_jq(mag[:, 8:9])))
                    o.step(V.tensor_copy(pkv(H0), as_jq(prm[:, 3:4])))
                    last = o.step(V.tensor_copy(pkv(H0 + 1), as_jq(prm[:, 4:5])))
                    dve.wait_ge(o.sem, last)
                    dve.wait_ge(par_ev, 2)
                    o.then(V.tensor_copy(pk[:, :, PKW - 1], vec[:, 0:8]))
                    ar, ai = prm[:, 0], prm[:, 1]
                    nr, ni, den, t1 = cf[:, 0], cf[:, 1], cf[:, 2], cf[:, 3]
                    jq = lambda a: a.rearrange("p (j q) -> p j q", q=4)
                    o.then(V.tensor_scalar(jq(nr), pkv(AR + 1)[:, 0], -1.0, None, ALU.add))
                    o.then(V.tensor_copy(jq(ni), pkv(AI + 1)[:, 0]))
                    o.then(V.tensor_tensor(den, ar, ar, ALU.mult))
                    o.then(V.tensor_tensor(t1, ai, ai, ALU.mult))
                    o.then(V.tensor_tensor(den, den, t1, ALU.add))
                    o.then(V.reciprocal(den, den))
                    for i, (a, b, op) in enumerate(((nr, ni, ALU.add), (ni, nr, ALU.subtract))):
                        c = cf[:, 4 + i]
                        o.then(V.tensor_tensor(c, a, ar, ALU.mult))
                        o.then(V.tensor_tensor(t1, b, ai, ALU.mult))
                        o.then(V.tensor_tensor(c, c, t1, op))
                        o.then(V.tensor_tensor(c, c, den, ALU.mult))
                    x_scale(5)
                    x_rest(4)
                    dve.wait_ge(ld_c, 16 * 20)
                    v3 = lambda a: a.rearrange("p (r c) -> p r c", c=GC)
                    for i, op in ((0, ALU.subtract), (1, ALU.add)):
                        c0 = cf[:, 4].unsqueeze(2).to_broadcast([P, 32, GC])
                        c1 = cf[:, 5].unsqueeze(2).to_broadcast([P, 32, GC])
                        o.then(V.tensor_tensor(v3(tmpb[0]), v3(braw[:, i]), c0, ALU.mult))
                        o.then(V.tensor_tensor(v3(tmpb[1]), v3(braw[:, 1 - i]), c1, ALU.mult))
                        out = pk[:, :, NPR * 4 + 64 * i:NPR * 4 + 64 * (i + 1)]
                        ins = V.tensor_tensor(out, tmpb[0].rearrange("p (j c) -> p j c", j=8),
                                              tmpb[1].rearrange("p (j c) -> p j c", j=8), op)
                        if i == 0:
                            o.then(ins)
                        else:
                            ins.then_inc(pk_done, 1)
                    for m in range(5, TT):
                        if m + 1 < TT:
                            x_scale(m + 1)
                        x_rest(m)

        with ExitStack() as st:
            sbp = pool_of(st)
            U = sbp("U", [P, 8 * SC])
            Ug = U[:].rearrange("p (g c) -> p g c", c=SC)
            UZ = sbp("UZ", [P, TOK])
            UC = sbp("UC", [P, 1024])
            UCS = sbp("UCS", [P, 1024])
            SS = sbp("SS", [P, 2, 4 * SC])
            M1 = sbp("M1", [P, 2, 4 * SC])
            M2 = sbp("M2", [P, 2, 4 * SC])
            TR = sbp("TR", [P, 2, 4, SC])
            DC = sbp("DC", [P, 4, SC])
            H = sbp("H", [P, 8, HC])
            LS = sbp("LS", [P, 8, P])
            Q = sbp("Q", [P, 8, 9 * GC])
            MT = sbp("MT", [P, 8, P])
            KS = sbp("KS", [P, P])
            PJ = sbp("PJ", [P, PKW])
            BD = sbp("BD", [P, 8, 2 * GC])
            FB = sbp("FB", [P, 16])
            FS = sbp("FS", [16, P])
            flat = lambda a: a.rearrange("p a b -> p (a b)")
            GR = flat(M1[:])[:, 0:1024].rearrange("p (a q r c) -> p a q r c", a=2, q=4, r=L)
            GT = flat(SS[:])[:, 0:1024].rearrange("p (a q r c) -> p a q r c", a=2, q=4, r=L)
            Y = flat(SS[:]).rearrange("p (g c) -> p g c", c=SC)
            row = lambda r, n=1: PJ[:, 4 * r:4 * (r + n)].rearrange("p (n q) -> p n q", q=4)
            bc_ = lambda i: PJ[:, NPR * 4 + 64 * i:NPR * 4 + 64 * (i + 1)].rearrange("p (q c) -> p q c", c=GC)
            W = Weights("ssm", w_in_v, XH, XL)
            NPC = 2 * KT // PIECE
            names = ("pj_in", "g_ready", "bd_ready", "q_ready", "t_ready", "ls_mm", "k_mm", "ls_act", "ls_dve", "ks_ready",
                     "kpad_out", "mt_in", "ga", "gd", "st1_mm", "st1_act", "st1_dve", "st2_mm", "st2_act", "st2_dve",
                     "s_mm", "s_act", "m1_done", "m2_done", "gre_done", "gim_done", "scan_done", "p1_done", "p2_done",
                     "h_dve", "h_pool", "y_mm", "y_act", "y_dve", "yt_mm", "yt_act", "yt_dve", "z_mm", "z_act", "zg_out", "zs_out",
                     "fb_ready", "fin_mm", "fin_ev", "fin_out", "dec_ready", "zero_done")
            e = {n: sem("ssm_" + n) for n in names}

            with nc.Block() as block:
                @block.sync
                def _(sp):
                    with sp.Fori(0, 8) as j:
                        for s in range(NPC):
                            col = j * P + (0 if s < NPC // 2 else D_SSM)
                            W.load(sp, j * NPC + s, s, col, PIECE * (s % (NPC // 2)))
                    for s in range(SPL):
                        W.load(sp, 8 * NPC + s, s, 0, 0)

                @block.scalar
                def _(act):
                    act.wait_ge(e["zero_done"], 1)
                    act.dma_start(kpad_s[:, 0:112], UC[:, 0:112]).then_inc(e["kpad_out"], 16)
                    for s in range(SPL):
                        W.split_hi(s, s, 1)
                    with act.Fori(0, 8) as j:
                        for s in range(NPC):
                            m = s + SPL
                            if s == 0:
                                act.wait_ge(e["g_ready"], j)
                                act.wait_ge(e["bd_ready"], j)
                                act.wait_ge(e["q_ready"], j)
                                act.wait_ge(e["ks_ready"], j)
                                act.wait_ge(e["dec_ready"], j)
                                act.wait_ge(e["s_act"], 4 * j)
                                act.dma_start(PJ[:], pk_s[:, ds(j * PKW, PKW)]).then_inc(e["pj_in"], 16)
                            W.split_hi(j * NPC + m, m, j * (NPC // RAW) + m // RAW + 1)
                            if s == 7:
                                act.wait_ge(W.mm, W.multiplied(j * NPC + s))
                                act.wait_ge(e["zg_out"], 16 * j)
                                S.copy(cols(UZ, 0), group(GB, 0))
                                S.copy(cols(UZ, 2), group(GB, 2)).then_inc(e["ga"], 1)
                                act.wait_ge(e["ls_mm"], j + 1)
                                S.copy(LS[:, 0:4], TB[:, 0:512].rearrange("p (a b) -> p a b", a=4)).then_inc(e["ls_act"], 1)
                            if s == 8:
                                act.wait_ge(e["ks_ready"], j + 1)
                                act.dma_start(kpad_s[:, 112:240], KS[:]).then_inc(e["kpad_out"], 16)
                                act.wait_ge(e["st1_mm"], j + 1)
                                S.copy(UC[:].rearrange("p (g r c) -> p r g c", g=8, r=L)[:, 0:4],
                                       TB[:, 3 * 512:4 * 512].rearrange("p (r g c) -> p r g c", r=4, g=8))
                                S.copy(UCS[0:8].rearrange("p (g r c) -> p r g c", g=8, r=L)[:, 0:4],
                                       TB[0:8, 0:512].rearrange("p (r g c) -> p r g c", r=4, g=8)).then_inc(e["st1_act"], 1)
                            if s == 9:
                                act.wait_ge(e["kpad_out"], 16 * (j + 2))
                                for r in range(L):
                                    act.dma_start(MT[r * GC:(r + 1) * GC],
                                                  kpad_s[:, GC * r:GC * r + P].rearrange("(g c) n -> c g n", g=8)
                                                  ).then_inc(e["mt_in"], 16)
                                act.wait_ge(e["st2_mm"], j + 1)
                                act.wait_ge(e["zs_out"], 16 * j)
                                S.copy(Ug[:, 0:4, 0:NB], TB[:, 2 * 512:3 * 512].rearrange("p (g c) -> p g c", g=4)
                                       ).then_inc(e["st2_act"], 1)
                            if s == 10:
                                act.wait_ge(e["s_mm"], j + 1)
                                for b in range(3):
                                    n = min(3, 8 - 3 * b) * SC
                                    S.copy(flat(SS[:])[:, 3 * b * SC:3 * b * SC + n], TB[:, 512 * b:512 * b + n]
                                           ).then_inc(e["s_act"], 1)
                                act.wait_ge(e["s_act"], 4 * j + 3)
                                S.copy(flat(SS[:]).rearrange("p (a c) -> p a c", c=SC)[:, :, NB],
                                       PJ[:, 4 * H0:4 * H0 + 8]).then_inc(e["s_act"], 1)
                            if s == 13:
                                act.wait_ge(e["y_mm"], j + 1)
                                S.copy(Y[:, 0:3], TB[:, 3 * 512:3 * 512 + 3 * SC].rearrange("p (g c) -> p g c", g=3))
                                S.copy(Y[:, 6:8], TB[:, 0:2 * SC].rearrange("p (g c) -> p g c", g=2)).then_inc(e["y_act"], 1)
                            if s == 14:
                                act.wait_ge(e["yt_mm"], j + 1)
                                S.copy(UC[:].rearrange("p (t g c) -> p g t c", t=L, g=8)[:, 0:4],
                                       TB[:, 512:1024].rearrange("p (g t c) -> p g t c", g=4, t=L))
                                S.copy(UCS[0:8].rearrange("p (t g c) -> p g t c", t=L, g=8)[:, 0:4],
                                       TB[0:8, 3 * 512:4 * 512].rearrange("p (g t c) -> p g t c", g=4, t=L)).then_inc(e["yt_act"], 1)
                            if s == 15:
                                act.wait_ge(W.mm, W.multiplied(j * NPC + s))
                                for src, dst in halves(GB, U):
                                    ins = S.activation(dst, src, ACT.Silu)
                                ins.then_inc(e["ga"], 1)
                                act.wait_ge(e["ga"], 2 * j + 2)
                                act.dma_start(zs_s[ds(j * P, P), :], U[:, 0:TOK]).then_inc(e["zs_out"], 16)
                                act.wait_ge(e["z_mm"], j + 1)
                                zt = lambda a: a.rearrange("p (c t) -> p t c", t=L)
                                for hlf in range(2):
                                    S.activation(zt(UZ[:, 0:SEQ])[:, 4 * hlf:4 * hlf + 4],
                                                 TB[:, 512 * (1 + hlf):512 * (2 + hlf)].rearrange("p (t c) -> p t c", t=4), ACT.Gelu)
                                S.activation(zt(UZ[:, SEQ:TOK]), TB[:, 0:DEC].rearrange("p (t c) -> p t c", t=L),
                                             ACT.Gelu).then_inc(e["z_act"], 1)
                                act.wait_ge(e["z_act"], j + 1)
                                act.dma_start(zg_s[ds(j * P, P), :], UZ[:]).then_inc(e["zg_out"], 16)
                                act.wait_ge(e["fin_ev"], j + 1)
                                for i, dst in enumerate((hre_prompt, him_prompt, hre_sample, him_sample)):
                                    act.dma_start(dst[0, 0, ds(8 * j, 8), :],
                                                  FS[8 * (i // 2):8 * (i // 2) + 8, (i % 2) * NP:(i % 2 + 1) * NP]
                                                  ).then_inc(e["fin_out"], 16)
                    act.wait_ge(e["zs_out"], 16 * 8)
                    act.wait_ge(e["zg_out"], 16 * 8)
                    act.wait_ge(e["fin_out"], 64 * 8)
                    act.wait_ge(W.w_in[0], 16 * (8 * NPC // RAW + 1))
                    act.wait_ge(W.w_in[1], 16 * (8 * NPC // RAW + 1))

                @block.vector
                def _(dve):
                    o = Order(dve, "dve_ssm")
                    V.memset(UC[:, 0:112], 0.0).then_inc(e["zero_done"], 1)
                    V.memset(BD[:], 0.0).then_inc(e["zero_done"], 1)
                    V.memset(H[:, :, 0:1], 0.0).then_inc(e["zero_done"], 1)
                    dve.wait_ge(e["zero_done"], 3)
                    dve.sem_inc(W.lo, RAW)
                    for s in range(SPL):
                        W.split_lo(s, s)
                    with dve.Fori(0, 8) as j:
                        o.enter(j, 4)
                        for s in range(NPC):
                            m = s + SPL
                            W.split_lo(j * NPC + m, m)
                            if s == 0:
                                dve.wait_ge(e["pj_in"], 16 * (j + 1))
                                dve.wait_ge(e["z_mm"], j)
                                o.then(V.tensor_copy(DC[:], row(MG)[:, 0].unsqueeze(2).to_broadcast([P, 4, SC])))
                                V.memset(DC[:, :, 0:NB + 1:NB], 0.0).then_inc(e["dec_ready"], 1)
                                for i in range(2):
                                    for g in range(2):
                                        ins = V.tensor_copy(BD[i * NP:(i + 1) * NP, g::2, g * GC:(g + 1) * GC],
                                                            bc_(i)[g * NP:(g + 1) * NP])
                                ins.then_inc(e["bd_ready"], 1)
                                qa = lambda base: row(base, 9).rearrange("p r q -> p q r").unsqueeze(3).to_broadcast([P, 4, 9, GC])
                                qc = lambda i: bc_(i).unsqueeze(2).to_broadcast([P, 4, 9, GC])
                                q4 = lambda t: t[:, 0:576].rearrange("p (q r c) -> p q r c", q=4, r=9)
                                q3 = lambda t, g: t[g * NP:(g + 1) * NP, 0:576].rearrange("p (q n) -> p q n", q=4)
                                V.tensor_tensor(q4(UC), qa(AR), qc(2), ALU.mult)
                                o.then(V.tensor_tensor(q4(UCS), qa(AI), qc(3), ALU.mult))
                                for g in range(2):
                                    ins = V.tensor_tensor(Q[0:NP, g::2], q3(UC, g), q3(UCS, g), ALU.subtract)
                                o.then(ins)
                                V.tensor_tensor(q4(UC), qa(AI), qc(2), ALU.mult)
                                o.then(V.tensor_tensor(q4(UCS), qa(AR), qc(3), ALU.mult))
                                for g in range(2):
                                    ins = V.scalar_tensor_tensor(Q[NP:P, g::2], q3(UC, g), -1.0, q3(UCS, g), ALU.mult, ALU.subtract)
                                ins.then_inc(e["q_ready"], 1)
                            if s == 7:
                                dve.wait_ge(W.mm, W.multiplied(j * NPC + s))
                                dve.wait_ge(e["zg_out"], 16 * j)
                                V.tensor_copy(cols(UZ, 1), group(GB, 1)).then_inc(e["gd"], 1)
                                dve.wait_ge(e["ls_mm"], j + 1)
                                V.tensor_copy(LS[:, 4:8], TB[:, 512:1024].rearrange("p (a b) -> p a b", a=4)).then_inc(e["ls_dve"], 1)
                                dve.wait_ge(e["k_mm"], j + 1)
                                dve.wait_ge(e["kpad_out"], 16 * (j + 1))
                                V.tensor_copy(KS[:, GC:P], TB[:, 2 * 512 + GC:2 * 512 + P])
                                V.scalar_tensor_tensor(KS[:, 0:GC], delta[:], PJ[:, PKW - 1:PKW], TB[:, 2 * 512:2 * 512 + GC],
                                                       ALU.mult, ALU.add).then_inc(e["ks_ready"], 1)
                            if s == 8:
                                dve.wait_ge(e["st1_mm"], j + 1)
                                V.tensor_copy(UC[:].rearrange("p (g r c) -> p r g c", g=8, r=L)[:, 4:8],
                                              TB[:, 4 * 512:5 * 512].rearrange("p (r g c) -> p r g c", r=4, g=8))
                                V.tensor_copy(UCS[0:8].rearrange("p (g r c) -> p r g c", g=8, r=L)[:, 4:8],
                                              TB[0:8, 512:1024].rearrange("p (r g c) -> p r g c", r=4, g=8)).then_inc(e["st1_dve"], 1)
                            if s == 9:
                                dve.wait_ge(e["st2_mm"], j + 1)
                                dve.wait_ge(e["zs_out"], 16 * j)
                                V.memset(Ug[:, :, NB:NB + 1], 0.0)
                                V.tensor_copy(Ug[:, 4:8, 0:NB], TB[:, 3 * 512:4 * 512].rearrange("p (g c) -> p g c", g=4))
                                V.tensor_copy(Ug[:, :, NB + 1:SC], TB[:, 4 * 512:4 * 512 + DEC].rearrange("p (g c) -> p g c", g=8)
                                              ).then_inc(e["st2_dve"], 1)
                            if s == 10:
                                tr = lambda i: TR[:, i].rearrange("p a b -> p (a b)").unsqueeze(1).to_broadcast([P, 2, 4 * SC])
                                dve.wait_ge(e["s_act"], 4 * (j + 1))
                                dve.wait_ge(e["t_ready"], j + 1)
                                V.tensor_tensor(M1[:], SS[:], tr(0), ALU.mult).then_inc(e["m1_done"], 1)
                                dve.wait_ge(e["m1_done"], j + 1)
                                dve.wait_ge(e["m2_done"], j + 1)
                                V.tensor_tensor(SS[:, 0], M1[:, 0], M2[:, 1], ALU.subtract).then_inc(e["gre_done"], 1)
                                dve.wait_ge(e["gre_done"], j + 1)
                                dve.wait_ge(e["gim_done"], j + 1)
                                dcf = DC[:].rearrange("p a b -> p (a b)")
                                V.tensor_tensor_scan(M1[:, 0], dcf, SS[:, 0], 0.0, ALU.mult, ALU.add)
                                V.tensor_tensor_scan(M1[:, 1], dcf, SS[:, 1], 0.0, ALU.mult, ALU.add).then_inc(e["scan_done"], 1)
                                dve.wait_ge(e["scan_done"], j + 1)
                                V.tensor_tensor(SS[:], M1[:], tr(0), ALU.mult).then_inc(e["p1_done"], 1)
                                dve.wait_ge(e["p1_done"], j + 1)
                                dve.wait_ge(e["p2_done"], j + 1)
                                h4 = lambda t, i, g: t[g * NP:(g + 1) * NP, i].rearrange("p (q c) -> p q c", q=4)
                                V.tensor_tensor(H[0:NP, 1::2, 1:HC], h4(SS, 0, 1), h4(M2, 1, 1), ALU.add)
                                V.tensor_tensor(H[NP:P, 0::2, 1:HC], h4(SS, 1, 0), h4(M2, 0, 0), ALU.subtract).then_inc(e["h_dve"], 1)
                            if s == 13:
                                dve.wait_ge(e["h_dve"], j + 1)
                                dve.wait_ge(e["h_pool"], j + 1)
                                V.tensor_copy(FB[:, 0:8], H[:, :, NB])
                                V.tensor_copy(FB[:, 8:16], H[:, :, HC - 1]).then_inc(e["fb_ready"], 1)
                                dve.wait_ge(e["y_mm"], j + 1)
                                V.tensor_copy(Y[:, 3:6], TB[:, 4 * 512:4 * 512 + 3 * SC].rearrange("p (g c) -> p g c", g=3)
                                              ).then_inc(e["y_dve"], 1)
                            if s == 14:
                                dve.wait_ge(e["yt_mm"], j + 1)
                                V.tensor_copy(UC[:].rearrange("p (t g c) -> p g t c", t=L, g=8)[:, 4:8],
                                              TB[:, 1024:1536].rearrange("p (g t c) -> p g t c", g=4, t=L))
                                V.tensor_copy(UCS[0:8].rearrange("p (t g c) -> p g t c", t=L, g=8)[:, 4:8],
                                              TB[0:8, 4 * 512:5 * 512].rearrange("p (g t c) -> p g t c", g=4, t=L)).then_inc(e["yt_dve"], 1)
                            if s == 15:
                                dve.wait_ge(e["fin_mm"], j + 1)
                                dve.wait_ge(e["fin_out"], 64 * j)
                                V.tensor_copy(FS[:], TB[0:16, 4 * 512:4 * 512 + P]).then_inc(e["fin_ev"], 1)
                    o.leave(8)

                @block.gpsimd
                def _(pool):
                    o = Order(pool, "pool_ssm")
                    PO = 32
                    with pool.Fori(0, 8) as j:
                        o.enter(j, PO)
                        pool.wait_ge(e["pj_in"], 16 * (j + 1))
                        pool.wait_ge(e["p1_done"], j)
                        pool.wait_ge(e["z_mm"], j)
                        stand(pool, "pool")
                        G.memset(TR[:, 0, :, 0:1], 1.0)
                        o.then(G.memset(TR[:, 1, :, 0:1], 0.0))
                        for lv in range(NLV):
                            n = 1 << lv
                            w = lambda r: row(r + lv).unsqueeze(3).to_broadcast([P, 1, 4, n])
                            m1 = M1[:].rearrange("p a (q c) -> p a q c", q=4)[:, :, :, 0:n] if False else None
                            ta = M2[:, 0, 0:4 * n].rearrange("p (q c) -> p q c", q=4)
                            tb = M2[:, 1, 0:4 * n].rearrange("p (q c) -> p q c", q=4)
                            wr = row(WR + lv)[:, 0].unsqueeze(2).to_broadcast([P, 4, n])
                            wi = row(WI + lv)[:, 0].unsqueeze(2).to_broadcast([P, 4, n])
                            re, im = TR[:, 0, :, 0:n], TR[:, 1, :, 0:n]
                            G.tensor_tensor(ta, re, wr, ALU.mult)
                            o.then(G.tensor_tensor(tb, im, wi, ALU.mult))
                            o.then(G.tensor_tensor(TR[:, 0, :, n:2 * n], ta, tb, ALU.subtract))
                            G.tensor_tensor(ta, re, wi, ALU.mult)
                            o.then(G.tensor_tensor(tb, im, wr, ALU.mult))
                            o.then(G.tensor_tensor(TR[:, 1, :, n:2 * n], ta, tb, ALU.add))
                        stand(pool, "pool")
                        G.tensor_copy(TR[:].rearrange("p a q c -> p (a q) c")[:, :, NB:SC],
                                      TR[:].rearrange("p a q c -> p (a q) c")[:, :, 0:NBS + 1]).then_inc(e["t_ready"], 1)
                        a = lambda base: row(base, L).rearrange("p r q -> p q r").unsqueeze(3).to_broadcast([P, 4, L, GC])
                        b = lambda i: bc_(i).unsqueeze(2).to_broadcast([P, 4, L, GC])
                        G.tensor_tensor(GT[:, 0], a(AR), b(0), ALU.mult)
                        o.then(G.tensor_tensor(GT[:, 1], a(AI), b(1), ALU.mult))
                        o.then(G.tensor_tensor(GR[:, 0], GT[:, 0], GT[:, 1], ALU.subtract))
                        G.tensor_tensor(GT[:, 0], a(AR), b(1), ALU.mult)
                        o.then(G.tensor_tensor(GT[:, 1], a(AI), b(0), ALU.mult))
                        G.tensor_tensor(GR[:, 1], GT[:, 0], GT[:, 1], ALU.add).then_inc(e["g_ready"], 1)
                        tr = lambda i: TR[:, i].rearrange("p a b -> p (a b)").unsqueeze(1).to_broadcast([P, 2, 4 * SC])
                        pool.wait_ge(e["t_ready"], j + 1)
                        pool.wait_ge(e["s_act"], 4 * (j + 1))
                        G.tensor_tensor(M2[:], SS[:], tr(1), ALU.mult).then_inc(e["m2_done"], 1)
                        pool.wait_ge(e["m2_done"], j + 1)
                        pool.wait_ge(e["m1_done"], j + 1)
                        G.tensor_tensor(SS[:, 1], M1[:, 1], M2[:, 0], ALU.add).then_inc(e["gim_done"], 1)
                        pool.wait_ge(e["scan_done"], j + 1)
                        G.tensor_tensor(M2[:], M1[:], tr(1), ALU.mult).then_inc(e["p2_done"], 1)
                        pool.wait_ge(e["p2_done"], j + 1)
                        pool.wait_ge(e["p1_done"], j + 1)
                        h4 = lambda t, i, g: t[g * NP:(g + 1) * NP, i].rearrange("p (q c) -> p q c", q=4)
                        G.tensor_tensor(H[0:NP, 0::2, 1:HC], h4(SS, 0, 0), h4(M2, 1, 0), ALU.add)
                        G.tensor_tensor(H[NP:P, 1::2, 1:HC], h4(SS, 1, 1), h4(M2, 0, 1), ALU.subtract).then_inc(e["h_pool"], 1)
                    o.leave(8)

                @block.tensor
                def _(pe):
                    pe.wait_ge(e["zero_done"], 3)
                    W.credit("pe")
                    gb = (2, 3, 4)
                    with pe.Fori(0, 8) as j:
                        for s in range(NPC):
                            if s == 0:
                                pe.wait_ge(e["ga"], 2 * j)
                            if s == 8:
                                pe.wait_ge(e["ga"], 2 * j + 1)
                                pe.wait_ge(e["gd"], j + 1)
                            k = PIECE * (s % 8)
                            W.multiply(j * NPC + s, s, k, k == 0, k == KT - PIECE)
                            if s == 7:
                                pe.wait_ge(e["g_ready"], j + 1)
                                pe.wait_ge(e["z_act"], j)
                                pe.wait_ge(e["fin_ev"], j)
                                for i in range(8):
                                    ins = T.transpose(TB[:, i * P:(i + 1) * P], GR[:, i // 4, i % 4].rearrange("p r c -> p (r c)"),
                                                      ident[:])
                                ins.then_inc(e["ls_mm"], 1)
                                pe.wait_ge(e["bd_ready"], j + 1)
                                pe.wait_ge(e["q_ready"], j + 1)
                                for g in range(8):
                                    q = g // 2
                                    ins = T.matmul(TB[32 * q:32 * q + 32, 1024:1024 + P], BD[:, g], Q[:, g, 0:P],
                                                   start=g % 2 == 0, stop=g % 2 == 1)
                                ins.then_inc(e["k_mm"], 1)
                            if s == 8:
                                pe.wait_ge(e["ls_act"], j + 1)
                                pe.wait_ge(e["ls_dve"], j + 1)
                                pe.wait_ge(e["ga"], 2 * j + 1)
                                pe.wait_ge(e["gd"], j + 1)
                                for r in range(L):
                                    i = L - 1 - r
                                    T.transpose(TB[:, 3 * 512 + r * P:3 * 512 + (r + 1) * P], UZ[:, i:SEQ:L], ident[:])
                                    ins = T.transpose(TB[0:NBS, r * P:(r + 1) * P], UZ[:, SEQ + i:TOK:L], ident[:])
                                ins.then_inc(e["st1_mm"], 1)
                            if s == 9:
                                pe.wait_ge(e["st1_act"], j + 1)
                                pe.wait_ge(e["st1_dve"], j + 1)
                                pe.wait_ge(e["ks_ready"], j + 1)
                                for g in range(8):
                                    T.transpose(TB[:, 1024 + g * P:1024 + (g + 1) * P], UC[:, g * P:(g + 1) * P], ident[:])
                                    ins = T.transpose(TB[:, 4 * 512 + g * NBS:4 * 512 + (g + 1) * NBS],
                                                      UCS[0:NBS, g * P:(g + 1) * P], ident[0:NBS, 0:NBS])
                                ins.then_inc(e["st2_mm"], 1)
                            if s == 10:
                                pe.wait_ge(e["st2_act"], j + 1)
                                pe.wait_ge(e["st2_dve"], j + 1)
                                for i in range(8):
                                    for g in range(2):
                                        c = 512 * (i // 3) + (i % 3) * SC
                                        ins = T.matmul(TB[g * NP:(g + 1) * NP, c:c + SC], LS[:, i, g * NP:(g + 1) * NP],
                                                       Ug[:, 2 * (i % 4) + g], start=True, stop=True)
                                ins.then_inc(e["s_mm"], 1)
                            if s == 13:
                                pe.wait_ge(e["h_dve"], j + 1)
                                pe.wait_ge(e["h_pool"], j + 1)
                                pe.wait_ge(e["mt_in"], P * (j + 1))
                                for g in range(8):
                                    c = 512 * (3, 4, 0)[g // 3] + (g % 3) * SC
                                    T.matmul(TB[:, c:c + SC], MT[:, g], Ug[:, g], start=True, stop=False)
                                    ins = T.matmul(TB[:, c:c + SC], Q[:, g, GC:], H[:, g, 0:SC], start=False, stop=True)
                                ins.then_inc(e["y_mm"], 1)
                            if s == 14:
                                pe.wait_ge(e["y_act"], j + 1)
                                pe.wait_ge(e["y_dve"], j + 1)
                                for g in range(8):
                                    T.transpose(TB[:, 512 + g * P:512 + (g + 1) * P], Y[:, g, 0:NB], ident[:])
                                    ins = T.transpose(TB[0:NBS, 3 * 512 + g * P:3 * 512 + (g + 1) * P], Y[:, g, NB + 1:SC], ident[:])
                                ins.then_inc(e["yt_mm"], 1)
                            if s == 15:
                                pe.wait_ge(e["yt_act"], j + 1)
                                pe.wait_ge(e["yt_dve"], j + 1)
                                for t in range(L):
                                    T.transpose(TB[:, 512 + t * P:512 + (t + 1) * P], UC[:, t * P:(t + 1) * P], ident[:])
                                    ins = T.transpose(TB[:, t * NBS:(t + 1) * NBS], UCS[0:NBS, t * P:(t + 1) * P],
                                                      ident[0:NBS, 0:NBS])
                                ins.then_inc(e["z_mm"], 1)
                                pe.wait_ge(e["fb_ready"], j + 1)
                                T.transpose(TB[0:16, 4 * 512:4 * 512 + P], FB[:], ident[:]).then_inc(e["fin_mm"], 1)

        free_semaphores()

        CT = SEQ + PAST + DEC
        with ExitStack() as st:
            sbp = pool_of(st)
            wf = sbp("wf", [P, KT, NH])
            WF = sbp("WF", [P, KT, P], r32)
            fx = sbp("fx", [NH, TOK])
            fl = sbp("fl", [NH, TOK])
            fe = sbp("fe", [NH, TOK])
            one8 = sbp("one8", [NH, SEQ])
            lfs = sbp("lfs", [NH, PAST + DEC])
            cum = sbp("cum", [NH, CT])
            ncum = sbp("ncum", [NH, CT])
            bf = sbp("bf", [NH, 1])
            cl = sbp("cl", [P, NH])
            lt = sbp("lt", [P, TT, NH])
            names = ("in", "zero", "hi", "lo", "mm", "fn", "ex", "e1", "ln", "lf", "t_mm", "t_ev", "cum", "out", "fl", "x", "neg")
            e = {n: sem("gate_" + n) for n in names}
            with nc.Block() as block:
                @block.sync
                def _(sp):
                    sp.dma_start(wf[:], w_in_v[:, :, D_PROJ - NH:D_PROJ]).then_inc(e["in"], 16)
                    sp.dma_start(bf[:], b_f.rearrange("o h -> h o")).then_inc(e["in"], 16)
                    sp.dma_start(cl[:], cache_logf[0, 0]).then_inc(e["in"], 16)
                    sp.wait_ge(e["t_ev"], 2)
                    sp.dma_start(logf_prompt[0, 0].rearrange("(m p) h -> p m h", p=P), lt[:, 0:TT - 1]).then_inc(e["out"], 16)
                    sp.dma_start(logf_sample[0, 0], lt[0:DEC, TT - 1]).then_inc(e["out"], 16)
                    sp.wait_ge(e["neg"], 1)
                    sp.dma_start(nc_s, ncum[:]).then_inc(e["out"], 16)
                    sp.wait_ge(e["out"], 48)

                @block.scalar
                def _(act):
                    act.wait_ge(e["zero"], 1)
                    act.wait_ge(e["in"], 48)
                    S.copy(WF[:, :, 0:NH], wf[:]).then_inc(e["hi"], 1)
                    act.wait_ge(e["fn"], 1)
                    S.activation(fe[:], fl[:], ACT.Exp).then_inc(e["ex"], 1)
                    act.wait_ge(e["e1"], 1)
                    S.activation(fe[:], fe[:], ACT.Ln).then_inc(e["ln"], 1)

                @block.vector
                def _(dve):
                    V.memset(WF[:].rearrange("p a b -> p (a b)").bitcast(f32), 0.0).then_inc(e["zero"], 1)
                    V.memset(one8[:], 1.0)
                    dve.wait_ge(e["hi"], 1)
                    V.tensor_tensor(WF[:, :, 32:32 + NH], wf[:], WF[:, :, 0:NH].bitcast(f32), ALU.subtract).then_inc(e["lo"], 1)
                    dve.wait_ge(e["mm"], 1)
                    for src, dst in halves(GB, fl, slice(32, 32 + NH)):
                        ins = V.tensor_copy(dst, src)
                    ins.then_inc(e["fl"], 1)
                    dve.wait_ge(e["fl"], 1)
                    for (src, dst), (_, low) in zip(halves(GB, fx, slice(0, NH)), halves(GB, fl)):
                        ins = V.scalar_tensor_tensor(dst, src, bf[:], low, ALU.add, ALU.add)
                    ins.then_inc(e["x"], 1)
                    dve.wait_ge(e["x"], 1)
                    V.scalar_tensor_tensor(fl[:], fx[:], -1.0, fx[:], ALU.mult, ALU.min).then_inc(e["fn"], 1)
                    dve.wait_ge(e["ex"], 1)
                    V.tensor_scalar(fe[:], fe[:], 1.0, None, ALU.add).then_inc(e["e1"], 1)
                    dve.wait_ge(e["ln"], 1)
                    V.scalar_tensor_tensor(fx[:], fx[:], 0.0, fe[:], ALU.min, ALU.subtract).then_inc(e["lf"], 1)
                    dve.wait_ge(e["t_mm"], 1)
                    V.tensor_copy(lt[:, 0:TT - 1], TB[:, 0:64].rearrange("p (m h) -> p m h", h=NH)).then_inc(e["t_ev"], 1)
                    V.tensor_copy(lt[0:DEC, TT - 1], TB[0:DEC, 64:72]).then_inc(e["t_ev"], 1)
                    V.tensor_copy(lfs[:, 0:PAST], TB[0:NH, 512:512 + PAST]).then_inc(e["cum"], 1)
                    V.tensor_copy(lfs[:, PAST:], fx[:, SEQ:TOK]).then_inc(e["cum"], 1)
                    V.tensor_tensor_scan(cum[:, 0:SEQ], one8[:], fx[:, 0:SEQ], 0.0, ALU.mult, ALU.add).then_inc(e["cum"], 1)
                    dve.wait_ge(e["cum"], 3)
                    V.tensor_tensor_scan(cum[:, SEQ:], one8[:, 0:PAST + DEC], lfs[:], 0.0, ALU.mult, ALU.add).then_inc(e["cum"], 1)
                    dve.wait_ge(e["cum"], 4)
                    V.tensor_scalar(ncum[:], cum[:], -1.0, None, ALU.mult).then_inc(e["neg"], 1)

                @block.tensor
                def _(pe):
                    pe.wait_ge(e["lo"], 1)
                    for k in range(KT):
                        for x in (XH, XL):
                            for b, (c, n) in enumerate(COLS):
                                ins = T.matmul(group(GB, b), WF[:, k], x[:, k, c:c + n],
                                               start=k == 0 and x is XH, stop=k == KT - 1 and x is XL)
                    ins.then_inc(e["mm"], 1)
                    pe.wait_ge(e["in"], 48)
                    T.transpose(TB[0:NH, 512:512 + PAST], cl[:], ident[:])
                    pe.wait_ge(e["lf"], 1)
                    for m in range(TT):
                        n = min(P, TOK - m * P)
                        ins = T.transpose(TB[0:n, m * NH:(m + 1) * NH], fx[:, m * P:m * P + n], ident[0:NH, 0:NH])
                    ins.then_inc(e["t_mm"], 1)

        with ExitStack() as st:
            sbp = pool_of(st)
            QR, KR, VR, ZR = (sbp(n, [P, TOK]) for n in ("QR", "KR", "VR", "ZR"))
            QN, KN = sbp("QN", [P, TOK]), sbp("KN", [P, TOK])
            VT = sbp("VT", [P, TT, P])
            KO = sbp("KO", [P, TT, P])
            SQ = sbp("SQ", [P, TOK])
            NCB = sbp("NCB", [P, CT])
            PR = sbp("PR", [P, SEQ])
            PT = sbp("PT", [P, SEQ])
            CK, CV, KPT = sbp("CK", [PAST, P]), sbp("CV", [PAST, P]), sbp("KPT", [P, PAST])
            SQA = sbp("SQA", [P, TOK])
            qg = sbp("qg", [P, 1])
            mx, nmx, rsum, rrec = (sbp(n, [P, 1]) for n in ("mx", "nmx", "rsum", "rrec"))
            W = Weights("att", w_in_v, XH, XL)
            NPC = 4 * KT // PIECE
            NR = 9
            names = ("ga", "gd", "sq", "ss_mm", "rt", "qn_r", "qn", "kn", "kpt_mm", "kpt", "s_mm", "nmx", "exp", "pn",
                     "pt_mm", "pt_act", "pt_dve", "o_mm", "y", "v_mm", "v_act", "v_dve", "k_mm", "k_act", "k_dve",
                     "in", "k_out", "v_out", "y_out", "ysq", "sqa", "init", "qg", "sqa_out", "rr")
            e = {n: sem("att_" + n) for n in names}
            sq_at = {8: (0, QR), 17: (1, KR)}
            REC = 8
            RW = TOK // REC

            def keys(i):
                return (P * (i + 1), P) if i < NR - 1 else (PAST + DEC, DEC)

            with nc.Block() as block:
                @block.sync
                def _(sp):
                    with sp.Fori(0, NH) as h:
                        for s in range(NPC):
                            col = h * P + 2 * D_SSM + D_ATT * (s // 8)
                            W.load(sp, h * NPC + s, s, col, PIECE * (s % 8))
                    for s in range(SPL):
                        W.load(sp, NH * NPC + s, s, 0, 0)

                @block.gpsimd
                def _(pool):
                    G.memset(SQA[:], 0.0).then_inc(e["init"], 1)
                    pool.wait_ge(e["init"], 1)

                    def part(h, gemm, att, ha):
                        if att:
                            pool.wait_ge(e["ysq"], ha + 1)
                            G.tensor_tensor(SQA[:], SQA[:], SQ[:], ALU.add).then_inc(e["sqa"], 1)
                            pool.wait_ge(e["sqa"], ha + 1)
                            pool.wait_ge(e["y"], NR * (ha + 1))
                            stand(pool, "pool")
                            pool.dma_start(ya_s[ds(ha * P, P), :], ZR[:]).then_inc(e["y_out"], 16)
                        if gemm:
                            pool.wait_ge(e["qn_r"], h + 1)
                            if att:
                                pool.wait_ge(e["s_mm"], NR * (ha + 1))
                            stand(pool, "pool")
                            G.tensor_copy(QN[:], QR[:]).then_inc(e["qn"], 1)
                            if att:
                                pool.wait_ge(e["o_mm"], NR * (ha + 1))
                                pool.wait_ge(e["nmx"], NR * (ha + 1))
                            stand(pool, "pool")
                            for dst, src in ((CK[:], cache_k[0, 0]), (CV[:], cache_v[0, 0])):
                                pool.dma_start(dst, src.rearrange("t h d -> t (h d)")[:, ds(h * P, P)]).then_inc(e["in"], 16)
                            pool.dma_start(NCB[:], nc_s[ds(h, 1), :].to_broadcast([P, CT])).then_inc(e["in"], 16)
                            for n, src, po, so in (("v", VT, v_prompt, v_sample), ("k", KO, k_prompt, k_sample)):
                                pool.wait_ge(e[n + "_act"], h + 1)
                                pool.wait_ge(e[n + "_dve"], h + 1)
                                stand(pool, "pool")
                                pool.dma_start(po[0, 0].rearrange("(m p) h d -> p m (h d)", p=P)[:, :, ds(h * P, P)],
                                               src[:, 0:TT - 1]).then_inc(e[n + "_out"], 16)
                                pool.dma_start(so[0, 0].rearrange("p h d -> p (h d)")[:, ds(h * P, P)],
                                               src[0:DEC, TT - 1]).then_inc(e[n + "_out"], 16)
                    part(0, True, False, None)
                    with pool.Fori(1, NH) as h:
                        part(h, True, True, h - 1)
                    part(None, False, True, NH - 1)
                    pool.dma_start(sqa_s, SQA[:]).then_inc(e["sqa_out"], 16)
                    pool.wait_ge(e["sqa_out"], 16)
                    pool.wait_ge(e["y_out"], 16 * NH)
                    pool.wait_ge(e["k_out"], 32 * NH)
                    pool.wait_ge(e["v_out"], 32 * NH)

                @block.scalar
                def _(act):
                    for s in range(SPL):
                        W.split_hi(s, s, 1)

                    def part(h, gemm, att, ha):
                        for s in range(NPC):
                            if gemm:
                                m = s + SPL
                                W.split_hi(h * NPC + m, m, h * (NPC // RAW) + m // RAW + 1)
                            if att and s == 1:
                                act.wait_ge(e["kpt_mm"], ha + 1)
                                S.copy(KPT[:], TB[:, 1024:1024 + PAST]).then_inc(e["kpt"], 1)
                            if att and s % 3 == 1 and s // 3 < NR:
                                i = s // 3
                                w, n = keys(i)
                                act.wait_ge(e["nmx"], NR * ha + i + 1)
                                S.activation(PR[0:n, 0:w], PR[0:n, 0:w], ACT.Exp, bias=nmx[0:n],
                                             accum_out=rsum[0:n]).then_inc(e["exp"], 1)
                            if att and s % 3 == 2 and s // 3 < NR:
                                i = s // 3
                                act.wait_ge(e["pt_mm"], NR * ha + i + 1)
                                if i < NR - 1:
                                    b = min(i + 1, 4) * P
                                    S.copy(PT[:, 0:b], TB[:, 1024:1024 + b]).then_inc(e["pt_act"], 1)
                                else:
                                    S.copy(PT[:, 0:DEC], TB[:, 1024:1024 + DEC])
                                    S.copy(PT[0:DEC, P:P + DEC], TB[0:DEC, 1024 + P:1024 + P + DEC]).then_inc(e["pt_act"], 1)
                            if gemm and s in (7, 15, 23):
                                act.wait_ge(W.mm, W.multiplied(h * NPC + s))
                                if s == 23:
                                    if att:
                                        pass
                                raw = {7: QR, 15: KR, 23: VR}[s]
                                if s == 7 and att:
                                    act.wait_ge(e["qn"], h)
                                S.copy(cols(raw, 0), group(GB, 0))
                                S.copy(cols(raw, 2), group(GB, 2)).then_inc(e["ga"], 1)
                            if gemm and s in sq_at:
                                w, raw = sq_at[s]
                                act.wait_ge(e["ga"], 4 * h + w + 1)
                                act.wait_ge(e["gd"], 3 * h + w + 1)
                                if w:
                                    act.wait_ge(e["qn_r"], h + 1)
                                elif att:
                                    act.wait_ge(e["kn"], h)
                                    act.wait_ge(e["sqa"], ha)
                                S.activation(SQ[:], raw[:], ACT.Square).then_inc(e["sq"], 1)
                            if gemm and s - 1 in (8, 19):
                                w = 0 if s == 9 else 1
                                act.wait_ge(e["ss_mm"], 2 * h + w + 1)
                                S.activation(SQ[:, 0:SEQ], TB[:, 0:SEQ], ACT.Sqrt, bias=epsc[:], scale=1.0 / HD)
                                S.activation(SQ[:, SEQ:TOK], TB[:, 4 * 512 + P:4 * 512 + P + DEC], ACT.Sqrt, bias=epsc[:],
                                             scale=1.0 / HD).then_inc(e["rt"], 1)
                            if att and s == 29:
                                act.wait_ge(e["y"], NR * (ha + 1))
                                if gemm:
                                    act.wait_ge(e["kn"], h + 1)
                                S.activation(SQ[:], ZR[:], ACT.Square).then_inc(e["ysq"], 1)
                            if gemm and s == 30:
                                act.wait_ge(e["k_mm"], h + 1)
                                act.wait_ge(e["k_out"], 32 * h)
                                S.copy(KO[:, 0:4], TB[:, 0:512].rearrange("p (m d) -> p m d", m=4))
                                S.copy(KO[0:DEC, TT - 1], TB[0:DEC, 4 * 512:4 * 512 + P]).then_inc(e["k_act"], 1)
                            if gemm and s == 31:
                                act.wait_ge(W.mm, W.multiplied(h * NPC + s))
                                if att:
                                    act.wait_ge(e["y_out"], 16 * h)
                                for src, dst in halves(GB, ZR):
                                    ins = S.activation(dst, src, ACT.Silu)
                                ins.then_inc(e["ga"], 1)
                                act.wait_ge(e["v_mm"], h + 1)
                                act.wait_ge(e["v_out"], 32 * h)
                                S.copy(VT[:, 0:4], TB[:, 1024:1536].rearrange("p (m d) -> p m d", m=4))
                                S.copy(VT[0:DEC, TT - 1], TB[0:DEC, 4 * 512:4 * 512 + P]).then_inc(e["v_act"], 1)
                    part(0, True, False, None)
                    with act.Fori(1, NH) as h:
                        part(h, True, True, h - 1)
                    part(None, False, True, NH - 1)

                @block.vector
                def _(dve):
                    V.tensor_scalar(qg[:], vec[:, 32:33], HD ** -0.5, None, ALU.mult).then_inc(e["qg"], 1)
                    dve.sem_inc(W.lo, RAW)
                    dve.wait_ge(e["qg"], 1)
                    for s in range(SPL):
                        W.split_lo(s, s)
                    o = Order(dve, "dve_att")

                    def part(h, gemm, att, ha):
                        for s in range(NPC):
                            if gemm:
                                m = s + SPL
                                W.split_lo(h * NPC + m, m)
                            if att and s % 3 == 0 and 1 <= s // 3 <= NR:
                                i = s // 3 - 1
                                n = keys(i)[1]
                                dve.wait_ge(e["o_mm"], NR * ha + i + 1)
                                V.tensor_tensor(ZR[:, i * P:i * P + n], TB[:, 4 * 512:4 * 512 + n], ZR[:, i * P:i * P + n],
                                                ALU.mult).then_inc(e["y"], 1)
                            if att and s % 3 == 0 and s // 3 < NR:
                                i = s // 3
                                w, n = keys(i)
                                c = 0 if i < NR - 1 else SEQ
                                if i == 0:
                                    dve.wait_ge(e["in"], 48 * (ha + 1))
                                dve.wait_ge(e["s_mm"], NR * ha + i + 1)
                                stand(dve, "dve")
                                o.then(V.tensor_tensor_reduce(out=PR[0:n, 0:w], in0=TB[0:n, 0:w], in1=NCB[0:n, c:c + w], scale=1.0,
                                                              scalar=-3e38, op0=ALU.add, op1=ALU.max, accum_out=mx[0:n]))
                                V.tensor_scalar(nmx[0:n], mx[0:n], -1.0, None, ALU.mult).then_inc(e["nmx"], 1)
                            if att and s % 3 == 1 and s // 3 < NR:
                                i = s // 3
                                w, n = keys(i)
                                dve.wait_ge(e["exp"], NR * ha + i + 1)
                                o.then(V.reciprocal(rrec[0:n], rsum[0:n]))
                                V.tensor_scalar(PR[0:n, 0:w], PR[0:n, 0:w], rrec[0:n], None, ALU.mult).then_inc(e["pn"], 1)
                            if att and s % 3 == 2 and 4 <= s // 3 < NR - 1:
                                i = s // 3
                                dve.wait_ge(e["pt_mm"], NR * ha + i + 1)
                                V.tensor_copy(PT[:, 512:P * (i + 1)], TB[:, 1536:1024 + P * (i + 1)]).then_inc(e["pt_dve"], 1)
                            if gemm and s in (7, 15, 23):
                                dve.wait_ge(W.mm, W.multiplied(h * NPC + s))
                                raw = {7: QR, 15: KR, 23: VR}[s]
                                if s == 7 and att:
                                    dve.wait_ge(e["qn"], h)
                                V.tensor_copy(cols(raw, 1), group(GB, 1)).then_inc(e["gd"], 1)
                            for w, first in ((0, 9), (1, 20)):
                                if gemm and first <= s < first + REC:
                                    if s == first:
                                        dve.wait_ge(e["rt"], 2 * h + w + 1)
                                    a = SQ[:, RW * (s - first):RW * (s - first + 1)]
                                    o.then(V.reciprocal(a, a))
                            if gemm and s == 16:
                                V.scalar_tensor_tensor(QR[:], QR[:], qg[:], SQ[:], ALU.mult, ALU.mult).then_inc(e["qn_r"], 1)
                            if gemm and s == 28:
                                V.scalar_tensor_tensor(KN[:], KR[:], vec[:, 33:34], SQ[:], ALU.mult, ALU.mult).then_inc(e["kn"], 1)
                            if gemm and s == 30:
                                dve.wait_ge(e["k_mm"], h + 1)
                                dve.wait_ge(e["k_out"], 32 * h)
                                V.tensor_copy(KO[:, 4:8], TB[:, 512:1024].rearrange("p (m d) -> p m d", m=4)).then_inc(e["k_dve"], 1)
                            if gemm and s == 31:
                                dve.wait_ge(e["v_mm"], h + 1)
                                dve.wait_ge(e["v_out"], 32 * h)
                                V.tensor_copy(VT[:, 4:8], TB[:, 1536:2048].rearrange("p (m d) -> p m d", m=4)).then_inc(e["v_dve"], 1)
                    part(0, True, False, None)
                    with dve.Fori(1, NH) as h:
                        o.enter(h - 1, 2 * NR + 2 * REC)
                        part(h, True, True, h - 1)
                    o.leave(NH - 1)
                    part(None, False, True, NH - 1)

                @block.tensor
                def _(pe):
                    W.credit("pe")

                    def part(h, gemm, att, ha):
                        for s in range(NPC):
                            if gemm:
                                if s % 8 == 0:
                                    pe.wait_ge(e["ga"], 4 * h + s // 8)
                                    pe.wait_ge(e["gd"], 3 * h + s // 8)
                                k = PIECE * (s % 8)
                                W.multiply(h * NPC + s, s, k, k == 0, k == KT - PIECE)
                            if gemm and s in (9, 21):
                                pe.wait_ge(e["rt"], 2 * h + s // 9)
                            if att and s % 3 == 0 and 1 <= s // 3 <= NR:
                                i = s // 3 - 1
                                w, n = keys(i)
                                pe.wait_ge(e["pt_act"], NR * ha + i + 1)
                                if 4 <= i < NR - 1:
                                    pe.wait_ge(e["pt_dve"], 4 * ha + i - 3)
                                if i:
                                    pe.wait_ge(e["y"], NR * ha + i)
                                O = TB[:, 4 * 512:4 * 512 + n]
                                if i < NR - 1:
                                    for b in range(i + 1):
                                        ins = T.matmul(O, VT[:, b], PT[:, b * P:(b + 1) * P], start=b == 0, stop=b == i)
                                else:
                                    T.matmul(O, CV[:], PT[:, 0:DEC], start=True, stop=False)
                                    ins = T.matmul(O, VT[0:DEC, TT - 1], PT[0:DEC, P:P + DEC], start=False, stop=True)
                                ins.then_inc(e["o_mm"], 1)
                            if att and s % 3 == 0 and s // 3 < NR:
                                i = s // 3
                                w, n = keys(i)
                                if i == 0:
                                    pe.wait_ge(e["qn"], ha + 1)
                                    pe.wait_ge(e["kn"], ha + 1)
                                    pe.wait_ge(e["k_act"], ha + 1)
                                    pe.wait_ge(e["k_dve"], ha + 1)
                                    pe.wait_ge(e["v_act"], ha + 1)
                                    pe.wait_ge(e["v_dve"], ha + 1)
                                else:
                                    pe.wait_ge(e["nmx"], NR * ha + i)
                                if i < NR - 1:
                                    q = QN[:, i * P:(i + 1) * P]
                                    for c in range(0, w, 512):
                                        cw = min(512, w - c)
                                        T.matmul(TB[:, c:c + cw], q, KN[:, c:c + cw], start=True, stop=c + cw < w)
                                    ins = T.matmul(TB[:, w - P:w], identb[:], maskb[:], start=False, stop=True)
                                else:
                                    pe.wait_ge(e["kpt"], ha + 1)
                                    q = QN[:, SEQ:TOK]
                                    T.matmul(TB[0:DEC, 0:PAST], q, KPT[:], start=True, stop=True)
                                    T.matmul(TB[0:DEC, PAST:w], q, KN[:, SEQ:TOK], start=True, stop=False)
                                    ins = T.matmul(TB[0:DEC, PAST:w], identb[0:DEC, 0:DEC], maskb[0:DEC, 0:DEC],
                                                   start=False, stop=True)
                                ins.then_inc(e["s_mm"], 1)
                            if att and s == 1:
                                pe.wait_ge(e["in"], 48 * (ha + 1))
                                T.transpose(TB[:, 1024:1024 + PAST], CK[:], ident[:]).then_inc(e["kpt_mm"], 1)
                            if att and s % 3 == 2 and s // 3 < NR:
                                i = s // 3
                                w, n = keys(i)
                                pe.wait_ge(e["pn"], NR * ha + i + 1)
                                if i == 0:
                                    pe.wait_ge(e["kpt"], ha + 1)
                                else:
                                    pe.wait_ge(e["pt_act"], NR * ha + i)
                                if i < NR - 1:
                                    for b in range(i + 1):
                                        ins = T.transpose(TB[:, 1024 + b * P:1024 + (b + 1) * P], PR[:, b * P:(b + 1) * P], ident[:])
                                else:
                                    stand(pe, "pe")
                                    T.transpose(TB[:, 1024:1024 + DEC], PR[0:DEC, 0:PAST], ident[0:DEC, 0:DEC])
                                    ins = T.transpose(TB[0:DEC, 1024 + P:1024 + P + DEC], PR[0:DEC, PAST:w], ident[0:DEC, 0:DEC])
                                ins.then_inc(e["pt_mm"], 1)
                            if gemm and s in (8, 19):
                                w = 0 if s == 8 else 1
                                pe.wait_ge(e["sq"], 2 * h + w + 1)
                                if att:
                                    i = 2 if s == 8 else 6
                                    pe.wait_ge(e["nmx"], NR * ha + i + 1)
                                    pe.wait_ge(e["y"], NR * ha + i)
                                for c, d, n in ((0, 0, 512), (512, 512, 512), (SEQ, 4 * 512 + P, DEC)):
                                    ins = T.matmul(TB[:, d:d + n], ones[:], SQ[:, c:c + n], start=True, stop=True)
                                ins.then_inc(e["ss_mm"], 1)
                            if gemm and s in (30, 31):
                                src, base, name = (KN, 0, "k") if s == 30 else (VR, 1024, "v")
                                if s == 30:
                                    pe.wait_ge(e["kn"], h + 1)
                                    if att:
                                        pe.wait_ge(e["y"], NR * (ha + 1))
                                else:
                                    pe.wait_ge(e["ga"], 4 * h + 3)
                                    pe.wait_ge(e["gd"], 3 * h + 3)
                                    pe.wait_ge(e["k_act"], h + 1)
                                for m in range(TT):
                                    n = min(P, TOK - m * P)
                                    d = base + m * P if m < TT - 1 else 4 * 512
                                    ins = T.transpose(TB[0:n, d:d + P], src[:, m * P:m * P + n], ident[:])
                                ins.then_inc(e[name + "_mm"], 1)
                    part(0, True, False, None)
                    with pe.Fori(1, NH) as h:
                        part(h, True, True, h - 1)
                    part(None, False, True, NH - 1)
        xs_stack.close()
        free_semaphores()

        KG = D_SSM // P
        with ExitStack() as st:
            sbp = pool_of(st)
            ZH, ZL = sbp("ZH", [P, KG, TOK], r32), sbp("ZL", [P, KG, TOK], r32)
            zf = sbp("zf", [P, KG, TOK])
            zsc = sbp("zsc", [P, 2, TOK])
            yc = sbp("yc", [P, 2, TOK])
            sqc = sbp("sqc", [P, TOK])
            SQS = sbp("SQS", [P, TOK])
            W = Weights("glu", w_glu_v, ZH, ZL)
            NPC = KG // PIECE
            names = ("zf", "zhi", "zlo", "zs0", "zs1", "sig", "y1", "y", "sq", "sqs", "y_out0", "y_out1", "sqs_out", "init")
            e = {n: sem("glu_" + n) for n in names}
            with nc.Block() as block:
                @block.sync
                def _(sp):
                    zin = [sem(f"glu_zin{k}") for k in range(KG)]
                    for k in range(KG):
                        sp.dma_start(zf[:, k], zg_s[k * P:(k + 1) * P, :]).then_inc(zin[k], 16)
                    for n in range(KG):
                        for s in range(NPC):
                            W.load(sp, n * NPC + s, n * NPC + s, n * P, PIECE * s)

                def finish_glu(pool, n):
                    pool.wait_ge(e["y"], n + 1)
                    pool.dma_start(ys_s[n * P:(n + 1) * P, :], yc[:, n % 2]).then_inc(e[f"y_out{n % 2}"], 16)
                    pool.wait_ge(e["sq"], n + 1)
                    G.tensor_tensor(SQS[:], SQS[:], sqc[:], ALU.add).then_inc(e["sqs"], 1)
                    pool.wait_ge(e["sqs"], n + 1)

                @block.gpsimd
                def _(pool):
                    G.memset(SQS[:], 0.0).then_inc(e["init"], 1)
                    pool.wait_ge(e["init"], 1)
                    for n in range(KG):
                        if n >= 2:
                            pool.wait_ge(e["y"], n - 1)
                        pool.dma_start(zsc[:, n % 2], zs_s[n * P:(n + 1) * P, :]).then_inc(e[f"zs{n % 2}"], 16)
                        if n:
                            finish_glu(pool, n - 1)
                    finish_glu(pool, KG - 1)
                    pool.dma_start(sqs_s, SQS[:]).then_inc(e["sqs_out"], 16)
                    pool.wait_ge(e["sqs_out"], 16)
                    pool.wait_ge(e["y_out0"], 16 * (KG // 2))
                    pool.wait_ge(e["y_out1"], 16 * (KG // 2))

                @block.scalar
                def _(act):
                    zin = [sem(f"glu_zin{k}") for k in range(KG)]
                    for s in range(SPL):
                        W.split_hi(s, s, 1)
                    for k in range(KG):
                        act.wait_ge(zin[k], 16)
                        S.copy(ZH[:, k], zf[:, k]).then_inc(e["zhi"], 1)
                    for n in range(KG):
                        for s in range(NPC):
                            m = n * NPC + s + SPL
                            if m < KG * NPC:
                                W.split_hi(m, m, m // RAW + 1)
                        act.wait_ge(W.mm, W.multiplied(n * NPC + NPC - 1))
                        if n >= 2:
                            act.wait_ge(e[f"y_out{n % 2}"], 16 * (n // 2))
                        for src, dst in halves((GB, TB)[n % 2], yc[:, n % 2]):
                            ins = S.activation(dst, src, ACT.Sigmoid, bias=vec[:, 8 + n:9 + n])
                        ins.then_inc(e["sig"], 1)
                        act.wait_ge(e["y"], n + 1)
                        if n:
                            act.wait_ge(e["sqs"], n)
                        S.activation(sqc[:], yc[:, n % 2], ACT.Square).then_inc(e["sq"], 1)

                @block.vector
                def _(dve):
                    dve.sem_inc(W.lo, RAW)
                    for s in range(SPL):
                        W.split_lo(s, s)
                    for k in range(KG):
                        dve.wait_ge(e["zhi"], k + 1)
                        V.tensor_tensor(ZL[:, k], zf[:, k], ZH[:, k].bitcast(f32), ALU.subtract).then_inc(e["zlo"], 1)
                    for n in range(KG):
                        for s in range(NPC):
                            m = n * NPC + s + SPL
                            if m < KG * NPC:
                                W.split_lo(m, m)
                        dve.wait_ge(e["sig"], n + 1)
                        V.tensor_tensor(yc[:, n % 2], yc[:, n % 2], zf[:, n], ALU.mult).then_inc(e["y1"], 1)
                        dve.wait_ge(e["y1"], n + 1)
                        dve.wait_ge(e[f"zs{n % 2}"], 16 * (n // 2 + 1))
                        V.tensor_tensor(yc[:, n % 2], yc[:, n % 2], zsc[:, n % 2], ALU.mult).then_inc(e["y"], 1)

                @block.tensor
                def _(pe):
                    W.credit("pe")
                    for n in range(KG):
                        if n >= 2:
                            pe.wait_ge(e["sig"], n - 1)
                        for s in range(NPC):
                            if n == 0:
                                pe.wait_ge(e["zlo"], PIECE * (s + 1))
                            W.multiply(n * NPC + s, n * NPC + s, PIECE * s, s == 0, s == NPC - 1, (GB, TB)[n % 2])

        with ExitStack() as st:
            sbp = pool_of(st)
            YH, YL = sbp("YH", [P, KT, TOK], r32), sbp("YL", [P, KT, TOK], r32)
            sqb = sbp("sqb", [P, 2, TOK])
            yf = sbp("yf", [P, 3, TOK])
            OT = sbp("OT", [P, TOK])
            XO = sbp("XO", [P, 2, TT, P])
            W = Weights("out", w_out_v, YH, YL)
            NPC = KT // PIECE
            NCH = D_MODEL // P
            names = ("sq_in", "ss", "rt", "rr", "sc", "yhi", "ylo", "ga", "gd", "t_mm", "add", "x_in0", "x_in1", "o_out0", "o_out1")
            e = {n: sem("out_" + n) for n in names}
            with nc.Block() as block:
                @block.sync
                def _(sp):
                    yin = [sem(f"out_yin{k}") for k in range(3)]
                    sp.dma_start(sqb[:, 0], sqs_s).then_inc(e["sq_in"], 16)
                    sp.dma_start(sqb[:, 1], sqa_s).then_inc(e["sq_in"], 16)
                    for m in range(RAW):
                        W.load(sp, m, m, 0, PIECE * m)
                    for k in range(KT):
                        if k >= 3:
                            sp.wait_ge(e["ylo"], k - 2)
                        src = (ys_s if k < KG else ya_s)[(k % KG) * P:(k % KG + 1) * P, :]
                        sp.dma_start(yf[:, k % 3], src).then_inc(yin[k % 3], 16)
                    for m in range(RAW, NPC):
                        W.load(sp, m, m, 0, PIECE * m)
                    with sp.Fori(1, D_MODEL // P) as n:
                        for s in range(NPC):
                            W.load(sp, n * NPC + s, s, n * P, PIECE * s)
                    for s in range(SPL):
                        W.load(sp, (D_MODEL // P) * NPC + s, s, 0, 0)

                @block.gpsimd
                def _(pool):
                    def residual(n, b, first, turn):
                        if not first:
                            pool.wait_ge(e[f"o_out{b}"], 32 * turn)
                            stand(pool, "pool")
                        pool.dma_start(XO[:, b, 0:TT - 1], x_prompt[0].rearrange("(m p) n -> p m n", p=P)[:, :, ds(n * P, P)]
                                       ).then_inc(e[f"x_in{b}"], 16)
                        pool.dma_start(XO[0:DEC, b, TT - 1], x_sample[0][:, ds(n * P, P)]).then_inc(e[f"x_in{b}"], 16)

                    def store(n, b):
                        pool.wait_ge(e["add"], 2 * n + 2)
                        stand(pool, "pool")
                        pool.dma_start(y_prompt[0].rearrange("(m p) n -> p m n", p=P)[:, :, ds(n * P, P)], XO[:, b, 0:TT - 1]
                                       ).then_inc(e[f"o_out{b}"], 16)
                        pool.dma_start(y_sample[0][:, ds(n * P, P)], XO[0:DEC, b, TT - 1]).then_inc(e[f"o_out{b}"], 16)
                    residual(0, 0, True, 0)
                    residual(1, 1, True, 0)
                    with pool.Fori(0, NCH // 2 - 1) as i:
                        for b in range(2):
                            store(2 * i + b, b)
                            residual(2 * i + b + 2, b, False, i + 1)
                    for b in range(2):
                        store(NCH - 2 + b, b)
                    for b in range(2):
                        pool.wait_ge(e[f"o_out{b}"], 32 * (NCH // 2))

                @block.scalar
                def _(act):
                    yin = [sem(f"out_yin{k}") for k in range(3)]
                    for w in range(2):
                        act.wait_ge(e["ss"], w + 1)
                        for src, dst in halves((GB, TB)[w], sqb[:, w]):
                            ins = S.activation(dst, src, ACT.Sqrt, bias=epsc[:], scale=1.0 / D_SSM)
                        ins.then_inc(e["rt"], 1)
                    for s in range(SPL):
                        W.split_hi(s, s, 1)
                    for k in range(KT):
                        act.wait_ge(e["sc"], k + 1)
                        S.copy(YH[:, k], yf[:, k % 3]).then_inc(e["yhi"], 1)

                    def part(n, gemm, tr):
                        for s in range(NPC):
                            if gemm:
                                m = s + SPL
                                W.split_hi(n * NPC + m, m, n * (NPC // RAW) + m // RAW + 1)
                            if gemm and s == NPC - 1:
                                act.wait_ge(W.mm, W.multiplied(n * NPC + s))
                                if tr:
                                    act.wait_ge(e["t_mm"], n)
                                S.copy(cols(OT, 0), group(GB, 0))
                                S.copy(cols(OT, 2), group(GB, 2)).then_inc(e["ga"], 1)
                    part(0, True, False)
                    with act.Fori(1, NCH) as n:
                        part(n, True, True)

                @block.vector
                def _(dve):
                    dve.sem_inc(W.lo, RAW)
                    for w in range(2):
                        dve.wait_ge(e["rt"], w + 1)
                        V.reciprocal(sqb[:, w], sqb[:, w]).then_inc(e["rr"], 1)
                    for s in range(SPL):
                        W.split_lo(s, s)
                    dve.wait_ge(e["rr"], 2)
                    yin = [sem(f"out_yin{k}") for k in range(3)]

                    def scale(k):
                        dve.wait_ge(yin[k % 3], 16 * (k // 3 + 1))
                        V.scalar_tensor_tensor(yf[:, k % 3], yf[:, k % 3], vec[:, 16 + k:17 + k], sqb[:, k // KG],
                                               ALU.mult, ALU.mult).then_inc(e["sc"], 1)
                    scale(0)
                    for k in range(KT):
                        if k + 1 < KT:
                            scale(k + 1)
                        dve.wait_ge(e["yhi"], k + 1)
                        V.tensor_tensor(YL[:, k], yf[:, k % 3], YH[:, k].bitcast(f32), ALU.subtract).then_inc(e["ylo"], 1)

                    def part(n, gemm, tr, b, turn):
                        for s in range(NPC):
                            if gemm:
                                m = s + SPL
                                W.split_lo(n * NPC + m, m)
                            if tr and s == 1:
                                dve.wait_ge(e["t_mm"], n)
                                dve.wait_ge(e[f"x_in{b}"], 32 * turn)
                                V.tensor_tensor(XO[:, b, 0:TT - 1], XO[:, b, 0:TT - 1],
                                                TB[:, 0:SEQ].rearrange("p (m n) -> p m n", n=P), ALU.add).then_inc(e["add"], 1)
                                V.tensor_tensor(XO[0:DEC, b, TT - 1], XO[0:DEC, b, TT - 1], TB[0:DEC, SEQ:SEQ + P],
                                                ALU.add).then_inc(e["add"], 1)
                            if gemm and s == NPC - 1:
                                dve.wait_ge(W.mm, W.multiplied(n * NPC + s))
                                if tr:
                                    dve.wait_ge(e["t_mm"], n)
                                V.tensor_copy(cols(OT, 1), group(GB, 1)).then_inc(e["gd"], 1)
                    part(0, True, False, 0, 0)
                    part(1, True, True, 0, 1)
                    with dve.Fori(0, NCH // 2 - 1) as i:
                        part(2 * i + 2, True, True, 1, i + 1)
                        part(2 * i + 3, True, True, 0, i + 2)
                    part(NCH, False, True, 1, NCH // 2)

                @block.tensor
                def _(pe):
                    W.credit("pe")
                    pe.wait_ge(e["sq_in"], 32)
                    for w, bank in ((0, GB), (1, TB)):
                        for b, (c, n) in enumerate(COLS):
                            ins = T.matmul(group(bank, b), ones[:], sqb[:, w, c:c + n], start=True, stop=True)
                        ins.then_inc(e["ss"], 1)

                    def part(n, gemm, tr):
                        for s in range(NPC):
                            if gemm:
                                if s == 0:
                                    if tr:
                                        pe.wait_ge(e["ga"], n)
                                        pe.wait_ge(e["gd"], n)
                                    else:
                                        pe.wait_ge(e["rt"], 2)
                                if not tr:
                                    pe.wait_ge(e["ylo"], PIECE * (s + 1))
                                W.multiply(n * NPC + s, s, PIECE * s, s == 0, s == NPC - 1)
                            if tr and s == 0:
                                pe.wait_ge(e["ga"], n)
                                pe.wait_ge(e["gd"], n)
                                pe.wait_ge(e["add"], 2 * (n - 1))
                                for m in range(TT):
                                    w = min(P, TOK - m * P)
                                    ins = T.transpose(TB[0:w, m * P:(m + 1) * P], OT[:, m * P:m * P + w], ident[:])
                                ins.then_inc(e["t_mm"], 1)
                    part(0, True, False)
                    with pe.Fori(1, NCH) as n:
                        part(n, True, True)
                    part(NCH, False, True)


_INS = ["x_prompt", "x_sample", "cache_k", "cache_v", "cache_logf", "state_ssm_re", "state_ssm_im",
        "norm_gain", "w_in", "b_f", "q_norm_gain", "k_norm_gain", "ssm_log_dt", "ssm_a_re", "ssm_a_im",
        "ssm_b_re", "ssm_b_im", "ssm_c_re", "ssm_c_im", "ssm_d", "w_glu", "b_glu",
        "ssm_out_norm", "att_out_norm", "w_out"]
_OUTS = [("y_prompt", (1, SEQ, D_MODEL)), ("y_sample", (1, DEC, D_MODEL)),
         ("k_prompt", (1, 1, SEQ, NH, HD)), ("v_prompt", (1, 1, SEQ, NH, HD)), ("logf_prompt", (1, 1, SEQ, NH)),
         ("hre_prompt", (1, 1, NG, NP)), ("him_prompt", (1, 1, NG, NP)),
         ("k_sample", (1, 1, DEC, NH, HD)), ("v_sample", (1, 1, DEC, NH, HD)), ("logf_sample", (1, 1, DEC, NH)),
         ("hre_sample", (1, 1, NG, NP)), ("him_sample", (1, 1, NG, NP))]


def kernel(**inputs):
    import numpy as _np
    import concourse.bacc as _bacc
    from concourse import mybir as _mybir
    from concourse.bass_utils import run_bass_kernel_spmd as _run

    nc = _bacc.Bacc("TRN2", target_bir_lowering=False, num_devices=1)
    arrays, args = {}, []
    for name in _INS:
        a = _np.ascontiguousarray(inputs[name])
        arrays[f"in_{name}"] = a
        args.append(nc.dram_tensor(f"in_{name}", a.shape, _mybir.dt.from_np(a.dtype), kind="ExternalInput").ap())
    for name, shape in _OUTS:
        args.append(nc.dram_tensor(f"out_{name}", shape, _mybir.dt.float32, kind="ExternalOutput").ap())
    build_kernel(nc, *args)
    r = _run(nc, [arrays], core_ids=[0])
    return tuple(r.results[0][f"out_{name}"] for name, _ in _OUTS)
```

```python
import math
from contextlib import ExitStack

import concourse.bass as bass
import concourse.mybir as mybir

D_MODEL, SEQ, DEC, PAST = 2048, 1024, 64, 128
D_SSM = D_ATT = 1024
NH, HD = 8, 128
NG, GC, NP = 64, 16, 64
D_PROJ = 2 * D_SSM + 4 * D_ATT + NH
EPS = 1e-6
P = 128
TOK = SEQ + DEC
KT = D_MODEL // P
TT = SEQ // P + 1
L = 8
NB = SEQ // L
NBS = DEC // L
SC = NB + 1 + NBS
HC = SC + 1
RAW, SPL = 4, 4
PIECE = 2
NLV = 7
AR, AI, WR, WI, MG, H0 = 0, 9, 18, 25, 32, 33
NPR = 35
PKW = NPR * 4 + 4 * 4 * GC + 1
CW = 384
COLS = ((0, CW), (CW, CW), (2 * CW, TOK - 2 * CW))
MAGIC = 12582912.0
NEG = -1e30


def build_kernel(nc, x_prompt, x_sample, cache_k, cache_v, cache_logf, state_ssm_re, state_ssm_im,
                 norm_gain, w_in, b_f, q_norm_gain, k_norm_gain, ssm_log_dt, ssm_a_re, ssm_a_im,
                 ssm_b_re, ssm_b_im, ssm_c_re, ssm_c_im, ssm_d, w_glu, b_glu,
                 ssm_out_norm, att_out_norm, w_out,
                 y_prompt, y_sample, k_prompt, v_prompt, logf_prompt, hre_prompt, him_prompt,
                 k_sample, v_sample, logf_sample, hre_sample, him_sample):
    f32, r32, bf16, i32 = mybir.dt.float32, mybir.dt.float32r, mybir.dt.bfloat16, mybir.dt.int32
    ALU, ACT, AX = mybir.AluOpType, mybir.ActivationFunctionType, mybir.AxisListType
    ds = bass.ds
    V, S, G, T = nc.vector, nc.scalar, nc.gpsimd, nc.tensor
    ctx = ExitStack()
    sems, phase = {}, [0]

    def sem(name):
        if name not in sems:
            sems[name] = nc.alloc_semaphore(name=f"{name}_{phase[0]}")
        return sems[name]

    def stand(eng, name):
        eng.sem_inc(sem("stand_" + name), 1)

    def free_semaphores():
        nc.clear_and_free_semaphores(list(sems.values()))
        nc.all_engine_barrier()
        sems.clear()
        phase[0] += 1

    def pool_of(stack):
        def sb(name, shape, dt=f32):
            return stack.enter_context(nc.sbuf_tensor(name, shape, dt))
        return sb

    class Order:

        def __init__(self, eng, name):
            self.eng, self.sem, self.base, self.n = eng, sem(name), 0, 0

        def step(self, ins):
            ins.then_inc(self.sem, 1)
            self.n += 1
            return self.base + self.n

        def then(self, ins):
            self.eng.wait_ge(self.sem, self.step(ins))

        def enter(self, it, per):
            self.start, self.per = self.n, per
            self.base = it * per

        def leave(self, count):
            assert self.n - self.start == self.per, ("steps", self.sem, self.n - self.start, self.per)
            self.base, self.n = 0, self.start + self.per * count

    def scratch(name, shape):
        return nc.dram_tensor(name, shape, f32).ap()

    pk_s = scratch("pk_s", [P, 8 * PKW])
    kpad_s = scratch("kpad_s", [P, 240])
    zg_s = scratch("zg_s", [D_SSM, TOK])
    zs_s = scratch("zs_s", [D_SSM, TOK])
    ya_s = scratch("ya_s", [D_ATT, TOK])
    ys_s = scratch("ys_s", [D_SSM, TOK])
    nc_s = scratch("nc_s", [NH, SEQ + PAST + DEC])
    sqa_s = scratch("sqa_s", [P, TOK])
    sqs_s = scratch("sqs_s", [P, TOK])
    w_in_v = w_in[0].rearrange("(k p) n -> p k n", p=P)
    w_glu_v = w_glu[0].rearrange("(k p) n -> p k n", p=P)
    w_out_v = w_out[0].rearrange("(k p) n -> p k n", p=P)

    with ctx:
        sb = pool_of(ctx)
        ident = sb("ident", [P, P])
        identb = sb("identb", [P, P], bf16)
        maskb = sb("maskb", [P, P], bf16)
        ones = sb("ones", [P, P])
        delta = sb("delta", [P, GC])
        vec = sb("vec", [P, 34])
        epsc = sb("epsc", [P, 1])
        wraw = sb("wraw", [P, RAW, PIECE, P])
        whi = sb("whi", [P, SPL, PIECE, P], r32)
        wlo = sb("wlo", [P, SPL, PIECE, P], r32)
        GB = ctx.enter_context(nc.psum_tensor("GB", [P, 3 * 512], f32))
        TB = ctx.enter_context(nc.psum_tensor("TB", [P, 5 * 512], f32))

        def group(bank, b, p=slice(0, P)):
            return bank[p, 512 * b:512 * b + COLS[b][1]]

        def cols(a, b):
            return a[:, COLS[b][0]:COLS[b][0] + COLS[b][1]]

        def halves(bank, a, p=slice(0, P)):
            return ((bank[p, 0:1024].rearrange("p (b c) -> p b c", b=2)[:, :, 0:CW],
                     a[:, 0:2 * CW].rearrange("p (b c) -> p b c", b=2)), (group(bank, 2, p), cols(a, 2)))

        class Weights:

            def __init__(self, tag, view, xh, xl):
                self.view, self.xh, self.xl, self.tag = view, xh, xl, tag
                self.w_in = [sem(f"{tag}_w_in{i}") for i in range(RAW)]
                self.hi, self.lo, self.mm = sem(f"{tag}_w_hi"), sem(f"{tag}_w_lo"), sem(f"{tag}_w_mm")

            def load(self, eng, m, s, col, k):
                eng.wait_ge(self.lo, m + 1)
                eng.dma_start(wraw[:, s % RAW], self.view[:, k:k + PIECE, ds(col, P)]).then_inc(self.w_in[s % RAW], 16)

            def split_hi(self, m, s, loads):
                S.wait_ge(self.w_in[s % RAW], 16 * loads)
                S.wait_ge(self.mm, m + 1)
                S.copy(whi[:, s % SPL], wraw[:, s % RAW]).then_inc(self.hi, 1)

            def split_lo(self, m, s):
                V.wait_ge(self.hi, m + 1)
                V.tensor_tensor(wlo[:, s % SPL], wraw[:, s % RAW], whi[:, s % SPL].bitcast(f32),
                                ALU.subtract).then_inc(self.lo, 1)

            def multiply(self, m, s, k, first, last, bank=GB, free=None):
                T.wait_ge(self.lo, m + 1 + RAW)
                for kk in range(PIECE):
                    for w, x in ((whi, self.xh), (whi, self.xl), (wlo, self.xh)):
                        for b, (c, n) in enumerate(COLS):
                            if free and kk == 0 and w is whi and x is self.xh:
                                free(b)
                            ins = T.matmul(bank[:, 512 * b:512 * b + n], w[:, s % SPL, kk], x[:, k + kk, c:c + n],
                                           start=first and kk == 0 and w is whi and x is self.xh,
                                           stop=last and kk == PIECE - 1 and w is wlo)
                ins.then_inc(self.mm, 1)

            def multiplied(self, m):
                return m + 1 + SPL

            def credit(self, which):
                if which == "pe":
                    T.sem_inc(self.mm, SPL)
                else:
                    V.sem_inc(self.lo, RAW)

        xs_stack = ctx.enter_context(ExitStack())
        XH = xs_stack.enter_context(nc.sbuf_tensor("XH", [P, KT, TOK], r32))
        XL = xs_stack.enter_context(nc.sbuf_tensor("XL", [P, KT, TOK], r32))
        with ExitStack() as st:
            sbp = pool_of(st)
            xt = sbp("xt", [P, 2, D_MODEL])
            gain = sbp("gain", [P, D_MODEL])
            junk = sbp("junk", [P, 1])
            ssq = sbp("ssq", [P, TT, 3])
            vin = sbp("vin", [34, P])
            pin = sbp("pin", [32, 5, P])
            ldt = sbp("ldt", [32, 2])
            cin = wraw[:].rearrange("p a b c -> p (a b c)").rearrange("p (i n) -> p i n", i=8)
            braw = sbp("braw", [P, 2, 512])
            prm = sbp("prm", [P, 5, 32])
            dtt = sbp("dtt", [P, 32])
            ath = sbp("ath", [P, 2, 32])
            arg = sbp("arg", [P, 14, 32])
            trg = sbp("trg", [P, 2, 14, 32])
            wk = sbp("wk", [P, 2, 14 * 32])
            mag = sbp("mag", [P, 9, 32])
            wki = sbp("wki", [P, 256], i32)
            cf = sbp("cf", [P, 8, 32])
            tmpb = (GB[:, 1024:1536], wk[:].rearrange("p a b -> p (a b)")[:, 0:512])
            pk = sbp("pk", [P, 8, PKW])
            ld_x = [sem("ld_x0"), sem("ld_x1")]
            ld_gain, ld_par, ld_c, st_pk = sem("ld_gain"), sem("ld_par"), sem("ld_c"), sem("st_pk")
            ident_done, par_t, par_ev = sem("ident_done"), sem("par_t"), sem("par_ev")
            sq_done, xs_done, x_t, x_hi, x_lo = (sem(n) for n in ("sq_done", "xs_done", "x_t", "x_hi", "x_lo"))
            sqrt_done, ssq_v, trg_in, trg_sin, c_t, pk_done = (
                sem(n) for n in ("sqrt_done", "ssq_v", "trg_in", "trg_sin", "c_t", "pk_done"))
            rows = [P] * (TT - 1) + [DEC]

            def pkv(row, n=1):
                return pk[:, :, 4 * row:4 * (row + n)].rearrange("p j (n q) -> p n j q", q=4)

            block = ctx.enter_context(ExitStack())
            with nc.Block() as block:
                @block.sync
                def _(sp):
                    def row128(a):
                        return a.rearrange("o (r p) -> (o r) p", p=P)
                    sp.dma_start(xt[:, 0], x_prompt[0, 0:P]).then_inc(ld_x[0], 16)
                    sp.dma_start(gain[:], norm_gain[0:1, :].to_broadcast([P, D_MODEL])).then_inc(ld_gain, 16)
                    for i, a in enumerate((ssm_a_re, ssm_a_im, state_ssm_re, state_ssm_im)):
                        a = a[0, 0] if len(a.shape) == 4 else a[0]
                        i = i if i < 2 else i + 1
                        sp.dma_start(pin[:, i].rearrange("r (g p) -> r g p", g=2),
                                     a.rearrange("(r g) p -> r g p", g=2)).then_inc(ld_par, 16)
                    sp.dma_start(ldt[:], ssm_log_dt[0].rearrange("(r g) -> r g", g=2)).then_inc(ld_par, 16)
                    sp.dma_start(vin[0:8], ssm_d[0].rearrange("(r g) c -> r (g c)", g=8)).then_inc(ld_par, 16)
                    sp.dma_start(vin[8:16], row128(b_glu)).then_inc(ld_par, 16)
                    sp.dma_start(vin[16:24], row128(ssm_out_norm)).then_inc(ld_par, 16)
                    sp.dma_start(vin[24:32], row128(att_out_norm)).then_inc(ld_par, 16)
                    sp.dma_start(vin[32:33], q_norm_gain).then_inc(ld_par, 16)
                    sp.dma_start(vin[33:34], k_norm_gain).then_inc(ld_par, 16)
                    for i, a in enumerate((ssm_c_re, ssm_c_im)):
                        for q in range(4):
                            for g in range(2):
                                src = a[0].rearrange("(q r g) c p -> q g r c p", q=4, g=2)[q, g]
                                sp.dma_start(cin[:, 4 * i + q, g * NP:(g + 1) * NP],
                                             src).then_inc(ld_c, 16)
                    for i, a in enumerate((ssm_b_re, ssm_b_im)):
                        for g in range(2):
                            sp.dma_start(braw[g * NP:(g + 1) * NP, i].rearrange("p (r c) -> p r c", c=GC),
                                         a[0].rearrange("(r g) p c -> g p r c", g=2)[g]).then_inc(ld_c, 16)
                    for m in range(1, TT):
                        if m >= 2:
                            sp.wait_ge(x_t, 4 * (m - 1))
                        src = x_prompt[0, m * P:(m + 1) * P] if m < TT - 1 else x_sample[0]
                        sp.dma_start(xt[0:rows[m], m % 2], src).then_inc(ld_x[m % 2], 16)
                    sp.wait_ge(pk_done, 1)
                    sp.dma_start(pk_s, pk[:].rearrange("p a b -> p (a b)")).then_inc(st_pk, 16)
                    sp.wait_ge(st_pk, 16)

                @block.gpsimd
                def _(pool):
                    o = Order(pool, "pool_order")
                    G.memset(junk[:], 0.0)
                    G.memset(epsc[:], EPS)
                    o.then(G.memset(ident[:], 0.0))
                    o.then(G.affine_select(out=ident[:], in_=ident[:], compare_op=ALU.not_equal, fill=1.0, base=0,
                                           pattern=[[-1, P]], channel_multiplier=1))
                    o.then(G.memset(ones[:], 1.0))
                    o.then(G.memset(identb[:], 0.0))
                    G.affine_select(out=maskb[:], in_=identb[:], compare_op=ALU.is_ge, fill=NEG, base=0,
                                    pattern=[[-1, P]], channel_multiplier=1).then_inc(ident_done, 1)
                    pool.wait_ge(ident_done, 1)
                    G.tensor_copy(identb[:], ident[:]).then_inc(ident_done, 1)

                @block.scalar
                def _(act):
                    act.wait_ge(ident_done, 2)
                    o = Order(act, "act_order")

                    def x_square(m):
                        act.wait_ge(ld_x[m % 2], 16 * (m // 2 + 1))
                        n = rows[m]
                        for h in range(2):
                            last = S.activation(GB[0:n, 0:1024], xt[0:n, m % 2, 1024 * h:1024 * (h + 1)], ACT.Square,
                                                accum_out=ssq[0:n, m, h:h + 1])
                            if h == 0:
                                o.then(last)
                        last.then_inc(sq_done, 1)
                        act.wait_ge(ssq_v, m + 1)
                        S.activation(ssq[0:n, m, 2:3], ssq[0:n, m, 0:1], ACT.Sqrt).then_inc(sqrt_done, 1)

                    def x_split(m):
                        n = rows[m]
                        for b in range(4):
                            act.wait_ge(x_t, 4 * m + b + 1)
                            S.copy(XH[:, 4 * b:4 * b + 4, m * P:m * P + n],
                                   TB[:, b * 512:(b + 1) * 512].rearrange("p (k t) -> p k t", k=4)[:, :, 0:n]
                                   ).then_inc(x_hi, 1)
                    x_square(0)
                    for m in range(TT):
                        if m + 1 < TT:
                            x_square(m + 1)
                        x_split(m)
                        if m == 2:
                            act.wait_ge(trg_in, 1)
                            S.activation(trg[:].rearrange("p a b c -> p (a b c)"),
                                         trg[:].rearrange("p a b c -> p (a b c)"), ACT.Sin).then_inc(trg_sin, 1)

                @block.tensor
                def _(pe):
                    pe.wait_ge(ident_done, 2)
                    pe.wait_ge(ld_par, 16 * 11)
                    dt_bc = sem("dt_bc")
                    pe.wait_ge(dt_bc, 1)
                    T.transpose(TB[:, 4 * 512:4 * 512 + 34], vin[:], ident[0:34, 0:34])
                    for i in range(5):
                        ins = T.transpose(TB[:, 4 * 512 + 64 + 32 * i:4 * 512 + 96 + 32 * i], pin[:, i], ident[0:32, 0:32])
                    ins.then_inc(par_t, 1)

                    def tiles(m):
                        n = rows[m]
                        pe.wait_ge(xs_done, m + 1)
                        for b in range(4):
                            if m:
                                pe.wait_ge(x_lo, 4 * (m - 1) + b + 1)
                            for k in range(4):
                                c = b * 512 + k * P
                                ins = T.transpose(TB[:, c:c + n], xt[0:n, m % 2, (4 * b + k) * P:(4 * b + k + 1) * P],
                                                  ident[0:n, 0:n])
                            ins.then_inc(x_t, 1)
                    for m in range(TT):
                        tiles(m)
                        if m == 0:
                            pe.wait_ge(ld_c, 16 * 20)
                            for i in range(8):
                                if i == 4:
                                    pe.wait_ge(par_ev, 3)
                                elif i == 0:
                                    pe.wait_ge(par_ev, 2)
                                ins = T.transpose(TB[:, 4 * 512 + (i % 4) * P:4 * 512 + (i % 4 + 1) * P], cin[:, i], ident[:])
                                if i % 4 == 3:
                                    ins.then_inc(c_t, 1)

                @block.vector
                def _(dve):
                    o = Order(dve, "dve_order")
                    dt_bc = sem("dt_bc")

                    def x_scale(m):
                        n = rows[m]
                        dve.wait_ge(sq_done, m + 1)
                        o.then(V.tensor_tensor(ssq[0:n, m, 0:1], ssq[0:n, m, 0:1], ssq[0:n, m, 1:2], ALU.add))
                        V.tensor_scalar(ssq[0:n, m, 0:1], ssq[0:n, m, 0:1], 1.0 / D_MODEL, EPS, ALU.mult, ALU.add
                                        ).then_inc(ssq_v, 1)
                        dve.wait_ge(sqrt_done, m + 1)
                        v, y, t = ssq[0:n, m, 0:1], ssq[0:n, m, 1:2], ssq[0:n, m, 2:3]
                        o.then(V.reciprocal(y, t))
                        o.then(V.tensor_tensor(t, y, y, ALU.mult))
                        o.then(V.scalar_tensor_tensor(t, t, -0.5, v, ALU.mult, ALU.mult))
                        o.then(V.scalar_tensor_tensor(y, t, 1.5, y, ALU.add, ALU.mult))
                        if m == 0:
                            dve.wait_ge(ld_gain, 16)
                        V.scalar_tensor_tensor(xt[0:n, m % 2], xt[0:n, m % 2], ssq[0:n, m, 1:2], gain[0:n],
                                               ALU.mult, ALU.mult).then_inc(xs_done, 1)

                    def x_rest(m):
                        n = rows[m]
                        for b in range(4):
                            dve.wait_ge(x_hi, 4 * m + b + 1)
                            tb = TB[:, b * 512:(b + 1) * 512].rearrange("p (k t) -> p k t", k=4)[:, :, 0:n]
                            V.tensor_tensor(XL[:, 4 * b:4 * b + 4, m * P:m * P + n], tb,
                                            XH[:, 4 * b:4 * b + 4, m * P:m * P + n].bitcast(f32),
                                            ALU.subtract).then_inc(x_lo, 1)

                    def exp_poly(out, x, n):
                        t, r = wk[:, 0, 0:n], wk[:, 1, 0:n]
                        o.then(V.tensor_scalar(x, x, -87.0, 88.0, ALU.max, ALU.min))
                        o.then(V.tensor_scalar(t, x, 1.0 / math.log(2.0), MAGIC, ALU.mult, ALU.add))
                        o.then(V.tensor_scalar(t, t, -MAGIC, None, ALU.add))
                        o.then(V.scalar_tensor_tensor(r, t, -0.693359375, x, ALU.mult, ALU.add))
                        o.then(V.scalar_tensor_tensor(r, t, 2.12194440e-4, r, ALU.mult, ALU.add))
                        o.then(V.tensor_scalar(out, r, 1.0 / 5040, None, ALU.mult))
                        for c in (1.0 / 720, 1.0 / 120, 1.0 / 24, 1.0 / 6, 0.5, 1.0):
                            o.then(V.scalar_tensor_tensor(out, out, c, r, ALU.add, ALU.mult))
                        o.then(V.tensor_scalar(out, out, 1.0, None, ALU.add))
                        o.then(V.tensor_scalar(wki[:, 0:n], t, 127.0, 8388608.0, ALU.add, ALU.mult))
                        o.then(V.tensor_tensor(out, out, wki[:, 0:n].bitcast(f32), ALU.mult))

                    dve.wait_ge(ld_par, 16 * 11)
                    V.tensor_copy(pin[:, 2].rearrange("r (g p) -> r g p", g=2),
                                  ldt[:].unsqueeze(2).to_broadcast([32, 2, NP])).then_inc(dt_bc, 1)
                    dve.wait_ge(ident_done, 2)
                    V.tensor_reduce(delta[:], ident[:].rearrange("p (g c) -> p c g", c=GC), AX.X, ALU.add)
                    x_scale(0)
                    dve.wait_ge(par_t, 1)
                    V.tensor_copy(vec[:], TB[:, 4 * 512:4 * 512 + 34]).then_inc(par_ev, 1)
                    V.tensor_copy(prm[:].rearrange("p a b -> p (a b)"), TB[:, 4 * 512 + 64:4 * 512 + 224]).then_inc(par_ev, 1)
                    dve.wait_ge(par_ev, 2)
                    x_scale(1)
                    x_rest(0)
                    dve.wait_ge(c_t, 1)
                    cre = pk[:, :, NPR * 4 + 128:NPR * 4 + 192]
                    cim = pk[:, :, NPR * 4 + 192:NPR * 4 + 256]
                    V.tensor_copy(cre, TB[:, 4 * 512:5 * 512].rearrange("p (j c) -> p j c", j=8)).then_inc(par_ev, 1)
                    dve.wait_ge(c_t, 2)
                    o.then(V.tensor_copy(cim, TB[:, 4 * 512:5 * 512].rearrange("p (j c) -> p j c", j=8)))
                    x_scale(2)
                    x_rest(1)
                    exp_poly(dtt[:], prm[:, 2], 32)
                    o.then(V.tensor_tensor(ath[:], prm[:, 0:2], dtt[:].unsqueeze(1).to_broadcast([P, 2, 32]), ALU.mult))
                    for k in range(14):
                        f = float(k + 1) if k < 8 else float(L << (k - 7))
                        last = o.step(V.tensor_scalar(arg[:, k], ath[:, 1], f, None, ALU.mult))
                    dve.wait_ge(o.sem, last)
                    argf = arg[:].rearrange("p a b -> p (a b)")
                    C1, C2, C3 = 6.28125, 1.9350051879882812e-3, 3.0199159819567e-7
                    for i, quarter in ((0, 0.25), (1, 0.0)):
                        t = wk[:, i]
                        r = trg[:, i].rearrange("p a b -> p (a b)")
                        o.then(V.tensor_scalar(t, argf, 1.0 / (2 * math.pi), quarter, ALU.mult, ALU.add))
                        o.then(V.tensor_scalar(t, t, MAGIC, None, ALU.add))
                        o.then(V.tensor_scalar(t, t, -MAGIC, None, ALU.add))
                        o.then(V.scalar_tensor_tensor(r, t, -C1, argf, ALU.mult, ALU.add))
                        o.then(V.scalar_tensor_tensor(r, t, -C2, r, ALU.mult, ALU.add))
                        o.then(V.scalar_tensor_tensor(r, t, -C3, r, ALU.mult, ALU.add))
                        if quarter:
                            o.then(V.tensor_scalar(r, r, math.pi / 2, None, ALU.add))
                        ins = V.tensor_scalar(r, r, -3.1415925, 3.1415925, ALU.max, ALU.min)
                        if quarter:
                            o.then(ins)
                        else:
                            ins.then_inc(trg_in, 1)
                    dve.wait_ge(trg_in, 1)
                    x_scale(3)
                    x_rest(2)
                    for k in range(8):
                        last = o.step(V.tensor_scalar(mag[:, k + 1], ath[:, 0], float(k + 1), None, ALU.mult))
                    dve.wait_ge(o.sem, last)
                    xm = tmpb[0][:, 0:256]
                    o.then(V.tensor_copy(xm, mag[:, 1:9].rearrange("p a b -> p (a b)")))
                    exp_poly(mag[:, 1:9].rearrange("p a b -> p (a b)"), xm, 256)
                    x_scale(4)
                    x_rest(3)
                    dve.wait_ge(trg_sin, 1)
                    o.then(V.memset(pkv(AR), 1.0))
                    o.then(V.memset(pkv(AI), 0.0))

                    def as_jq(a):
                        return a.rearrange("p n (j q) -> p n j q", q=4)
                    for k in range(8):
                        V.tensor_tensor(pkv(AR + 1 + k), as_jq(mag[:, k + 1:k + 2]), as_jq(trg[:, 0, k:k + 1]), ALU.mult)
                        last = o.step(V.tensor_tensor(pkv(AI + 1 + k), as_jq(mag[:, k + 1:k + 2]),
                                                      as_jq(trg[:, 1, k:k + 1]), ALU.mult))
                    for lv in range(NLV):
                        o.step(V.tensor_copy(pkv(WR + lv), as_jq(trg[:, 0, 7 + lv:8 + lv])))
                        o.step(V.tensor_scalar(pkv(WI + lv), as_jq(trg[:, 1, 7 + lv:8 + lv]), -1.0, None, ALU.mult))
                    o.step(V.tensor_copy(pkv(MG), as_jq(mag[:, 8:9])))
                    o.step(V.tensor_copy(pkv(H0), as_jq(prm[:, 3:4])))
                    last = o.step(V.tensor_copy(pkv(H0 + 1), as_jq(prm[:, 4:5])))
                    dve.wait_ge(o.sem, last)
                    dve.wait_ge(par_ev, 2)
                    o.then(V.tensor_copy(pk[:, :, PKW - 1], vec[:, 0:8]))
                    ar, ai = prm[:, 0], prm[:, 1]
                    nr, ni, den, t1 = cf[:, 0], cf[:, 1], cf[:, 2], cf[:, 3]
                    jq = lambda a: a.rearrange("p (j q) -> p j q", q=4)
                    o.then(V.tensor_scalar(jq(nr), pkv(AR + 1)[:, 0], -1.0, None, ALU.add))
                    o.then(V.tensor_copy(jq(ni), pkv(AI + 1)[:, 0]))
                    o.then(V.tensor_tensor(den, ar, ar, ALU.mult))
                    o.then(V.tensor_tensor(t1, ai, ai, ALU.mult))
                    o.then(V.tensor_tensor(den, den, t1, ALU.add))
                    o.then(V.reciprocal(den, den))
                    for i, (a, b, op) in enumerate(((nr, ni, ALU.add), (ni, nr, ALU.subtract))):
                        c = cf[:, 4 + i]
                        o.then(V.tensor_tensor(c, a, ar, ALU.mult))
                        o.then(V.tensor_tensor(t1, b, ai, ALU.mult))
                        o.then(V.tensor_tensor(c, c, t1, op))
                        o.then(V.tensor_tensor(c, c, den, ALU.mult))
                    x_scale(5)
                    x_rest(4)
                    dve.wait_ge(ld_c, 16 * 20)
                    v3 = lambda a: a.rearrange("p (r c) -> p r c", c=GC)
                    for i, op in ((0, ALU.subtract), (1, ALU.add)):
                        c0 = cf[:, 4].unsqueeze(2).to_broadcast([P, 32, GC])
                        c1 = cf[:, 5].unsqueeze(2).to_broadcast([P, 32, GC])
                        o.then(V.tensor_tensor(v3(tmpb[0]), v3(braw[:, i]), c0, ALU.mult))
                        o.then(V.tensor_tensor(v3(tmpb[1]), v3(braw[:, 1 - i]), c1, ALU.mult))
                        out = pk[:, :, NPR * 4 + 64 * i:NPR * 4 + 64 * (i + 1)]
                        ins = V.tensor_tensor(out, tmpb[0].rearrange("p (j c) -> p j c", j=8),
                                              tmpb[1].rearrange("p (j c) -> p j c", j=8), op)
                        if i == 0:
                            o.then(ins)
                        else:
                            ins.then_inc(pk_done, 1)
                    for m in range(5, TT):
                        if m + 1 < TT:
                            x_scale(m + 1)
                        x_rest(m)

        with ExitStack() as st:
            sbp = pool_of(st)
            U = sbp("U", [P, 8 * SC])
            Ug = U[:].rearrange("p (g c) -> p g c", c=SC)
            UZ = sbp("UZ", [P, TOK])
            UC = sbp("UC", [P, 1024])
            UCS = sbp("UCS", [P, 1024])
            SS = sbp("SS", [P, 2, 4 * SC])
            M1 = sbp("M1", [P, 2, 4 * SC])
            M2 = sbp("M2", [P, 2, 4 * SC])
            TR = sbp("TR", [P, 2, 4, SC])
            DC = sbp("DC", [P, 4, SC])
            H = sbp("H", [P, 8, HC])
            LS = sbp("LS", [P, 8, P])
            Q = sbp("Q", [P, 8, 9 * GC])
            MT = sbp("MT", [P, 8, P])
            KS = sbp("KS", [P, P])
            PJ = sbp("PJ", [P, PKW])
            BD = sbp("BD", [P, 8, 2 * GC])
            FB = sbp("FB", [P, 16])
            FS = sbp("FS", [16, P])
            flat = lambda a: a.rearrange("p a b -> p (a b)")
            GR = flat(M1[:])[:, 0:1024].rearrange("p (a q r c) -> p a q r c", a=2, q=4, r=L)
            GT = flat(SS[:])[:, 0:1024].rearrange("p (a q r c) -> p a q r c", a=2, q=4, r=L)
            Y = flat(SS[:]).rearrange("p (g c) -> p g c", c=SC)
            row = lambda r, n=1: PJ[:, 4 * r:4 * (r + n)].rearrange("p (n q) -> p n q", q=4)
            bc_ = lambda i: PJ[:, NPR * 4 + 64 * i:NPR * 4 + 64 * (i + 1)].rearrange("p (q c) -> p q c", c=GC)
            W = Weights("ssm", w_in_v, XH, XL)
            NPC = 2 * KT // PIECE
            names = ("pj_in", "g_ready", "bd_ready", "q_ready", "t_ready", "ls_mm", "k_mm", "ls_act", "ls_dve", "ks_ready",
                     "kpad_out", "mt_in", "ga", "gd", "st1_mm", "st1_act", "st1_dve", "st2_mm", "st2_act", "st2_dve",
                     "s_mm", "s_act", "m1_done", "m2_done", "g_done", "scan_done", "p1_done", "p2_done",
                     "h_dve", "h_pool", "y_mm", "y_act", "y_dve", "yt_mm", "yt_act", "yt_dve", "z_mm", "z_act", "zg_out", "zs_out",
                     "fb_ready", "fin_mm", "fin_ev", "fin_out", "dec_ready", "zero_done")
            e = {n: sem("ssm_" + n) for n in names}

            with nc.Block() as block:
                @block.sync
                def _(sp):
                    with sp.Fori(0, 8) as j:
                        for s in range(NPC):
                            col = j * P + (0 if s < NPC // 2 else D_SSM)
                            W.load(sp, j * NPC + s, s, col, PIECE * (s % (NPC // 2)))
                            if s == NPC - 1:
                                sp.wait_ge(e["y_mm"], j)
                                sp.wait_ge(e["kpad_out"], 16 * (j + 2))
                                for r in range(L):
                                    sp.dma_start(MT[r * GC:(r + 1) * GC],
                                                  kpad_s[:, GC * r:GC * r + P].rearrange("(g c) n -> c g n", g=8)
                                                  ).then_inc(e["mt_in"], 16)
                    for s in range(SPL):
                        W.load(sp, 8 * NPC + s, s, 0, 0)

                @block.scalar
                def _(act):
                    act.wait_ge(e["zero_done"], 1)
                    act.dma_start(kpad_s[:, 0:112], UC[:, 0:112]).then_inc(e["kpad_out"], 16)
                    for s in range(SPL):
                        W.split_hi(s, s, 1)
                    with act.Fori(0, 8) as j:
                        for s in range(NPC):
                            m = s + SPL
                            if s == 0:
                                act.wait_ge(e["g_ready"], j)
                                act.wait_ge(e["bd_ready"], j)
                                act.wait_ge(e["q_ready"], j)
                                act.wait_ge(e["ks_ready"], j)
                                act.wait_ge(e["dec_ready"], j)
                                act.wait_ge(e["s_act"], 4 * j)
                                act.dma_start(PJ[:], pk_s[:, ds(j * PKW, PKW)]).then_inc(e["pj_in"], 16)
                            if s == 7:
                                act.wait_ge(W.mm, W.multiplied(j * NPC + s))
                                act.wait_ge(e["zg_out"], 16 * j)
                                S.copy(cols(UZ, 0), group(GB, 0)).then_inc(e["ga"], 1)
                                S.copy(cols(UZ, 2), group(GB, 2)).then_inc(e["ga"], 1)
                            if s == NPC - 1:
                                act.wait_ge(W.mm, W.multiplied(j * NPC + s))
                                for src, dst in halves(GB, U):
                                    S.activation(dst, src, ACT.Silu).then_inc(e["ga"], 1)
                            W.split_hi(j * NPC + m, m, j * (NPC // RAW) + m // RAW + 1)
                            if s == 7:
                                act.wait_ge(e["ls_mm"], j + 1)
                                S.copy(LS[:, 0:4], TB[:, 0:512].rearrange("p (a b) -> p a b", a=4)).then_inc(e["ls_act"], 1)
                            if s == 6:
                                act.wait_ge(e["ks_ready"], j + 1)
                                act.dma_start(kpad_s[:, 112:240], KS[:]).then_inc(e["kpad_out"], 16)
                            if s == 8:
                                act.wait_ge(e["st1_mm"], j + 1)
                                S.copy(UC[:].rearrange("p (g r c) -> p r g c", g=8, r=L)[:, 0:4],
                                       TB[:, 3 * 512:4 * 512].rearrange("p (r g c) -> p r g c", r=4, g=8))
                                S.copy(UCS[0:8].rearrange("p (g r c) -> p r g c", g=8, r=L)[:, 0:4],
                                       TB[0:8, 0:512].rearrange("p (r g c) -> p r g c", r=4, g=8)).then_inc(e["st1_act"], 1)
                            if s == 9:
                                act.wait_ge(e["st2_mm"], j + 1)
                                act.wait_ge(e["zs_out"], 16 * j)
                                S.copy(Ug[:, 0:4, 0:NB], TB[:, 2 * 512:3 * 512].rearrange("p (g c) -> p g c", g=4)
                                       ).then_inc(e["st2_act"], 1)
                            if s == 10:
                                act.wait_ge(e["s_mm"], j + 1)
                                for b in range(3):
                                    n = min(3, 8 - 3 * b) * SC
                                    S.copy(flat(SS[:])[:, 3 * b * SC:3 * b * SC + n], TB[:, 512 * b:512 * b + n]
                                           ).then_inc(e["s_act"], 1)
                                act.wait_ge(e["s_act"], 4 * j + 3)
                                S.copy(flat(SS[:]).rearrange("p (a c) -> p a c", c=SC)[:, :, NB],
                                       PJ[:, 4 * H0:4 * H0 + 8]).then_inc(e["s_act"], 1)
                            if s == 13:
                                act.wait_ge(e["y_mm"], j + 1)
                                S.copy(Y[:, 0:3], TB[:, 3 * 512:3 * 512 + 3 * SC].rearrange("p (g c) -> p g c", g=3))
                                S.copy(Y[:, 6:8], TB[:, 0:2 * SC].rearrange("p (g c) -> p g c", g=2)).then_inc(e["y_act"], 1)
                            if s == 14:
                                act.wait_ge(e["yt_mm"], j + 1)
                                S.copy(UC[:].rearrange("p (t g c) -> p g t c", t=L, g=8)[:, 0:4],
                                       TB[:, 512:1024].rearrange("p (g t c) -> p g t c", g=4, t=L))
                                S.copy(UCS[0:8].rearrange("p (t g c) -> p g t c", t=L, g=8)[:, 0:4],
                                       TB[0:8, 3 * 512:4 * 512].rearrange("p (g t c) -> p g t c", g=4, t=L)).then_inc(e["yt_act"], 1)
                            if s == 15:
                                act.wait_ge(e["ga"], 4 * j + 4)
                                act.dma_start(zs_s[ds(j * P, P), :], U[:, 0:TOK]).then_inc(e["zs_out"], 16)
                                act.wait_ge(e["z_mm"], j + 1)
                                zt = lambda a: a.rearrange("p (c t) -> p t c", t=L)
                                for hlf in range(2):
                                    S.activation(zt(UZ[:, 0:SEQ])[:, 4 * hlf:4 * hlf + 4],
                                                 TB[:, 512 * (1 + hlf):512 * (2 + hlf)].rearrange("p (t c) -> p t c", t=4), ACT.Gelu)
                                S.activation(zt(UZ[:, SEQ:TOK]), TB[:, 0:DEC].rearrange("p (t c) -> p t c", t=L),
                                             ACT.Gelu).then_inc(e["z_act"], 1)
                                act.wait_ge(e["z_act"], j + 1)
                                act.dma_start(zg_s[ds(j * P, P), :], UZ[:]).then_inc(e["zg_out"], 16)
                                act.wait_ge(e["fin_ev"], j + 1)
                                for i, dst in enumerate((hre_prompt, him_prompt, hre_sample, him_sample)):
                                    act.dma_start(dst[0, 0, ds(8 * j, 8), :],
                                                  FS[8 * (i // 2):8 * (i // 2) + 8, (i % 2) * NP:(i % 2 + 1) * NP]
                                                  ).then_inc(e["fin_out"], 16)
                    act.wait_ge(e["zs_out"], 16 * 8)
                    act.wait_ge(e["zg_out"], 16 * 8)
                    act.wait_ge(e["fin_out"], 64 * 8)
                    act.wait_ge(W.w_in[0], 16 * (8 * NPC // RAW + 1))
                    act.wait_ge(W.w_in[1], 16 * (8 * NPC // RAW + 1))

                @block.vector
                def _(dve):
                    o = Order(dve, "dve_ssm")
                    V.memset(UC[:, 0:112], 0.0).then_inc(e["zero_done"], 1)
                    V.memset(BD[:], 0.0).then_inc(e["zero_done"], 1)
                    V.memset(H[:, :, 0:1], 0.0).then_inc(e["zero_done"], 1)
                    dve.wait_ge(e["zero_done"], 3)
                    dve.sem_inc(W.lo, RAW)
                    for s in range(SPL):
                        W.split_lo(s, s)
                    with dve.Fori(0, 8) as j:
                        o.enter(j, 4)
                        for s in range(NPC):
                            m = s + SPL
                            if s == 7:
                                dve.wait_ge(W.mm, W.multiplied(j * NPC + s))
                                dve.wait_ge(e["zg_out"], 16 * j)
                                V.tensor_copy(cols(UZ, 1), group(GB, 1)).then_inc(e["gd"], 1)
                            W.split_lo(j * NPC + m, m)
                            if s == 0:
                                dve.wait_ge(e["pj_in"], 16 * (j + 1))
                                dve.wait_ge(e["z_mm"], j)
                                o.then(V.tensor_copy(DC[:], row(MG)[:, 0].unsqueeze(2).to_broadcast([P, 4, SC])))
                                V.memset(DC[:, :, 0:NB + 1:NB], 0.0).then_inc(e["dec_ready"], 1)
                                for i in range(2):
                                    for g in range(2):
                                        ins = V.tensor_copy(BD[i * NP:(i + 1) * NP, g::2, g * GC:(g + 1) * GC],
                                                            bc_(i)[g * NP:(g + 1) * NP])
                                ins.then_inc(e["bd_ready"], 1)
                                qa = lambda base: row(base, 9).rearrange("p r q -> p q r").unsqueeze(3).to_broadcast([P, 4, 9, GC])
                                qc = lambda i: bc_(i).unsqueeze(2).to_broadcast([P, 4, 9, GC])
                                q4 = lambda t: t[:, 0:576].rearrange("p (q r c) -> p q r c", q=4, r=9)
                                q3 = lambda t, g: t[g * NP:(g + 1) * NP, 0:576].rearrange("p (q n) -> p q n", q=4)
                                V.tensor_tensor(q4(UC), qa(AR), qc(2), ALU.mult)
                                o.then(V.tensor_tensor(q4(UCS), qa(AI), qc(3), ALU.mult))
                                for g in range(2):
                                    ins = V.tensor_tensor(Q[0:NP, g::2], q3(UC, g), q3(UCS, g), ALU.subtract)
                                o.then(ins)
                                V.tensor_tensor(q4(UC), qa(AI), qc(2), ALU.mult)
                                o.then(V.tensor_tensor(q4(UCS), qa(AR), qc(3), ALU.mult))
                                for g in range(2):
                                    ins = V.scalar_tensor_tensor(Q[NP:P, g::2], q3(UC, g), -1.0, q3(UCS, g), ALU.mult, ALU.subtract)
                                ins.then_inc(e["q_ready"], 1)
                            if s == 5:
                                dve.wait_ge(e["k_mm"], j + 1)
                                dve.wait_ge(e["kpad_out"], 16 * (j + 1))
                                V.tensor_copy(KS[:, GC:P], TB[:, 2 * 512 + GC:2 * 512 + P])
                                V.scalar_tensor_tensor(KS[:, 0:GC], delta[:], PJ[:, PKW - 1:PKW], TB[:, 2 * 512:2 * 512 + GC],
                                                       ALU.mult, ALU.add).then_inc(e["ks_ready"], 1)
                            if s == 7:
                                dve.wait_ge(e["ls_mm"], j + 1)
                                V.tensor_copy(LS[:, 4:8], TB[:, 512:1024].rearrange("p (a b) -> p a b", a=4)).then_inc(e["ls_dve"], 1)
                            if s == 8:
                                dve.wait_ge(e["st1_mm"], j + 1)
                                V.tensor_copy(UC[:].rearrange("p (g r c) -> p r g c", g=8, r=L)[:, 4:8],
                                              TB[:, 4 * 512:5 * 512].rearrange("p (r g c) -> p r g c", r=4, g=8))
                                V.tensor_copy(UCS[0:8].rearrange("p (g r c) -> p r g c", g=8, r=L)[:, 4:8],
                                              TB[0:8, 512:1024].rearrange("p (r g c) -> p r g c", r=4, g=8)).then_inc(e["st1_dve"], 1)
                            if s == 9:
                                dve.wait_ge(e["st2_mm"], j + 1)
                                dve.wait_ge(e["zs_out"], 16 * j)
                                V.memset(Ug[:, :, NB:NB + 1], 0.0)
                                V.tensor_copy(Ug[:, 4:8, 0:NB], TB[:, 3 * 512:4 * 512].rearrange("p (g c) -> p g c", g=4))
                                V.tensor_copy(Ug[:, :, NB + 1:SC], TB[:, 4 * 512:4 * 512 + DEC].rearrange("p (g c) -> p g c", g=8)
                                              ).then_inc(e["st2_dve"], 1)
                            if s == 10:
                                th = lambda i: TR[:, i].rearrange("p a b -> p (a b)")
                                tr = lambda i: th(i).unsqueeze(1).to_broadcast([P, 2, 4 * SC])
                                dve.wait_ge(e["s_act"], 4 * (j + 1))
                                dve.wait_ge(e["t_ready"], j + 1)
                                V.tensor_tensor(M1[:], SS[:], tr(0), ALU.mult)
                                V.tensor_tensor(M2[:, 0], SS[:, 0], th(1), ALU.mult).then_inc(e["m1_done"], 1)
                                dve.wait_ge(e["m1_done"], j + 1)
                                dve.wait_ge(e["m2_done"], j + 1)
                                V.tensor_tensor(SS[:, 0], M1[:, 0], M2[:, 1], ALU.subtract).then_inc(e["g_done"], 1)
                                V.tensor_tensor(SS[:, 1], M1[:, 1], M2[:, 0], ALU.add).then_inc(e["g_done"], 1)
                                dcf = DC[:].rearrange("p a b -> p (a b)")
                                for i in range(2):
                                    dve.wait_ge(e["g_done"], 2 * j + 2)
                                    V.tensor_tensor_scan(M1[:, i], dcf, SS[:, i], 0.0, ALU.mult, ALU.add).then_inc(e["scan_done"], 1)
                                dve.wait_ge(e["scan_done"], 2 * j + 2)
                                V.tensor_tensor(SS[:], M1[:], tr(0), ALU.mult)
                                V.tensor_tensor(M2[:, 1], M1[:, 1], th(1), ALU.mult).then_inc(e["p1_done"], 1)
                                dve.wait_ge(e["p1_done"], j + 1)
                                dve.wait_ge(e["p2_done"], j + 1)
                                h4 = lambda t, i, g: t[g * NP:(g + 1) * NP, i].rearrange("p (q c) -> p q c", q=4)
                                V.tensor_tensor(H[0:NP, 1::2, 1:HC], h4(SS, 0, 1), h4(M2, 1, 1), ALU.add)
                                V.tensor_tensor(H[NP:P, 1::2, 1:HC], h4(SS, 1, 1), h4(M2, 0, 1), ALU.subtract)
                                V.tensor_tensor(H[NP:P, 0::2, 1:HC], h4(SS, 1, 0), h4(M2, 0, 0), ALU.subtract).then_inc(e["h_dve"], 1)
                            if s == 13:
                                dve.wait_ge(e["h_dve"], j + 1)
                                dve.wait_ge(e["h_pool"], j + 1)
                                V.tensor_copy(FB[:, 0:8], H[:, :, NB])
                                V.tensor_copy(FB[:, 8:16], H[:, :, HC - 1]).then_inc(e["fb_ready"], 1)
                                dve.wait_ge(e["y_mm"], j + 1)
                                V.tensor_copy(Y[:, 3:6], TB[:, 4 * 512:4 * 512 + 3 * SC].rearrange("p (g c) -> p g c", g=3)
                                              ).then_inc(e["y_dve"], 1)
                            if s == 14:
                                dve.wait_ge(e["yt_mm"], j + 1)
                                V.tensor_copy(UC[:].rearrange("p (t g c) -> p g t c", t=L, g=8)[:, 4:8],
                                              TB[:, 1024:1536].rearrange("p (g t c) -> p g t c", g=4, t=L))
                                V.tensor_copy(UCS[0:8].rearrange("p (t g c) -> p g t c", t=L, g=8)[:, 4:8],
                                              TB[0:8, 4 * 512:5 * 512].rearrange("p (g t c) -> p g t c", g=4, t=L)).then_inc(e["yt_dve"], 1)
                            if s == 15:
                                dve.wait_ge(e["fin_mm"], j + 1)
                                dve.wait_ge(e["fin_out"], 64 * j)
                                V.tensor_copy(FS[:], TB[0:16, 4 * 512:4 * 512 + P]).then_inc(e["fin_ev"], 1)
                    o.leave(8)

                @block.gpsimd
                def _(pool):
                    o = Order(pool, "pool_ssm")
                    PO = 32
                    with pool.Fori(0, 8) as j:
                        o.enter(j, PO)
                        pool.wait_ge(e["pj_in"], 16 * (j + 1))
                        pool.wait_ge(e["p1_done"], j)
                        pool.wait_ge(e["z_mm"], j)
                        stand(pool, "pool")
                        a = lambda base: row(base, L).rearrange("p r q -> p q r").unsqueeze(3).to_broadcast([P, 4, L, GC])
                        b = lambda i: bc_(i).unsqueeze(2).to_broadcast([P, 4, L, GC])
                        G.tensor_tensor(GT[:, 0], a(AR), b(0), ALU.mult)
                        o.then(G.tensor_tensor(GT[:, 1], a(AI), b(1), ALU.mult))
                        o.then(G.tensor_tensor(GR[:, 0], GT[:, 0], GT[:, 1], ALU.subtract))
                        G.tensor_tensor(GT[:, 0], a(AR), b(1), ALU.mult)
                        o.then(G.tensor_tensor(GT[:, 1], a(AI), b(0), ALU.mult))
                        G.tensor_tensor(GR[:, 1], GT[:, 0], GT[:, 1], ALU.add).then_inc(e["g_ready"], 1)
                        G.memset(TR[:, 0, :, 0:1], 1.0)
                        o.then(G.memset(TR[:, 1, :, 0:1], 0.0))
                        for lv in range(NLV):
                            n = 1 << lv
                            ta = M2[:, 0, 0:4 * n].rearrange("p (q c) -> p q c", q=4)
                            tb = M2[:, 1, 0:4 * n].rearrange("p (q c) -> p q c", q=4)
                            wr = row(WR + lv)[:, 0].unsqueeze(2).to_broadcast([P, 4, n])
                            wi = row(WI + lv)[:, 0].unsqueeze(2).to_broadcast([P, 4, n])
                            re, im = TR[:, 0, :, 0:n], TR[:, 1, :, 0:n]
                            G.tensor_tensor(ta, re, wr, ALU.mult)
                            o.then(G.tensor_tensor(tb, im, wi, ALU.mult))
                            o.then(G.tensor_tensor(TR[:, 0, :, n:2 * n], ta, tb, ALU.subtract))
                            G.tensor_tensor(ta, re, wi, ALU.mult)
                            o.then(G.tensor_tensor(tb, im, wr, ALU.mult))
                            o.then(G.tensor_tensor(TR[:, 1, :, n:2 * n], ta, tb, ALU.add))
                        stand(pool, "pool")
                        G.tensor_copy(TR[:].rearrange("p a q c -> p (a q) c")[:, :, NB:SC],
                                      TR[:].rearrange("p a q c -> p (a q) c")[:, :, 0:NBS + 1]).then_inc(e["t_ready"], 1)
                        th = TR[:, 1].rearrange("p a b -> p (a b)")
                        pool.wait_ge(e["t_ready"], j + 1)
                        pool.wait_ge(e["s_act"], 4 * (j + 1))
                        G.tensor_tensor(M2[:, 1], SS[:, 1], th, ALU.mult).then_inc(e["m2_done"], 1)
                        pool.wait_ge(e["scan_done"], 2 * j + 1)
                        G.tensor_tensor(M2[:, 0], M1[:, 0], th, ALU.mult).then_inc(e["p2_done"], 1)
                        pool.wait_ge(e["p1_done"], j + 1)
                        h4 = lambda t, i, g: t[g * NP:(g + 1) * NP, i].rearrange("p (q c) -> p q c", q=4)
                        G.tensor_tensor(H[0:NP, 0::2, 1:HC], h4(SS, 0, 0), h4(M2, 1, 0), ALU.add).then_inc(e["h_pool"], 1)
                    o.leave(8)

                @block.tensor
                def _(pe):
                    pe.wait_ge(e["zero_done"], 3)
                    W.credit("pe")
                    gb = (2, 3, 4)
                    with pe.Fori(0, 8) as j:
                        for s in range(NPC):
                            free = None
                            if s == 0:
                                def free(b):
                                    if b == 0:
                                        pe.wait_ge(e["ga"], 4 * j)
                            if s == 8:
                                def free(b):
                                    pe.wait_ge(e["gd"] if b == 1 else e["ga"], j + 1 if b == 1 else 4 * j + 1 + b // 2)
                            k = PIECE * (s % 8)
                            W.multiply(j * NPC + s, s, k, k == 0, k == KT - PIECE, free=free)
                            if s == 5:
                                pe.wait_ge(e["z_act"], j)
                                pe.wait_ge(e["bd_ready"], j + 1)
                                pe.wait_ge(e["q_ready"], j + 1)
                                for g in range(8):
                                    q = g // 2
                                    ins = T.matmul(TB[32 * q:32 * q + 32, 1024:1024 + P], BD[:, g], Q[:, g, 0:P],
                                                   start=g % 2 == 0, stop=g % 2 == 1)
                                ins.then_inc(e["k_mm"], 1)
                            if s == 7:
                                pe.wait_ge(e["g_ready"], j + 1)
                                pe.wait_ge(e["z_act"], j)
                                pe.wait_ge(e["fin_ev"], j)
                                for i in range(8):
                                    ins = T.transpose(TB[:, i * P:(i + 1) * P], GR[:, i // 4, i % 4].rearrange("p r c -> p (r c)"),
                                                      ident[:])
                                ins.then_inc(e["ls_mm"], 1)
                            if s == 8:
                                pe.wait_ge(e["ls_act"], j + 1)
                                pe.wait_ge(e["ls_dve"], j + 1)
                                pe.wait_ge(e["ga"], 4 * j + 2)
                                pe.wait_ge(e["gd"], j + 1)
                                for r in range(L):
                                    i = L - 1 - r
                                    T.transpose(TB[:, 3 * 512 + r * P:3 * 512 + (r + 1) * P], UZ[:, i:SEQ:L], ident[:])
                                    ins = T.transpose(TB[0:NBS, r * P:(r + 1) * P], UZ[:, SEQ + i:TOK:L], ident[:])
                                ins.then_inc(e["st1_mm"], 1)
                            if s == 9:
                                pe.wait_ge(e["st1_act"], j + 1)
                                pe.wait_ge(e["st1_dve"], j + 1)
                                pe.wait_ge(e["ks_ready"], j + 1)
                                for g in range(8):
                                    T.transpose(TB[:, 1024 + g * P:1024 + (g + 1) * P], UC[:, g * P:(g + 1) * P], ident[:])
                                    ins = T.transpose(TB[:, 4 * 512 + g * NBS:4 * 512 + (g + 1) * NBS],
                                                      UCS[0:NBS, g * P:(g + 1) * P], ident[0:NBS, 0:NBS])
                                ins.then_inc(e["st2_mm"], 1)
                            if s == 10:
                                pe.wait_ge(e["st2_act"], j + 1)
                                pe.wait_ge(e["st2_dve"], j + 1)
                                for i in range(8):
                                    for g in range(2):
                                        c = 512 * (i // 3) + (i % 3) * SC
                                        ins = T.matmul(TB[g * NP:(g + 1) * NP, c:c + SC], LS[:, i, g * NP:(g + 1) * NP],
                                                       Ug[:, 2 * (i % 4) + g], start=True, stop=True)
                                ins.then_inc(e["s_mm"], 1)
                            if s == 13:
                                pe.wait_ge(e["h_dve"], j + 1)
                                pe.wait_ge(e["h_pool"], j + 1)
                                pe.wait_ge(e["mt_in"], P * (j + 1))
                                for g in range(8):
                                    c = 512 * (3, 4, 0)[g // 3] + (g % 3) * SC
                                    T.matmul(TB[:, c:c + SC], MT[:, g], Ug[:, g], start=True, stop=False)
                                    ins = T.matmul(TB[:, c:c + SC], Q[:, g, GC:], H[:, g, 0:SC], start=False, stop=True)
                                ins.then_inc(e["y_mm"], 1)
                            if s == 14:
                                pe.wait_ge(e["y_act"], j + 1)
                                pe.wait_ge(e["y_dve"], j + 1)
                                for g in range(8):
                                    T.transpose(TB[:, 512 + g * P:512 + (g + 1) * P], Y[:, g, 0:NB], ident[:])
                                    ins = T.transpose(TB[0:NBS, 3 * 512 + g * P:3 * 512 + (g + 1) * P], Y[:, g, NB + 1:SC], ident[:])
                                ins.then_inc(e["yt_mm"], 1)
                            if s == 15:
                                pe.wait_ge(e["yt_act"], j + 1)
                                pe.wait_ge(e["yt_dve"], j + 1)
                                for t in range(L):
                                    T.transpose(TB[:, 512 + t * P:512 + (t + 1) * P], UC[:, t * P:(t + 1) * P], ident[:])
                                    ins = T.transpose(TB[:, t * NBS:(t + 1) * NBS], UCS[0:NBS, t * P:(t + 1) * P],
                                                      ident[0:NBS, 0:NBS])
                                ins.then_inc(e["z_mm"], 1)
                                pe.wait_ge(e["fb_ready"], j + 1)
                                T.transpose(TB[0:16, 4 * 512:4 * 512 + P], FB[:], ident[:]).then_inc(e["fin_mm"], 1)

        free_semaphores()

        CT = SEQ + PAST + DEC
        with ExitStack() as st:
            sbp = pool_of(st)
            wf = sbp("wf", [P, KT, NH])
            WF = sbp("WF", [P, KT, P], r32)
            fx = sbp("fx", [NH, TOK])
            fl = sbp("fl", [NH, TOK])
            fe = sbp("fe", [NH, TOK])
            one8 = sbp("one8", [NH, SEQ])
            lfs = sbp("lfs", [NH, PAST + DEC])
            cum = sbp("cum", [NH, CT])
            ncum = sbp("ncum", [NH, CT])
            bf = sbp("bf", [NH, 1])
            cl = sbp("cl", [P, NH])
            lt = sbp("lt", [P, TT, NH])
            names = ("in", "zero", "hi", "lo", "mm", "fn", "ex", "e1", "ln", "lf", "t_mm", "t_ev", "cum", "out", "fl", "x", "neg")
            e = {n: sem("gate_" + n) for n in names}
            with nc.Block() as block:
                @block.sync
                def _(sp):
                    sp.dma_start(wf[:], w_in_v[:, :, D_PROJ - NH:D_PROJ]).then_inc(e["in"], 16)
                    sp.dma_start(bf[:], b_f.rearrange("o h -> h o")).then_inc(e["in"], 16)
                    sp.dma_start(cl[:], cache_logf[0, 0]).then_inc(e["in"], 16)
                    sp.wait_ge(e["t_ev"], 2)
                    sp.dma_start(logf_prompt[0, 0].rearrange("(m p) h -> p m h", p=P), lt[:, 0:TT - 1]).then_inc(e["out"], 16)
                    sp.dma_start(logf_sample[0, 0], lt[0:DEC, TT - 1]).then_inc(e["out"], 16)
                    sp.wait_ge(e["neg"], 1)
                    sp.dma_start(nc_s, ncum[:]).then_inc(e["out"], 16)
                    sp.wait_ge(e["out"], 48)

                @block.scalar
                def _(act):
                    act.wait_ge(e["zero"], 1)
                    act.wait_ge(e["in"], 48)
                    S.copy(WF[:, :, 0:NH], wf[:]).then_inc(e["hi"], 1)
                    act.wait_ge(e["fn"], 1)
                    S.activation(fe[:], fl[:], ACT.Exp).then_inc(e["ex"], 1)
                    act.wait_ge(e["e1"], 1)
                    S.activation(fe[:], fe[:], ACT.Ln).then_inc(e["ln"], 1)

                @block.vector
                def _(dve):
                    V.memset(WF[:].rearrange("p a b -> p (a b)").bitcast(f32), 0.0).then_inc(e["zero"], 1)
                    V.memset(one8[:], 1.0)
                    dve.wait_ge(e["hi"], 1)
                    V.tensor_tensor(WF[:, :, 32:32 + NH], wf[:], WF[:, :, 0:NH].bitcast(f32), ALU.subtract).then_inc(e["lo"], 1)
                    dve.wait_ge(e["mm"], 1)
                    for src, dst in halves(GB, fl, slice(32, 32 + NH)):
                        ins = V.tensor_copy(dst, src)
                    ins.then_inc(e["fl"], 1)
                    dve.wait_ge(e["fl"], 1)
                    for (src, dst), (_, low) in zip(halves(GB, fx, slice(0, NH)), halves(GB, fl)):
                        ins = V.scalar_tensor_tensor(dst, src, bf[:], low, ALU.add, ALU.add)
                    ins.then_inc(e["x"], 1)
                    dve.wait_ge(e["x"], 1)
                    V.scalar_tensor_tensor(fl[:], fx[:], -1.0, fx[:], ALU.mult, ALU.min).then_inc(e["fn"], 1)
                    dve.wait_ge(e["ex"], 1)
                    V.tensor_scalar(fe[:], fe[:], 1.0, None, ALU.add).then_inc(e["e1"], 1)
                    dve.wait_ge(e["ln"], 1)
                    V.scalar_tensor_tensor(fx[:], fx[:], 0.0, fe[:], ALU.min, ALU.subtract).then_inc(e["lf"], 1)
                    dve.wait_ge(e["t_mm"], 1)
                    V.tensor_copy(lt[:, 0:TT - 1], TB[:, 0:64].rearrange("p (m h) -> p m h", h=NH)).then_inc(e["t_ev"], 1)
                    V.tensor_copy(lt[0:DEC, TT - 1], TB[0:DEC, 64:72]).then_inc(e["t_ev"], 1)
                    V.tensor_copy(lfs[:, 0:PAST], TB[0:NH, 512:512 + PAST]).then_inc(e["cum"], 1)
                    V.tensor_copy(lfs[:, PAST:], fx[:, SEQ:TOK]).then_inc(e["cum"], 1)
                    V.tensor_tensor_scan(cum[:, 0:SEQ], one8[:], fx[:, 0:SEQ], 0.0, ALU.mult, ALU.add).then_inc(e["cum"], 1)
                    dve.wait_ge(e["cum"], 3)
                    V.tensor_tensor_scan(cum[:, SEQ:], one8[:, 0:PAST + DEC], lfs[:], 0.0, ALU.mult, ALU.add).then_inc(e["cum"], 1)
                    dve.wait_ge(e["cum"], 4)
                    V.tensor_scalar(ncum[:], cum[:], -1.0, None, ALU.mult).then_inc(e["neg"], 1)

                @block.tensor
                def _(pe):
                    pe.wait_ge(e["lo"], 1)
                    for k in range(KT):
                        for x in (XH, XL):
                            for b, (c, n) in enumerate(COLS):
                                ins = T.matmul(group(GB, b), WF[:, k], x[:, k, c:c + n],
                                               start=k == 0 and x is XH, stop=k == KT - 1 and x is XL)
                    ins.then_inc(e["mm"], 1)
                    pe.wait_ge(e["in"], 48)
                    T.transpose(TB[0:NH, 512:512 + PAST], cl[:], ident[:])
                    pe.wait_ge(e["lf"], 1)
                    for m in range(TT):
                        n = min(P, TOK - m * P)
                        ins = T.transpose(TB[0:n, m * NH:(m + 1) * NH], fx[:, m * P:m * P + n], ident[0:NH, 0:NH])
                    ins.then_inc(e["t_mm"], 1)

        with ExitStack() as st:
            sbp = pool_of(st)
            QR, KR, VR, ZR = (sbp(n, [P, TOK]) for n in ("QR", "KR", "VR", "ZR"))
            QN, KN = sbp("QN", [P, TOK]), sbp("KN", [P, TOK])
            VT = sbp("VT", [P, TT, P])
            KO = sbp("KO", [P, TT, P])
            SQ = sbp("SQ", [P, TOK])
            NCB = sbp("NCB", [P, CT])
            PR = sbp("PR", [P, SEQ])
            PT = sbp("PT", [P, SEQ])
            CK, CV, KPT = sbp("CK", [PAST, P]), sbp("CV", [PAST, P]), sbp("KPT", [P, PAST])
            SQA = sbp("SQA", [P, TOK])
            qg, tabs = sbp("qg", [P, 1]), sbp("tabs", [P, 1])
            mx, nmx, rsum, rrec = (sbp(n, [P, 1]) for n in ("mx", "nmx", "rsum", "rrec"))
            W = Weights("att", w_in_v, XH, XL)
            NPC = 4 * KT // PIECE
            NR = 9
            names = ("ga", "gd", "sq", "ss_mm", "rt", "qn_r", "qn", "kn", "kpt_mm", "kpt", "s_mm", "nmx", "exp", "pn",
                     "pt_mm", "pt_act", "pt_dve", "o_mm", "y", "v_mm", "v_act", "v_dve", "k_mm", "k_act", "k_dve",
                     "in", "k_out", "v_out", "y_out", "ysq", "sqa", "init", "qg", "sqa_out", "rr")
            e = {n: sem("att_" + n) for n in names}
            ROWS = (0, 1, 2, 8, 3, 4, 5, 6, 7)
            S_AT = (0, 3, 5, 7, 10, 13, 16, 21, 24)
            T_AT = (2, 4, 6, 8, 12, 15, 18, 23, 26)
            O_AT = (3, 5, 7, 9, 13, 16, 19, 24, 27)
            KPT_AT = 5
            SQ_AT = {8: (0, QR), 19: (1, KR)}
            SS_AT = {9: (0, 4), 20: (1, 7)}
            RT_AT = {9: 0, 20: 1}
            REC = 8
            REC_AT = ((11, 12, 13, 14, 15, 16, 17, 18), (22, 22, 23, 23, 25, 25, 26, 26))
            QN_AT, KN_AT, YSQ_AT, KT_AT, VT_AT = 18, 27, 29, 29, 31
            RW = TOK // REC

            def keys(i):
                return (P * (i + 1), P) if i < NR - 1 else (PAST + DEC, DEC)

            def row_at(s, at):
                return ROWS[at.index(s)], at.index(s)

            with nc.Block() as block:
                @block.sync
                def _(sp):
                    with sp.Fori(0, NH) as h:
                        for s in range(NPC):
                            col = h * P + 2 * D_SSM + D_ATT * (s // 8)
                            W.load(sp, h * NPC + s, s, col, PIECE * (s % 8))
                    for s in range(SPL):
                        W.load(sp, NH * NPC + s, s, 0, 0)

                @block.gpsimd
                def _(pool):
                    G.memset(SQA[:], 0.0).then_inc(e["init"], 1)
                    pool.wait_ge(e["init"], 1)

                    def part(h, gemm, att, ha):
                        if att:
                            pool.wait_ge(e["ysq"], ha + 1)
                            G.tensor_tensor(SQA[:], SQA[:], SQ[:], ALU.add).then_inc(e["sqa"], 1)
                            pool.wait_ge(e["sqa"], ha + 1)
                            pool.wait_ge(e["y"], NR * (ha + 1))
                            stand(pool, "pool")
                            pool.dma_start(ya_s[ds(ha * P, P), :], ZR[:]).then_inc(e["y_out"], 16)
                        if gemm:
                            pool.wait_ge(e["qn_r"], h + 1)
                            if att:
                                pool.wait_ge(e["s_mm"], NR * (ha + 1))
                            stand(pool, "pool")
                            G.tensor_copy(QN[:], QR[:]).then_inc(e["qn"], 1)
                            if att:
                                pool.wait_ge(e["o_mm"], NR * (ha + 1))
                                pool.wait_ge(e["nmx"], NR * (ha + 1))
                            stand(pool, "pool")
                            for dst, src in ((CK[:], cache_k[0, 0]), (CV[:], cache_v[0, 0])):
                                pool.dma_start(dst, src.rearrange("t h d -> t (h d)")[:, ds(h * P, P)]).then_inc(e["in"], 16)
                            pool.dma_start(NCB[:], nc_s[ds(h, 1), :].to_broadcast([P, CT])).then_inc(e["in"], 16)
                            for n, src, po, so in (("v", VT, v_prompt, v_sample), ("k", KO, k_prompt, k_sample)):
                                pool.wait_ge(e[n + "_act"], h + 1)
                                pool.wait_ge(e[n + "_dve"], h + 1)
                                stand(pool, "pool")
                                pool.dma_start(po[0, 0].rearrange("(m p) h d -> p m (h d)", p=P)[:, :, ds(h * P, P)],
                                               src[:, 0:TT - 1]).then_inc(e[n + "_out"], 16)
                                pool.dma_start(so[0, 0].rearrange("p h d -> p (h d)")[:, ds(h * P, P)],
                                               src[0:DEC, TT - 1]).then_inc(e[n + "_out"], 16)
                    part(0, True, False, None)
                    with pool.Fori(1, NH) as h:
                        part(h, True, True, h - 1)
                    part(None, False, True, NH - 1)
                    pool.dma_start(sqa_s, SQA[:]).then_inc(e["sqa_out"], 16)
                    pool.wait_ge(e["sqa_out"], 16)
                    pool.wait_ge(e["y_out"], 16 * NH)
                    pool.wait_ge(e["k_out"], 32 * NH)
                    pool.wait_ge(e["v_out"], 32 * NH)

                @block.scalar
                def _(act):
                    for s in range(SPL):
                        W.split_hi(s, s, 1)
                    o = Order(act, "act_tables")

                    def table(func):
                        o.then(S.activation(tabs[:], epsc[:], func))

                    def part(h, gemm, att, ha):
                        for s in range(NPC):
                            if gemm and s in (7, 15, 23):
                                act.wait_ge(W.mm, W.multiplied(h * NPC + s))
                                raw = {7: QR, 15: KR, 23: VR}[s]
                                if s == 7 and att:
                                    act.wait_ge(e["qn"], h)
                                S.copy(cols(raw, 0), group(GB, 0)).then_inc(e["ga"], 1)
                                S.copy(cols(raw, 2), group(GB, 2)).then_inc(e["ga"], 1)
                            if gemm and s == NPC - 1:
                                act.wait_ge(W.mm, W.multiplied(h * NPC + s))
                                if att:
                                    act.wait_ge(e["y_out"], 16 * h)
                                for src, dst in halves(GB, ZR):
                                    S.activation(dst, src, ACT.Silu).then_inc(e["ga"], 1)
                            if gemm:
                                m = s + SPL
                                W.split_hi(h * NPC + m, m, h * (NPC // RAW) + m // RAW + 1)
                            if gemm and s in RT_AT:
                                w = RT_AT[s]
                                table(ACT.Sqrt)
                                act.wait_ge(e["ss_mm"], 2 * h + w + 1)
                                S.activation(SQ[:, 0:SEQ], TB[:, 0:SEQ], ACT.Sqrt, bias=epsc[:], scale=1.0 / HD)
                                S.activation(SQ[:, SEQ:TOK], TB[:, 4 * 512 + P:4 * 512 + P + DEC], ACT.Sqrt, bias=epsc[:],
                                             scale=1.0 / HD).then_inc(e["rt"], 1)
                                table(ACT.Exp)
                            if att and s in S_AT:
                                i, p = row_at(s, S_AT)
                                w, n = keys(i)
                                act.wait_ge(e["nmx"], NR * ha + p + 1)
                                S.activation(PR[0:n, 0:w], PR[0:n, 0:w], ACT.Exp, bias=nmx[0:n],
                                             accum_out=rsum[0:n]).then_inc(e["exp"], 1)
                            if att and s == KPT_AT:
                                act.wait_ge(e["kpt_mm"], ha + 1)
                                S.copy(KPT[:], TB[:, 1024:1024 + PAST]).then_inc(e["kpt"], 1)
                            if att and s in T_AT:
                                i, p = row_at(s, T_AT)
                                act.wait_ge(e["pt_mm"], NR * ha + p + 1)
                                if i < NR - 1:
                                    b = min(i + 1, 4) * P
                                    S.copy(PT[:, 0:b], TB[:, 1024:1024 + b]).then_inc(e["pt_act"], 1)
                                else:
                                    S.copy(PT[:, 0:DEC], TB[:, 1024:1024 + DEC])
                                    S.copy(PT[0:DEC, P:P + DEC], TB[0:DEC, 1024 + P:1024 + P + DEC]).then_inc(e["pt_act"], 1)
                            if gemm and s in SQ_AT:
                                w, raw = SQ_AT[s]
                                act.wait_ge(e["ga"], 8 * h + 2 * w + 2)
                                act.wait_ge(e["gd"], 3 * h + w + 1)
                                if w:
                                    act.wait_ge(e["qn_r"], h + 1)
                                elif att:
                                    act.wait_ge(e["kn"], h)
                                    act.wait_ge(e["sqa"], ha)
                                S.activation(SQ[:], raw[:], ACT.Square).then_inc(e["sq"], 1)
                            if att and s == YSQ_AT:
                                act.wait_ge(e["y"], NR * (ha + 1))
                                if gemm:
                                    act.wait_ge(e["kn"], h + 1)
                                S.activation(SQ[:], ZR[:], ACT.Square).then_inc(e["ysq"], 1)
                            if gemm and s == KT_AT:
                                act.wait_ge(e["k_mm"], h + 1)
                                act.wait_ge(e["k_out"], 32 * h)
                                S.copy(KO[:, 0:4], TB[:, 0:512].rearrange("p (m d) -> p m d", m=4))
                                S.copy(KO[0:DEC, TT - 1], TB[0:DEC, 4 * 512:4 * 512 + P]).then_inc(e["k_act"], 1)
                            if gemm and s == NPC - 2:
                                table(ACT.Silu)
                            if gemm and s == VT_AT:
                                act.wait_ge(e["v_mm"], h + 1)
                                act.wait_ge(e["v_out"], 32 * h)
                                S.copy(VT[:, 0:4], TB[:, 1024:1536].rearrange("p (m d) -> p m d", m=4))
                                S.copy(VT[0:DEC, TT - 1], TB[0:DEC, 4 * 512:4 * 512 + P]).then_inc(e["v_act"], 1)
                                table(ACT.Exp)
                    part(0, True, False, None)
                    with act.Fori(1, NH) as h:
                        o.enter(h - 1, 6)
                        part(h, True, True, h - 1)
                    o.leave(NH - 1)
                    part(None, False, True, NH - 1)

                @block.vector
                def _(dve):
                    V.tensor_scalar(qg[:], vec[:, 32:33], HD ** -0.5, None, ALU.mult).then_inc(e["qg"], 1)
                    dve.sem_inc(W.lo, RAW)
                    dve.wait_ge(e["qg"], 1)
                    for s in range(SPL):
                        W.split_lo(s, s)
                    o = Order(dve, "dve_att")

                    def part(h, gemm, att, ha):
                        for s in range(NPC):
                            if gemm and s in (7, 15, 23):
                                dve.wait_ge(W.mm, W.multiplied(h * NPC + s))
                                raw = {7: QR, 15: KR, 23: VR}[s]
                                if s == 7 and att:
                                    dve.wait_ge(e["qn"], h)
                                V.tensor_copy(cols(raw, 1), group(GB, 1)).then_inc(e["gd"], 1)
                            if gemm:
                                m = s + SPL
                                W.split_lo(h * NPC + m, m)
                            if att and s in O_AT:
                                i, p = row_at(s, O_AT)
                                n = keys(i)[1]
                                dve.wait_ge(e["o_mm"], NR * ha + p + 1)
                                V.tensor_tensor(ZR[:, i * P:i * P + n], TB[:, 4 * 512:4 * 512 + n], ZR[:, i * P:i * P + n],
                                                ALU.mult).then_inc(e["y"], 1)
                            if att and s in S_AT:
                                i, p = row_at(s, S_AT)
                                w, n = keys(i)
                                c = 0 if i < NR - 1 else SEQ
                                if p == 0:
                                    dve.wait_ge(e["in"], 48 * (ha + 1))
                                dve.wait_ge(e["s_mm"], NR * ha + p + 1)
                                stand(dve, "dve")
                                o.then(V.tensor_tensor_reduce(out=PR[0:n, 0:w], in0=TB[0:n, 0:w], in1=NCB[0:n, c:c + w], scale=1.0,
                                                              scalar=-3e38, op0=ALU.add, op1=ALU.max, accum_out=mx[0:n]))
                                V.tensor_scalar(nmx[0:n], mx[0:n], -1.0, None, ALU.mult).then_inc(e["nmx"], 1)
                                dve.wait_ge(e["exp"], NR * ha + p + 1)
                                o.then(V.reciprocal(rrec[0:n], rsum[0:n]))
                                V.tensor_scalar(PR[0:n, 0:w], PR[0:n, 0:w], rrec[0:n], None, ALU.mult).then_inc(e["pn"], 1)
                            if att and s in T_AT and 4 <= row_at(s, T_AT)[0] < NR - 1:
                                i, p = row_at(s, T_AT)
                                dve.wait_ge(e["pt_mm"], NR * ha + p + 1)
                                V.tensor_copy(PT[:, 512:P * (i + 1)], TB[:, 1536:1024 + P * (i + 1)]).then_inc(e["pt_dve"], 1)
                            for w in range(2):
                                for x, at in enumerate(REC_AT[w]):
                                    if gemm and at == s:
                                        if x == 0:
                                            dve.wait_ge(e["rt"], 2 * h + w + 1)
                                        a = SQ[:, RW * x:RW * (x + 1)]
                                        o.then(V.reciprocal(a, a))
                            if gemm and s == QN_AT:
                                V.scalar_tensor_tensor(QR[:], QR[:], qg[:], SQ[:], ALU.mult, ALU.mult).then_inc(e["qn_r"], 1)
                            if gemm and s == KN_AT:
                                V.scalar_tensor_tensor(KN[:], KR[:], vec[:, 33:34], SQ[:], ALU.mult, ALU.mult).then_inc(e["kn"], 1)
                            if gemm and s == KT_AT:
                                dve.wait_ge(e["k_mm"], h + 1)
                                dve.wait_ge(e["k_out"], 32 * h)
                                V.tensor_copy(KO[:, 4:8], TB[:, 512:1024].rearrange("p (m d) -> p m d", m=4)).then_inc(e["k_dve"], 1)
                            if gemm and s == VT_AT:
                                dve.wait_ge(e["v_mm"], h + 1)
                                dve.wait_ge(e["v_out"], 32 * h)
                                V.tensor_copy(VT[:, 4:8], TB[:, 1536:2048].rearrange("p (m d) -> p m d", m=4)).then_inc(e["v_dve"], 1)
                    part(0, True, False, None)
                    with dve.Fori(1, NH) as h:
                        o.enter(h - 1, 2 * NR + 2 * REC)
                        part(h, True, True, h - 1)
                    o.leave(NH - 1)
                    part(None, False, True, NH - 1)

                @block.tensor
                def _(pe):
                    W.credit("pe")

                    def part(h, gemm, att, ha):
                        for s in range(NPC):
                            if gemm:
                                def free(b):
                                    if b == 1 and s:
                                        pe.wait_ge(e["gd"], 3 * h + s // 8)
                                    elif b == 2 or s:
                                        pe.wait_ge(e["ga"], 8 * h + s // 4 - (b == 0))
                                    elif b == 0:
                                        if att:
                                            pe.wait_ge(e["ga"], 8 * h - 1)
                                k = PIECE * (s % 8)
                                W.multiply(h * NPC + s, s, k, k == 0, k == KT - PIECE, free=free if k == 0 else None)
                            if gemm and s - 1 in RT_AT:
                                pe.wait_ge(e["rt"], 2 * h + RT_AT[s - 1] + 1)
                            if att and s in O_AT:
                                i, p = row_at(s, O_AT)
                                w, n = keys(i)
                                pe.wait_ge(e["pt_act"], NR * ha + p + 1)
                                if 4 <= i < NR - 1:
                                    pe.wait_ge(e["pt_dve"], 4 * ha + i - 3)
                                if p:
                                    pe.wait_ge(e["y"], NR * ha + p)
                                O = TB[:, 4 * 512:4 * 512 + n]
                                if i < NR - 1:
                                    for b in range(i + 1):
                                        ins = T.matmul(O, VT[:, b], PT[:, b * P:(b + 1) * P], start=b == 0, stop=b == i)
                                else:
                                    T.matmul(O, CV[:], PT[:, 0:DEC], start=True, stop=False)
                                    ins = T.matmul(O, VT[0:DEC, TT - 1], PT[0:DEC, P:P + DEC], start=False, stop=True)
                                ins.then_inc(e["o_mm"], 1)
                            if att and s in S_AT:
                                i, p = row_at(s, S_AT)
                                w, n = keys(i)
                                if p == 0:
                                    pe.wait_ge(e["qn"], ha + 1)
                                    pe.wait_ge(e["kn"], ha + 1)
                                    pe.wait_ge(e["k_act"], ha + 1)
                                    pe.wait_ge(e["k_dve"], ha + 1)
                                    pe.wait_ge(e["v_act"], ha + 1)
                                    pe.wait_ge(e["v_dve"], ha + 1)
                                else:
                                    pe.wait_ge(e["nmx"], NR * ha + p)
                                if i < NR - 1:
                                    q = QN[:, i * P:(i + 1) * P]
                                    for c in range(0, w, 512):
                                        cw = min(512, w - c)
                                        T.matmul(TB[:, c:c + cw], q, KN[:, c:c + cw], start=True, stop=c + cw < w)
                                    ins = T.matmul(TB[:, w - P:w], identb[:], maskb[:], start=False, stop=True)
                                else:
                                    pe.wait_ge(e["kpt"], ha + 1)
                                    q = QN[:, SEQ:TOK]
                                    T.matmul(TB[0:DEC, 0:PAST], q, KPT[:], start=True, stop=True)
                                    T.matmul(TB[0:DEC, PAST:w], q, KN[:, SEQ:TOK], start=True, stop=False)
                                    ins = T.matmul(TB[0:DEC, PAST:w], identb[0:DEC, 0:DEC], maskb[0:DEC, 0:DEC],
                                                   start=False, stop=True)
                                ins.then_inc(e["s_mm"], 1)
                            if att and s == KPT_AT:
                                pe.wait_ge(e["in"], 48 * (ha + 1))
                                pe.wait_ge(e["pt_act"], NR * ha + sum(t < s for t in T_AT))
                                T.transpose(TB[:, 1024:1024 + PAST], CK[:], ident[:]).then_inc(e["kpt_mm"], 1)
                            if att and s in T_AT:
                                i, p = row_at(s, T_AT)
                                w, n = keys(i)
                                pe.wait_ge(e["pn"], NR * ha + p + 1)
                                if s > KPT_AT:
                                    pe.wait_ge(e["kpt"], ha + 1)
                                if p:
                                    pe.wait_ge(e["pt_act"], NR * ha + p)
                                if i < NR - 1:
                                    for b in range(i + 1):
                                        ins = T.transpose(TB[:, 1024 + b * P:1024 + (b + 1) * P], PR[:, b * P:(b + 1) * P], ident[:])
                                else:
                                    stand(pe, "pe")
                                    T.transpose(TB[:, 1024:1024 + DEC], PR[0:DEC, 0:PAST], ident[0:DEC, 0:DEC])
                                    ins = T.transpose(TB[0:DEC, 1024 + P:1024 + P + DEC], PR[0:DEC, PAST:w], ident[0:DEC, 0:DEC])
                                ins.then_inc(e["pt_mm"], 1)
                            if gemm and s in SS_AT:
                                w, p = SS_AT[s]
                                pe.wait_ge(e["sq"], 2 * h + w + 1)
                                if att:
                                    pe.wait_ge(e["nmx"], NR * ha + p)
                                    pe.wait_ge(e["y"], NR * ha + p)
                                for c, d, n in ((0, 0, 512), (512, 512, 512), (SEQ, 4 * 512 + P, DEC)):
                                    ins = T.matmul(TB[:, d:d + n], ones[:], SQ[:, c:c + n], start=True, stop=True)
                                ins.then_inc(e["ss_mm"], 1)
                            if gemm and s in (KT_AT, VT_AT):
                                src, base, name = (KN, 0, "k") if s == KT_AT else (VR, 1024, "v")
                                if s == KT_AT:
                                    pe.wait_ge(e["kn"], h + 1)
                                    if att:
                                        pe.wait_ge(e["y"], NR * (ha + 1))
                                else:
                                    pe.wait_ge(e["ga"], 8 * h + 6)
                                    pe.wait_ge(e["gd"], 3 * h + 3)
                                    pe.wait_ge(e["k_act"], h + 1)
                                for m in range(TT):
                                    n = min(P, TOK - m * P)
                                    d = base + m * P if m < TT - 1 else 4 * 512
                                    ins = T.transpose(TB[0:n, d:d + P], src[:, m * P:m * P + n], ident[:])
                                ins.then_inc(e[name + "_mm"], 1)
                    part(0, True, False, None)
                    with pe.Fori(1, NH) as h:
                        part(h, True, True, h - 1)
                    part(None, False, True, NH - 1)
        xs_stack.close()
        free_semaphores()

        KG = D_SSM // P
        with ExitStack() as st:
            sbp = pool_of(st)
            ZH, ZL = sbp("ZH", [P, KG, TOK], r32), sbp("ZL", [P, KG, TOK], r32)
            zf = sbp("zf", [P, KG, TOK])
            zsc = sbp("zsc", [P, 2, TOK])
            yc = sbp("yc", [P, 2, TOK])
            sqc = sbp("sqc", [P, TOK])
            SQS = sbp("SQS", [P, TOK])
            W = Weights("glu", w_glu_v, ZH, ZL)
            NPC = KG // PIECE
            names = ("zf", "zhi", "zlo", "zs0", "zs1", "sig", "y1", "y", "sq", "sqs", "y_out0", "y_out1", "sqs_out", "init")
            e = {n: sem("glu_" + n) for n in names}
            with nc.Block() as block:
                @block.sync
                def _(sp):
                    zin = [sem(f"glu_zin{k}") for k in range(KG)]
                    for k in range(KG):
                        sp.dma_start(zf[:, k], zg_s[k * P:(k + 1) * P, :]).then_inc(zin[k], 16)
                    for n in range(KG):
                        for s in range(NPC):
                            W.load(sp, n * NPC + s, n * NPC + s, n * P, PIECE * s)

                def finish_glu(pool, n):
                    pool.wait_ge(e["y"], n + 1)
                    pool.dma_start(ys_s[n * P:(n + 1) * P, :], yc[:, n % 2]).then_inc(e[f"y_out{n % 2}"], 16)
                    pool.wait_ge(e["sq"], n + 1)
                    G.tensor_tensor(SQS[:], SQS[:], sqc[:], ALU.add).then_inc(e["sqs"], 1)
                    pool.wait_ge(e["sqs"], n + 1)

                @block.gpsimd
                def _(pool):
                    G.memset(SQS[:], 0.0).then_inc(e["init"], 1)
                    pool.wait_ge(e["init"], 1)
                    for n in range(KG):
                        if n >= 2:
                            pool.wait_ge(e["y"], n - 1)
                        pool.dma_start(zsc[:, n % 2], zs_s[n * P:(n + 1) * P, :]).then_inc(e[f"zs{n % 2}"], 16)
                        if n:
                            finish_glu(pool, n - 1)
                    finish_glu(pool, KG - 1)
                    pool.dma_start(sqs_s, SQS[:]).then_inc(e["sqs_out"], 16)
                    pool.wait_ge(e["sqs_out"], 16)
                    pool.wait_ge(e["y_out0"], 16 * (KG // 2))
                    pool.wait_ge(e["y_out1"], 16 * (KG // 2))

                @block.scalar
                def _(act):
                    zin = [sem(f"glu_zin{k}") for k in range(KG)]
                    for s in range(SPL):
                        W.split_hi(s, s, 1)
                    for k in range(KG):
                        act.wait_ge(zin[k], 16)
                        S.copy(ZH[:, k], zf[:, k]).then_inc(e["zhi"], 1)
                    for n in range(KG):
                        for s in range(NPC):
                            m = n * NPC + s + SPL
                            if m < KG * NPC:
                                W.split_hi(m, m, m // RAW + 1)
                        act.wait_ge(W.mm, W.multiplied(n * NPC + NPC - 1))
                        if n >= 2:
                            act.wait_ge(e[f"y_out{n % 2}"], 16 * (n // 2))
                        for src, dst in halves((GB, TB)[n % 2], yc[:, n % 2]):
                            ins = S.activation(dst, src, ACT.Sigmoid, bias=vec[:, 8 + n:9 + n])
                        ins.then_inc(e["sig"], 1)
                        act.wait_ge(e["y"], n + 1)
                        if n:
                            act.wait_ge(e["sqs"], n)
                        S.activation(sqc[:], yc[:, n % 2], ACT.Square).then_inc(e["sq"], 1)

                @block.vector
                def _(dve):
                    dve.sem_inc(W.lo, RAW)
                    for s in range(SPL):
                        W.split_lo(s, s)
                    for k in range(KG):
                        dve.wait_ge(e["zhi"], k + 1)
                        V.tensor_tensor(ZL[:, k], zf[:, k], ZH[:, k].bitcast(f32), ALU.subtract).then_inc(e["zlo"], 1)
                    for n in range(KG):
                        for s in range(NPC):
                            m = n * NPC + s + SPL
                            if m < KG * NPC:
                                W.split_lo(m, m)
                        dve.wait_ge(e["sig"], n + 1)
                        V.tensor_tensor(yc[:, n % 2], yc[:, n % 2], zf[:, n], ALU.mult).then_inc(e["y1"], 1)
                        dve.wait_ge(e["y1"], n + 1)
                        dve.wait_ge(e[f"zs{n % 2}"], 16 * (n // 2 + 1))
                        V.tensor_tensor(yc[:, n % 2], yc[:, n % 2], zsc[:, n % 2], ALU.mult).then_inc(e["y"], 1)

                @block.tensor
                def _(pe):
                    W.credit("pe")
                    for n in range(KG):
                        if n >= 2:
                            pe.wait_ge(e["sig"], n - 1)
                        for s in range(NPC):
                            if n == 0:
                                pe.wait_ge(e["zlo"], PIECE * (s + 1))
                            W.multiply(n * NPC + s, n * NPC + s, PIECE * s, s == 0, s == NPC - 1, (GB, TB)[n % 2])

        with ExitStack() as st:
            sbp = pool_of(st)
            YH, YL = sbp("YH", [P, KT, TOK], r32), sbp("YL", [P, KT, TOK], r32)
            sqb = sbp("sqb", [P, 2, TOK])
            yf = sbp("yf", [P, 3, TOK])
            OT = sbp("OT", [P, 2, TOK])
            XO = sbp("XO", [P, 2, TT, P])
            W = Weights("out", w_out_v, YH, YL)
            NPC = KT // PIECE
            NCH = D_MODEL // P
            names = ("sq_in", "ss", "rt", "rr", "sc", "yhi", "ylo", "ga", "gd", "t_mm", "add", "x_in0", "x_in1", "o_out0", "o_out1")
            e = {n: sem("out_" + n) for n in names}
            with nc.Block() as block:
                @block.sync
                def _(sp):
                    yin = [sem(f"out_yin{k}") for k in range(3)]
                    sp.dma_start(sqb[:, 0], sqs_s).then_inc(e["sq_in"], 16)
                    sp.dma_start(sqb[:, 1], sqa_s).then_inc(e["sq_in"], 16)
                    for m in range(RAW):
                        W.load(sp, m, m, 0, PIECE * m)
                    for k in range(KT):
                        if k >= 3:
                            sp.wait_ge(e["ylo"], k - 2)
                        src = (ys_s if k < KG else ya_s)[(k % KG) * P:(k % KG + 1) * P, :]
                        sp.dma_start(yf[:, k % 3], src).then_inc(yin[k % 3], 16)
                    for m in range(RAW, NPC):
                        W.load(sp, m, m, 0, PIECE * m)
                    with sp.Fori(1, D_MODEL // P) as n:
                        for s in range(NPC):
                            W.load(sp, n * NPC + s, s, n * P, PIECE * s)
                    for s in range(SPL):
                        W.load(sp, (D_MODEL // P) * NPC + s, s, 0, 0)

                @block.gpsimd
                def _(pool):
                    def residual(n, b, first, turn):
                        if not first:
                            pool.wait_ge(e[f"o_out{b}"], 32 * turn)
                            stand(pool, "pool")
                        pool.dma_start(XO[:, b, 0:TT - 1], x_prompt[0].rearrange("(m p) n -> p m n", p=P)[:, :, ds(n * P, P)]
                                       ).then_inc(e[f"x_in{b}"], 16)
                        pool.dma_start(XO[0:DEC, b, TT - 1], x_sample[0][:, ds(n * P, P)]).then_inc(e[f"x_in{b}"], 16)

                    def store(n, b):
                        pool.wait_ge(e["add"], 2 * n + 2)
                        stand(pool, "pool")
                        pool.dma_start(y_prompt[0].rearrange("(m p) n -> p m n", p=P)[:, :, ds(n * P, P)], XO[:, b, 0:TT - 1]
                                       ).then_inc(e[f"o_out{b}"], 16)
                        pool.dma_start(y_sample[0][:, ds(n * P, P)], XO[0:DEC, b, TT - 1]).then_inc(e[f"o_out{b}"], 16)
                    residual(0, 0, True, 0)
                    residual(1, 1, True, 0)
                    with pool.Fori(0, NCH // 2 - 1) as i:
                        for b in range(2):
                            store(2 * i + b, b)
                            residual(2 * i + b + 2, b, False, i + 1)
                    for b in range(2):
                        store(NCH - 2 + b, b)
                    for b in range(2):
                        pool.wait_ge(e[f"o_out{b}"], 32 * (NCH // 2))

                @block.scalar
                def _(act):
                    yin = [sem(f"out_yin{k}") for k in range(3)]
                    for w in range(2):
                        act.wait_ge(e["ss"], w + 1)
                        for src, dst in halves((GB, TB)[w], sqb[:, w]):
                            ins = S.activation(dst, src, ACT.Sqrt, bias=epsc[:], scale=1.0 / D_SSM)
                        ins.then_inc(e["rt"], 1)
                    for s in range(SPL):
                        W.split_hi(s, s, 1)
                    for k in range(KT):
                        act.wait_ge(e["sc"], k + 1)
                        S.copy(YH[:, k], yf[:, k % 3]).then_inc(e["yhi"], 1)

                    def chunk(n, b):
                        for s in range(NPC):
                            if s == NPC - 1:
                                act.wait_ge(W.mm, W.multiplied(n * NPC + s))
                                if not isinstance(n, int):
                                    act.wait_ge(e["t_mm"], n - 1)
                                S.copy(cols(OT[:, b], 0), group(GB, 0)).then_inc(e["ga"], 1)
                                S.copy(cols(OT[:, b], 2), group(GB, 2)).then_inc(e["ga"], 1)
                            m = s + SPL
                            W.split_hi(n * NPC + m, m, n * (NPC // RAW) + m // RAW + 1)
                    chunk(0, 0)
                    chunk(1, 1)
                    with act.Fori(1, NCH // 2) as i:
                        chunk(2 * i, 0)
                        chunk(2 * i + 1, 1)

                @block.vector
                def _(dve):
                    dve.sem_inc(W.lo, RAW)
                    for w in range(2):
                        dve.wait_ge(e["rt"], w + 1)
                        V.reciprocal(sqb[:, w], sqb[:, w]).then_inc(e["rr"], 1)
                    for s in range(SPL):
                        W.split_lo(s, s)
                    dve.wait_ge(e["rr"], 2)
                    yin = [sem(f"out_yin{k}") for k in range(3)]

                    def scale(k):
                        dve.wait_ge(yin[k % 3], 16 * (k // 3 + 1))
                        V.scalar_tensor_tensor(yf[:, k % 3], yf[:, k % 3], vec[:, 16 + k:17 + k], sqb[:, k // KG],
                                               ALU.mult, ALU.mult).then_inc(e["sc"], 1)
                    scale(0)
                    for k in range(KT):
                        if k + 1 < KT:
                            scale(k + 1)
                        dve.wait_ge(e["yhi"], k + 1)
                        V.tensor_tensor(YL[:, k], yf[:, k % 3], YH[:, k].bitcast(f32), ALU.subtract).then_inc(e["ylo"], 1)

                    def part(n, gemm, tr, b, turn):
                        for s in range(NPC):
                            if gemm and s == NPC - 1:
                                dve.wait_ge(W.mm, W.multiplied(n * NPC + s))
                                if not isinstance(n, int):
                                    dve.wait_ge(e["t_mm"], n - 1)
                                V.tensor_copy(cols(OT[:, 1 - b], 1), group(GB, 1)).then_inc(e["gd"], 1)
                            if gemm:
                                m = s + SPL
                                W.split_lo(n * NPC + m, m)
                            if tr and s == NPC - 1:
                                dve.wait_ge(e["t_mm"], n)
                                dve.wait_ge(e[f"x_in{b}"], 32 * turn)
                                V.tensor_tensor(XO[:, b, 0:TT - 1], XO[:, b, 0:TT - 1],
                                                TB[:, 0:SEQ].rearrange("p (m n) -> p m n", n=P), ALU.add).then_inc(e["add"], 1)
                                V.tensor_tensor(XO[0:DEC, b, TT - 1], XO[0:DEC, b, TT - 1], TB[0:DEC, SEQ:SEQ + P],
                                                ALU.add).then_inc(e["add"], 1)
                    part(0, True, False, 1, 0)
                    part(1, True, True, 0, 1)
                    with dve.Fori(0, NCH // 2 - 1) as i:
                        part(2 * i + 2, True, True, 1, i + 1)
                        part(2 * i + 3, True, True, 0, i + 2)
                    part(NCH, False, True, 1, NCH // 2)

                @block.tensor
                def _(pe):
                    W.credit("pe")
                    pe.wait_ge(e["sq_in"], 32)
                    for w, bank in ((0, GB), (1, TB)):
                        for b, (c, n) in enumerate(COLS):
                            ins = T.matmul(group(bank, b), ones[:], sqb[:, w, c:c + n], start=True, stop=True)
                        ins.then_inc(e["ss"], 1)

                    def chunk(n, first):
                        for s in range(NPC):
                            def free(b):
                                if first:
                                    if b == 0:
                                        pe.wait_ge(e["rt"], 2)
                                elif b == 1:
                                    pe.wait_ge(e["gd"], n)
                                else:
                                    pe.wait_ge(e["ga"], 2 * n - (b == 0))
                            if first:
                                pe.wait_ge(e["ylo"], PIECE * (s + 1))
                            W.multiply(n * NPC + s, s, PIECE * s, s == 0, s == NPC - 1, free=free if s == 0 else None)

                    def transposes(n, b):
                        pe.wait_ge(e["ga"], 2 * n + 2)
                        pe.wait_ge(e["gd"], n + 1)
                        if not isinstance(n, int) or n:
                            pe.wait_ge(e["add"], 2 * n)
                        for m in range(TT):
                            w = min(P, TOK - m * P)
                            ins = T.transpose(TB[0:w, m * P:(m + 1) * P], OT[:, b, m * P:m * P + w], ident[:])
                        ins.then_inc(e["t_mm"], 1)
                    chunk(0, True)
                    with pe.Fori(0, NCH // 2 - 1) as i:
                        chunk(2 * i + 1, False)
                        transposes(2 * i, 0)
                        chunk(2 * i + 2, False)
                        transposes(2 * i + 1, 1)
                    chunk(NCH - 1, False)
                    transposes(NCH - 2, 0)
                    transposes(NCH - 1, 1)


_INS = ["x_prompt", "x_sample", "cache_k", "cache_v", "cache_logf", "state_ssm_re", "state_ssm_im",
        "norm_gain", "w_in", "b_f", "q_norm_gain", "k_norm_gain", "ssm_log_dt", "ssm_a_re", "ssm_a_im",
        "ssm_b_re", "ssm_b_im", "ssm_c_re", "ssm_c_im", "ssm_d", "w_glu", "b_glu",
        "ssm_out_norm", "att_out_norm", "w_out"]
_OUTS = [("y_prompt", (1, SEQ, D_MODEL)), ("y_sample", (1, DEC, D_MODEL)),
         ("k_prompt", (1, 1, SEQ, NH, HD)), ("v_prompt", (1, 1, SEQ, NH, HD)), ("logf_prompt", (1, 1, SEQ, NH)),
         ("hre_prompt", (1, 1, NG, NP)), ("him_prompt", (1, 1, NG, NP)),
         ("k_sample", (1, 1, DEC, NH, HD)), ("v_sample", (1, 1, DEC, NH, HD)), ("logf_sample", (1, 1, DEC, NH)),
         ("hre_sample", (1, 1, NG, NP)), ("him_sample", (1, 1, NG, NP))]


def kernel(**inputs):
    import numpy as _np
    import concourse.bacc as _bacc
    from concourse import mybir as _mybir
    from concourse.bass_utils import run_bass_kernel_spmd as _run

    nc = _bacc.Bacc("TRN2", target_bir_lowering=False, num_devices=1)
    arrays, args = {}, []
    for name in _INS:
        a = _np.ascontiguousarray(inputs[name])
        arrays[f"in_{name}"] = a
        args.append(nc.dram_tensor(f"in_{name}", a.shape, _mybir.dt.from_np(a.dtype), kind="ExternalInput").ap())
    for name, shape in _OUTS:
        args.append(nc.dram_tensor(f"out_{name}", shape, _mybir.dt.float32, kind="ExternalOutput").ap())
    build_kernel(nc, *args)
    r = _run(nc, [arrays], core_ids=[0])
    return tuple(r.results[0][f"out_{name}"] for name, _ in _OUTS)
```

```python
import math
from contextlib import ExitStack

import concourse.bass as bass
import concourse.mybir as mybir

D_MODEL, SEQ, DEC, PAST = 2048, 1024, 64, 128
D_SSM = D_ATT = 1024
NH, HD = 8, 128
NG, GC, NP = 64, 16, 64
D_PROJ = 2 * D_SSM + 4 * D_ATT + NH
EPS = 1e-6
P = 128
TOK = SEQ + DEC
KT = D_MODEL // P
TT = SEQ // P + 1
L = 8
NB = SEQ // L
NBS = DEC // L
SC = NB + 1 + NBS
HC = SC + 1
RAW, SPL = 4, 4
PIECE = 2
NLV = 7
AR, AI, WR, WI, MG, H0 = 0, 9, 18, 25, 32, 33
NPR = 35
CT = SEQ + PAST + DEC
PKW = NPR * 4 + 4 * 4 * GC + 1
CW = 384
COLS = ((0, CW), (CW, CW), (2 * CW, TOK - 2 * CW))
YB = 6
MAGIC = 12582912.0
NEG = -1e30


def build_kernel(nc, x_prompt, x_sample, cache_k, cache_v, cache_logf, state_ssm_re, state_ssm_im,
                 norm_gain, w_in, b_f, q_norm_gain, k_norm_gain, ssm_log_dt, ssm_a_re, ssm_a_im,
                 ssm_b_re, ssm_b_im, ssm_c_re, ssm_c_im, ssm_d, w_glu, b_glu,
                 ssm_out_norm, att_out_norm, w_out,
                 y_prompt, y_sample, k_prompt, v_prompt, logf_prompt, hre_prompt, him_prompt,
                 k_sample, v_sample, logf_sample, hre_sample, him_sample):
    f32, r32, bf16, i32 = mybir.dt.float32, mybir.dt.float32r, mybir.dt.bfloat16, mybir.dt.int32
    ALU, ACT, AX = mybir.AluOpType, mybir.ActivationFunctionType, mybir.AxisListType
    ds = bass.ds
    V, S, G, T = nc.vector, nc.scalar, nc.gpsimd, nc.tensor
    ctx = ExitStack()
    sems, phase = {}, [0]

    def sem(name):
        if name not in sems:
            sems[name] = nc.alloc_semaphore(name=f"{name}_{phase[0]}")
        return sems[name]

    def stand(eng, name):
        eng.sem_inc(sem("stand_" + name), 1)

    def free_semaphores():
        nc.clear_and_free_semaphores(list(sems.values()))
        nc.all_engine_barrier()
        sems.clear()
        phase[0] += 1

    def pool_of(stack):
        def sb(name, shape, dt=f32):
            return stack.enter_context(nc.sbuf_tensor(name, shape, dt))
        return sb

    class Order:

        def __init__(self, eng, name):
            self.eng, self.sem, self.base, self.n = eng, sem(name), 0, 0

        def step(self, ins):
            ins.then_inc(self.sem, 1)
            self.n += 1
            return self.base + self.n

        def then(self, ins):
            self.eng.wait_ge(self.sem, self.step(ins))

        def enter(self, it, per):
            self.start, self.per = self.n, per
            self.base = it * per

        def leave(self, count):
            assert self.n - self.start == self.per, ("steps", self.sem, self.n - self.start, self.per)
            self.base, self.n = 0, self.start + self.per * count

    def scratch(name, shape):
        return nc.dram_tensor(name, shape, f32).ap()

    pk_s = scratch("pk_s", [P, 8 * PKW])
    kpad_s = scratch("kpad_s", [P, 240])
    zg_s = scratch("zg_s", [D_SSM, TOK])
    zs_s = scratch("zs_s", [D_SSM, TOK])
    ya_s = scratch("ya_s", [D_ATT, TOK])
    ys_s = scratch("ys_s", [D_SSM, TOK])
    nc_s = scratch("nc_s", [NH, SEQ + PAST + DEC])
    w_in_v = w_in[0].rearrange("(k p) n -> p k n", p=P)
    w_glu_v = w_glu[0].rearrange("(k p) n -> p k n", p=P)
    w_out_v = w_out[0].rearrange("(k p) n -> p k n", p=P)

    with ctx:
        sb = pool_of(ctx)
        ident = sb("ident", [P, P])
        identb = sb("identb", [P, P], bf16)
        maskb = sb("maskb", [P, P], bf16)
        ones = sb("ones", [P, P])
        delta = sb("delta", [P, GC])
        vec = sb("vec", [P, 34])
        epsc = sb("epsc", [P, 1])
        wraw = sb("wraw", [P, RAW, PIECE, P])
        whi = sb("whi", [P, SPL, PIECE, P], r32)
        wlo = sb("wlo", [P, SPL, PIECE, P], r32)
        GB = ctx.enter_context(nc.psum_tensor("GB", [P, 3 * 512], f32))
        TB = ctx.enter_context(nc.psum_tensor("TB", [P, 5 * 512], f32))

        def group(bank, b, p=slice(0, P)):
            return bank[p, 512 * b:512 * b + COLS[b][1]]

        def cols(a, b):
            return a[:, COLS[b][0]:COLS[b][0] + COLS[b][1]]

        def halves(bank, a, p=slice(0, P)):
            return ((bank[p, 0:1024].rearrange("p (b c) -> p b c", b=2)[:, :, 0:CW],
                     a[:, 0:2 * CW].rearrange("p (b c) -> p b c", b=2)), (group(bank, 2, p), cols(a, 2)))

        class Weights:

            def __init__(self, tag, view, xh, xl):
                self.view, self.xh, self.xl, self.tag = view, xh, xl, tag
                self.w_in = [sem(f"{tag}_w_in{i}") for i in range(RAW)]
                self.hi, self.lo, self.mm = sem(f"{tag}_w_hi"), sem(f"{tag}_w_lo"), sem(f"{tag}_w_mm")

            def load(self, eng, m, s, col, k, view=None, apart=False):
                eng.wait_ge(self.lo, m + 1)
                if apart:
                    stand(eng, "load")
                eng.dma_start(wraw[:, s % RAW], (self.view if view is None else view)[:, k:k + PIECE, ds(col, P)]).then_inc(self.w_in[s % RAW], 16)

            def split_hi(self, m, s, loads):
                S.wait_ge(self.w_in[s % RAW], 16 * loads)
                S.wait_ge(self.mm, m + 1)
                S.copy(whi[:, s % SPL], wraw[:, s % RAW]).then_inc(self.hi, 1)

            def split_lo(self, m, s):
                V.wait_ge(self.hi, m + 1)
                V.tensor_tensor(wlo[:, s % SPL], wraw[:, s % RAW], whi[:, s % SPL].bitcast(f32),
                                ALU.subtract).then_inc(self.lo, 1)

            def multiply(self, m, s, k, first, last, xh=None, xl=None, free=None):
                xh, xl = (self.xh, self.xl) if xh is None else (xh, xl)
                T.wait_ge(self.lo, m + 1 + RAW)
                for kk in range(PIECE):
                    for i, (w, x) in enumerate(((whi, xh), (whi, xl), (wlo, xh))):
                        for b, (c, n) in enumerate(COLS):
                            if free and kk == 0 and i == 0:
                                free(b)
                            ins = T.matmul(group(GB, b), w[:, s % SPL, kk], x[:, k + kk, c:c + n],
                                           start=first and kk == 0 and i == 0,
                                           stop=last and kk == PIECE - 1 and i == 2)
                ins.then_inc(self.mm, 1)

            def multiplied(self, m):
                return m + 1 + SPL

            def credit(self, which):
                if which == "pe":
                    T.sem_inc(self.mm, SPL)
                else:
                    V.sem_inc(self.lo, RAW)

        XH, XL = sb("XH", [P, KT, TOK], r32), sb("XL", [P, KT, TOK], r32)
        with ExitStack() as st:
            sbp = pool_of(st)
            xt = sbp("xt", [P, 2, D_MODEL])
            gain = sbp("gain", [P, D_MODEL])
            ssq = sbp("ssq", [P, TT, 3])
            vin = sbp("vin", [34, P])
            pin = sbp("pin", [32, 5, P])
            ldt = sbp("ldt", [32, 2])
            cin = wraw[:].rearrange("p a b c -> p (a b c)").rearrange("p (i n) -> p i n", i=8)
            braw = sbp("braw", [P, 2, 512])
            prm = sbp("prm", [P, 5, 32])
            dtt = sbp("dtt", [P, 32])
            ath = sbp("ath", [P, 2, 32])
            arg = sbp("arg", [P, 14, 32])
            trg = sbp("trg", [P, 2, 14, 32])
            wk = sbp("wk", [P, 2, 14 * 32])
            mag = sbp("mag", [P, 9, 32])
            wki = sbp("wki", [P, 256], i32)
            cf = sbp("cf", [P, 8, 32])
            tmpb = (gain[:, 1024:1536], wk[:].rearrange("p a b -> p (a b)")[:, 0:512])
            pk = sbp("pk", [P, 8, PKW])
            ld_x = [sem("ld_x0"), sem("ld_x1")]
            ld_gain, ld_par, ld_c, st_pk = sem("ld_gain"), sem("ld_par"), sem("ld_c"), sem("st_pk")
            ident_done, par_t, par_ev = sem("ident_done"), sem("par_t"), sem("par_ev")
            sq_done, xs_done, x_t, x_hi, x_lo = (sem(n) for n in ("sq_done", "xs_done", "x_t", "x_hi", "x_lo"))
            sqrt_done, ssq_v, trg_in, trg_sin, c_t, pk_done = (
                sem(n) for n in ("sqrt_done", "ssq_v", "trg_in", "trg_sin", "c_t", "pk_done"))
            rows = [P] * (TT - 1) + [DEC]
            wf = sbp("wf", [P, KT, NH])
            WF = lambda k: (whi, wlo)[k // KH][:, k % KH // PIECE, k % PIECE]
            KH = KT // 2
            xf, gf = xt[:].rearrange("p a n -> p (a n)"), gain
            fx, fl, fe = (xf[0:NH, i * TOK:(i + 1) * TOK] for i in range(3))
            cum = xf[0:NH, TOK:TOK + CT]
            lfs = xf[0:NH, 3 * TOK:3 * TOK + PAST + DEC]
            one8 = gf[0:NH, 0:SEQ]
            bf = sbp("bf", [NH, 1])
            cl = sbp("cl", [P, NH])
            lt = sbp("lt", [P, TT, NH])
            names = ("in", "zero", "hi", "lo", "mm", "fn", "ex", "e1", "ln", "lf", "t_mm", "t_ev", "cum", "out", "fl", "x", "neg", "one")
            e = {n: sem("gate_" + n) for n in names}

            def pkv(row, n=1):
                return pk[:, :, 4 * row:4 * (row + n)].rearrange("p j (n q) -> p n j q", q=4)

            block = ctx.enter_context(ExitStack())
            with nc.Block() as block:
                @block.sync
                def _(sp):
                    def row128(a):
                        return a.rearrange("o (r p) -> (o r) p", p=P)
                    sp.dma_start(xt[:, 0], x_prompt[0, 0:P]).then_inc(ld_x[0], 16)
                    sp.dma_start(gain[:], norm_gain[0:1, :].to_broadcast([P, D_MODEL])).then_inc(ld_gain, 16)
                    for i, a in enumerate((ssm_a_re, ssm_a_im, state_ssm_re, state_ssm_im)):
                        a = a[0, 0] if len(a.shape) == 4 else a[0]
                        i = i if i < 2 else i + 1
                        sp.dma_start(pin[:, i].rearrange("r (g p) -> r g p", g=2),
                                     a.rearrange("(r g) p -> r g p", g=2)).then_inc(ld_par, 16)
                    sp.dma_start(ldt[:], ssm_log_dt[0].rearrange("(r g) -> r g", g=2)).then_inc(ld_par, 16)
                    sp.dma_start(vin[0:8], ssm_d[0].rearrange("(r g) c -> r (g c)", g=8)).then_inc(ld_par, 16)
                    sp.dma_start(vin[8:16], row128(b_glu)).then_inc(ld_par, 16)
                    sp.dma_start(vin[16:24], row128(ssm_out_norm)).then_inc(ld_par, 16)
                    sp.dma_start(vin[24:32], row128(att_out_norm)).then_inc(ld_par, 16)
                    sp.dma_start(vin[32:33], q_norm_gain).then_inc(ld_par, 16)
                    sp.dma_start(vin[33:34], k_norm_gain).then_inc(ld_par, 16)
                    for i, a in enumerate((ssm_c_re, ssm_c_im)):
                        for q in range(4):
                            for g in range(2):
                                src = a[0].rearrange("(q r g) c p -> q g r c p", q=4, g=2)[q, g]
                                sp.dma_start(cin[:, 4 * i + q, g * NP:(g + 1) * NP],
                                             src).then_inc(ld_c, 16)
                    for i, a in enumerate((ssm_b_re, ssm_b_im)):
                        for g in range(2):
                            sp.dma_start(braw[g * NP:(g + 1) * NP, i].rearrange("p (r c) -> p r c", c=GC),
                                         a[0].rearrange("(r g) p c -> g p r c", g=2)[g]).then_inc(ld_c, 16)
                    sp.dma_start(wf[:], w_in_v[:, :, D_PROJ - NH:D_PROJ]).then_inc(e["in"], 16)
                    sp.dma_start(bf[:], b_f.rearrange("o h -> h o")).then_inc(e["in"], 16)
                    sp.dma_start(cl[:], cache_logf[0, 0]).then_inc(e["in"], 16)
                    for m in range(1, TT):
                        if m >= 2:
                            sp.wait_ge(x_t, 4 * (m - 1))
                        src = x_prompt[0, m * P:(m + 1) * P] if m < TT - 1 else x_sample[0]
                        sp.dma_start(xt[0:rows[m], m % 2], src).then_inc(ld_x[m % 2], 16)
                    sp.wait_ge(e["t_ev"], 2)
                    sp.dma_start(logf_prompt[0, 0].rearrange("(m p) h -> p m h", p=P), lt[:, 0:TT - 1]).then_inc(e["out"], 16)
                    sp.dma_start(logf_sample[0, 0], lt[0:DEC, TT - 1]).then_inc(e["out"], 16)
                    sp.wait_ge(e["neg"], 1)
                    sp.dma_start(nc_s, cum).then_inc(e["out"], 16)
                    sp.wait_ge(e["out"], 48)
                    sp.wait_ge(pk_done, 1)
                    sp.dma_start(pk_s, pk[:].rearrange("p a b -> p (a b)")).then_inc(st_pk, 16)
                    sp.wait_ge(st_pk, 16)

                @block.gpsimd
                def _(pool):
                    o = Order(pool, "pool_order")
                    G.memset(epsc[:], EPS)
                    o.then(G.memset(ident[:], 0.0))
                    o.then(G.affine_select(out=ident[:], in_=ident[:], compare_op=ALU.not_equal, fill=1.0, base=0,
                                           pattern=[[-1, P]], channel_multiplier=1))
                    o.then(G.memset(ones[:], 1.0))
                    o.then(G.memset(identb[:], 0.0))
                    G.affine_select(out=maskb[:], in_=identb[:], compare_op=ALU.is_ge, fill=NEG, base=0,
                                    pattern=[[-1, P]], channel_multiplier=1).then_inc(ident_done, 1)
                    pool.wait_ge(ident_done, 1)
                    G.tensor_copy(identb[:], ident[:]).then_inc(ident_done, 1)

                @block.scalar
                def _(act):
                    act.wait_ge(ident_done, 2)
                    o = Order(act, "act_order")

                    def x_square(m):
                        act.wait_ge(ld_x[m % 2], 16 * (m // 2 + 1))
                        n = rows[m]
                        for h in range(2):
                            last = S.activation(GB[0:n, 0:1024], xt[0:n, m % 2, 1024 * h:1024 * (h + 1)], ACT.Square,
                                                accum_out=ssq[0:n, m, h:h + 1])
                            if h == 0:
                                o.then(last)
                        last.then_inc(sq_done, 1)
                        act.wait_ge(ssq_v, m + 1)
                        S.activation(ssq[0:n, m, 2:3], ssq[0:n, m, 0:1], ACT.Sqrt).then_inc(sqrt_done, 1)

                    def x_split(m):
                        n = rows[m]
                        for b in range(4):
                            act.wait_ge(x_t, 4 * m + b + 1)
                            S.copy(XH[:, 4 * b:4 * b + 4, m * P:m * P + n],
                                   TB[:, b * 512:(b + 1) * 512].rearrange("p (k t) -> p k t", k=4)[:, :, 0:n]
                                   ).then_inc(x_hi, 1)
                    x_square(0)
                    for m in range(TT):
                        if m + 1 < TT:
                            x_square(m + 1)
                        x_split(m)
                        if m == 4:
                            act.wait_ge(e["zero"], 2)
                            act.wait_ge(e["in"], 48)
                            for i in range(2):
                                S.copy((whi, wlo)[i][:].rearrange("p a b c -> p (a b) c")[:, :, 0:NH],
                                       wf[:, i * KH:(i + 1) * KH]).then_inc(e["hi"], 1)
                    act.wait_ge(trg_in, 1)
                    S.activation(trg[:].rearrange("p a b c -> p (a b c)"),
                                 trg[:].rearrange("p a b c -> p (a b c)"), ACT.Sin).then_inc(trg_sin, 1)
                    act.wait_ge(e["fn"], 1)
                    S.activation(fe, fl, ACT.Exp).then_inc(e["ex"], 1)
                    act.wait_ge(e["e1"], 1)
                    S.activation(fe, fe, ACT.Ln).then_inc(e["ln"], 1)

                @block.tensor
                def _(pe):
                    pe.wait_ge(ident_done, 2)
                    pe.wait_ge(ld_par, 16 * 11)
                    dt_bc = sem("dt_bc")
                    pe.wait_ge(dt_bc, 1)
                    T.transpose(TB[:, 4 * 512:4 * 512 + 34], vin[:], ident[0:34, 0:34])
                    for i in range(5):
                        ins = T.transpose(TB[:, 4 * 512 + 64 + 32 * i:4 * 512 + 96 + 32 * i], pin[:, i], ident[0:32, 0:32])
                    ins.then_inc(par_t, 1)

                    def tiles(m):
                        n = rows[m]
                        pe.wait_ge(xs_done, m + 1)
                        for b in range(4):
                            if m:
                                pe.wait_ge(x_lo, 4 * (m - 1) + b + 1)
                            for k in range(4):
                                c = b * 512 + k * P
                                ins = T.transpose(TB[:, c:c + n], xt[0:n, m % 2, (4 * b + k) * P:(4 * b + k + 1) * P],
                                                  ident[0:n, 0:n])
                            ins.then_inc(x_t, 1)
                    for m in range(TT):
                        tiles(m)
                        if m == 0:
                            pe.wait_ge(ld_c, 16 * 20)
                            for i in range(8):
                                if i == 4:
                                    pe.wait_ge(par_ev, 3)
                                elif i == 0:
                                    pe.wait_ge(par_ev, 2)
                                ins = T.transpose(TB[:, 4 * 512 + (i % 4) * P:4 * 512 + (i % 4 + 1) * P], cin[:, i], ident[:])
                                if i % 4 == 3:
                                    ins.then_inc(c_t, 1)
                    pe.wait_ge(x_lo, 4 * TT)
                    pe.wait_ge(e["lo"], 2)
                    for k in range(KT):
                        for x in (XH, XL):
                            for b, (c, n) in enumerate(COLS):
                                ins = T.matmul(group(GB, b), WF(k), x[:, k, c:c + n],
                                               start=k == 0 and x is XH, stop=k == KT - 1 and x is XL)
                    ins.then_inc(e["mm"], 1)
                    T.transpose(TB[0:NH, 512:512 + PAST], cl[:], ident[:])
                    pe.wait_ge(e["lf"], 1)
                    for m in range(TT):
                        n = min(P, TOK - m * P)
                        ins = T.transpose(TB[0:n, m * NH:(m + 1) * NH], fx[:, m * P:m * P + n], ident[0:NH, 0:NH])
                    ins.then_inc(e["t_mm"], 1)

                @block.vector
                def _(dve):
                    o = Order(dve, "dve_order")
                    dt_bc = sem("dt_bc")

                    def x_scale(m):
                        n = rows[m]
                        dve.wait_ge(sq_done, m + 1)
                        o.then(V.tensor_tensor(ssq[0:n, m, 0:1], ssq[0:n, m, 0:1], ssq[0:n, m, 1:2], ALU.add))
                        V.tensor_scalar(ssq[0:n, m, 0:1], ssq[0:n, m, 0:1], 1.0 / D_MODEL, EPS, ALU.mult, ALU.add
                                        ).then_inc(ssq_v, 1)
                        dve.wait_ge(sqrt_done, m + 1)
                        v, y, t = ssq[0:n, m, 0:1], ssq[0:n, m, 1:2], ssq[0:n, m, 2:3]
                        o.then(V.reciprocal(y, t))
                        o.then(V.tensor_tensor(t, y, y, ALU.mult))
                        o.then(V.scalar_tensor_tensor(t, t, -0.5, v, ALU.mult, ALU.mult))
                        o.then(V.scalar_tensor_tensor(y, t, 1.5, y, ALU.add, ALU.mult))
                        if m == 0:
                            dve.wait_ge(ld_gain, 16)
                        V.scalar_tensor_tensor(xt[0:n, m % 2], xt[0:n, m % 2], ssq[0:n, m, 1:2], gain[0:n],
                                               ALU.mult, ALU.mult).then_inc(xs_done, 1)

                    def x_rest(m):
                        n = rows[m]
                        for b in range(4):
                            dve.wait_ge(x_hi, 4 * m + b + 1)
                            tb = TB[:, b * 512:(b + 1) * 512].rearrange("p (k t) -> p k t", k=4)[:, :, 0:n]
                            V.tensor_tensor(XL[:, 4 * b:4 * b + 4, m * P:m * P + n], tb,
                                            XH[:, 4 * b:4 * b + 4, m * P:m * P + n].bitcast(f32),
                                            ALU.subtract).then_inc(x_lo, 1)

                    def exp_poly(out, x, n):
                        t, r = wk[:, 0, 0:n], wk[:, 1, 0:n]
                        o.then(V.tensor_scalar(x, x, -87.0, 88.0, ALU.max, ALU.min))
                        o.then(V.tensor_scalar(t, x, 1.0 / math.log(2.0), MAGIC, ALU.mult, ALU.add))
                        o.then(V.tensor_scalar(t, t, -MAGIC, None, ALU.add))
                        o.then(V.scalar_tensor_tensor(r, t, -0.693359375, x, ALU.mult, ALU.add))
                        o.then(V.scalar_tensor_tensor(r, t, 2.12194440e-4, r, ALU.mult, ALU.add))
                        o.then(V.tensor_scalar(out, r, 1.0 / 5040, None, ALU.mult))
                        for c in (1.0 / 720, 1.0 / 120, 1.0 / 24, 1.0 / 6, 0.5, 1.0):
                            o.then(V.scalar_tensor_tensor(out, out, c, r, ALU.add, ALU.mult))
                        o.then(V.tensor_scalar(out, out, 1.0, None, ALU.add))
                        o.then(V.tensor_scalar(wki[:, 0:n], t, 127.0, 8388608.0, ALU.add, ALU.mult))
                        o.then(V.tensor_tensor(out, out, wki[:, 0:n].bitcast(f32), ALU.mult))

                    dve.wait_ge(ld_par, 16 * 11)
                    V.tensor_copy(pin[:, 2].rearrange("r (g p) -> r g p", g=2),
                                  ldt[:].unsqueeze(2).to_broadcast([32, 2, NP])).then_inc(dt_bc, 1)
                    dve.wait_ge(ident_done, 2)
                    V.tensor_reduce(delta[:], ident[:].rearrange("p (g c) -> p c g", c=GC), AX.X, ALU.add)
                    x_scale(0)
                    dve.wait_ge(par_t, 1)
                    V.tensor_copy(vec[:], TB[:, 4 * 512:4 * 512 + 34]).then_inc(par_ev, 1)
                    V.tensor_copy(prm[:].rearrange("p a b -> p (a b)"), TB[:, 4 * 512 + 64:4 * 512 + 224]).then_inc(par_ev, 1)
                    dve.wait_ge(par_ev, 2)
                    for i in range(2):
                        V.memset((whi, wlo)[i][:].rearrange("p a b c -> p (a b c)").bitcast(f32), 0.0).then_inc(e["zero"], 1)
                    x_scale(1)
                    x_rest(0)
                    dve.wait_ge(c_t, 1)
                    cre = pk[:, :, NPR * 4 + 128:NPR * 4 + 192]
                    cim = pk[:, :, NPR * 4 + 192:NPR * 4 + 256]
                    V.tensor_copy(cre, TB[:, 4 * 512:5 * 512].rearrange("p (j c) -> p j c", j=8)).then_inc(par_ev, 1)
                    dve.wait_ge(c_t, 2)
                    o.then(V.tensor_copy(cim, TB[:, 4 * 512:5 * 512].rearrange("p (j c) -> p j c", j=8)))
                    for m in range(1, TT):
                        if m + 1 < TT:
                            x_scale(m + 1)
                        x_rest(m)
                        if m == 5:
                            dve.wait_ge(e["hi"], 2)
                            for i in range(2):
                                w8 = (whi, wlo)[i][:].rearrange("p a b c -> p (a b) c")
                                V.tensor_tensor(w8[:, :, 32:32 + NH], wf[:, i * KH:(i + 1) * KH], w8[:, :, 0:NH].bitcast(f32),
                                                ALU.subtract).then_inc(e["lo"], 1)
                    exp_poly(dtt[:], prm[:, 2], 32)
                    o.then(V.tensor_tensor(ath[:], prm[:, 0:2], dtt[:].unsqueeze(1).to_broadcast([P, 2, 32]), ALU.mult))
                    for k in range(14):
                        f = float(k + 1) if k < 8 else float(L << (k - 7))
                        last = o.step(V.tensor_scalar(arg[:, k], ath[:, 1], f, None, ALU.mult))
                    dve.wait_ge(o.sem, last)
                    argf = arg[:].rearrange("p a b -> p (a b)")
                    C1, C2, C3 = 6.28125, 1.9350051879882812e-3, 3.0199159819567e-7
                    for i, quarter in ((0, 0.25), (1, 0.0)):
                        t = wk[:, i]
                        r = trg[:, i].rearrange("p a b -> p (a b)")
                        o.then(V.tensor_scalar(t, argf, 1.0 / (2 * math.pi), quarter, ALU.mult, ALU.add))
                        o.then(V.tensor_scalar(t, t, MAGIC, None, ALU.add))
                        o.then(V.tensor_scalar(t, t, -MAGIC, None, ALU.add))
                        o.then(V.scalar_tensor_tensor(r, t, -C1, argf, ALU.mult, ALU.add))
                        o.then(V.scalar_tensor_tensor(r, t, -C2, r, ALU.mult, ALU.add))
                        o.then(V.scalar_tensor_tensor(r, t, -C3, r, ALU.mult, ALU.add))
                        if quarter:
                            o.then(V.tensor_scalar(r, r, math.pi / 2, None, ALU.add))
                        ins = V.tensor_scalar(r, r, -3.1415925, 3.1415925, ALU.max, ALU.min)
                        if quarter:
                            o.then(ins)
                        else:
                            ins.then_inc(trg_in, 1)
                    dve.wait_ge(trg_in, 1)
                    dve.wait_ge(x_t, 4 * TT)
                    dve.wait_ge(e["mm"], 1)
                    V.memset(one8, 1.0).then_inc(e["one"], 1)
                    for src, dst in halves(GB, fl, slice(32, 32 + NH)):
                        ins = V.tensor_copy(dst, src)
                    ins.then_inc(e["fl"], 1)
                    dve.wait_ge(e["fl"], 1)
                    for (src, dst), (_, low) in zip(halves(GB, fx, slice(0, NH)), halves(GB, fl)):
                        ins = V.scalar_tensor_tensor(dst, src, bf[:], low, ALU.add, ALU.add)
                    ins.then_inc(e["x"], 1)
                    dve.wait_ge(e["x"], 1)
                    V.scalar_tensor_tensor(fl, fx, -1.0, fx, ALU.mult, ALU.min).then_inc(e["fn"], 1)
                    for k in range(8):
                        last = o.step(V.tensor_scalar(mag[:, k + 1], ath[:, 0], float(k + 1), None, ALU.mult))
                    dve.wait_ge(o.sem, last)
                    xm = tmpb[0][:, 0:256]
                    o.then(V.tensor_copy(xm, mag[:, 1:9].rearrange("p a b -> p (a b)")))
                    exp_poly(mag[:, 1:9].rearrange("p a b -> p (a b)"), xm, 256)
                    dve.wait_ge(e["ex"], 1)
                    V.tensor_scalar(fe, fe, 1.0, None, ALU.add).then_inc(e["e1"], 1)
                    dve.wait_ge(trg_sin, 1)
                    o.then(V.memset(pkv(AR), 1.0))
                    o.then(V.memset(pkv(AI), 0.0))

                    def as_jq(a):
                        return a.rearrange("p n (j q) -> p n j q", q=4)
                    for k in range(8):
                        V.tensor_tensor(pkv(AR + 1 + k), as_jq(mag[:, k + 1:k + 2]), as_jq(trg[:, 0, k:k + 1]), ALU.mult)
                        last = o.step(V.tensor_tensor(pkv(AI + 1 + k), as_jq(mag[:, k + 1:k + 2]),
                                                      as_jq(trg[:, 1, k:k + 1]), ALU.mult))
                    for lv in range(NLV):
                        o.step(V.tensor_copy(pkv(WR + lv), as_jq(trg[:, 0, 7 + lv:8 + lv])))
                        o.step(V.tensor_scalar(pkv(WI + lv), as_jq(trg[:, 1, 7 + lv:8 + lv]), -1.0, None, ALU.mult))
                    o.step(V.tensor_copy(pkv(MG), as_jq(mag[:, 8:9])))
                    o.step(V.tensor_copy(pkv(H0), as_jq(prm[:, 3:4])))
                    last = o.step(V.tensor_copy(pkv(H0 + 1), as_jq(prm[:, 4:5])))
                    dve.wait_ge(o.sem, last)
                    dve.wait_ge(par_ev, 2)
                    o.then(V.tensor_copy(pk[:, :, PKW - 1], vec[:, 0:8]))
                    dve.wait_ge(e["ln"], 1)
                    V.scalar_tensor_tensor(fx, fx, 0.0, fe, ALU.min, ALU.subtract).then_inc(e["lf"], 1)
                    ar, ai = prm[:, 0], prm[:, 1]
                    nr, ni, den, t1 = cf[:, 0], cf[:, 1], cf[:, 2], cf[:, 3]
                    jq = lambda a: a.rearrange("p (j q) -> p j q", q=4)
                    o.then(V.tensor_scalar(jq(nr), pkv(AR + 1)[:, 0], -1.0, None, ALU.add))
                    o.then(V.tensor_copy(jq(ni), pkv(AI + 1)[:, 0]))
                    o.then(V.tensor_tensor(den, ar, ar, ALU.mult))
                    o.then(V.tensor_tensor(t1, ai, ai, ALU.mult))
                    o.then(V.tensor_tensor(den, den, t1, ALU.add))
                    o.then(V.reciprocal(den, den))
                    for i, (a, b, op) in enumerate(((nr, ni, ALU.add), (ni, nr, ALU.subtract))):
                        c = cf[:, 4 + i]
                        o.then(V.tensor_tensor(c, a, ar, ALU.mult))
                        o.then(V.tensor_tensor(t1, b, ai, ALU.mult))
                        o.then(V.tensor_tensor(c, c, t1, op))
                        o.then(V.tensor_tensor(c, c, den, ALU.mult))
                    dve.wait_ge(e["t_mm"], 1)
                    V.tensor_copy(lt[:, 0:TT - 1], TB[:, 0:64].rearrange("p (m h) -> p m h", h=NH)).then_inc(e["t_ev"], 1)
                    V.tensor_copy(lt[0:DEC, TT - 1], TB[0:DEC, 64:72]).then_inc(e["t_ev"], 1)
                    V.tensor_copy(lfs[:, 0:PAST], TB[0:NH, 512:512 + PAST]).then_inc(e["cum"], 1)
                    V.tensor_copy(lfs[:, PAST:], fx[:, SEQ:TOK]).then_inc(e["cum"], 1)
                    dve.wait_ge(e["one"], 1)
                    V.tensor_tensor_scan(cum[:, 0:SEQ], one8, fx[:, 0:SEQ], 0.0, ALU.mult, ALU.add).then_inc(e["cum"], 1)
                    dve.wait_ge(e["cum"], 3)
                    V.tensor_tensor_scan(cum[:, SEQ:], one8[:, 0:PAST + DEC], lfs, 0.0, ALU.mult, ALU.add).then_inc(e["cum"], 1)
                    dve.wait_ge(e["cum"], 4)
                    V.tensor_scalar(cum, cum, -1.0, None, ALU.mult).then_inc(e["neg"], 1)
                    dve.wait_ge(ld_c, 16 * 20)
                    v3 = lambda a: a.rearrange("p (r c) -> p r c", c=GC)
                    for i, op in ((0, ALU.subtract), (1, ALU.add)):
                        c0 = cf[:, 4].unsqueeze(2).to_broadcast([P, 32, GC])
                        c1 = cf[:, 5].unsqueeze(2).to_broadcast([P, 32, GC])
                        o.then(V.tensor_tensor(v3(tmpb[0]), v3(braw[:, i]), c0, ALU.mult))
                        o.then(V.tensor_tensor(v3(tmpb[1]), v3(braw[:, 1 - i]), c1, ALU.mult))
                        out = pk[:, :, NPR * 4 + 64 * i:NPR * 4 + 64 * (i + 1)]
                        ins = V.tensor_tensor(out, tmpb[0].rearrange("p (j c) -> p j c", j=8),
                                              tmpb[1].rearrange("p (j c) -> p j c", j=8), op)
                        if i == 0:
                            o.then(ins)
                        else:
                            ins.then_inc(pk_done, 1)

        with ExitStack() as st:
            sbp = pool_of(st)
            U = sbp("U", [P, 8 * SC])
            Ug = U[:].rearrange("p (g c) -> p g c", c=SC)
            UZ = sbp("UZ", [P, TOK])
            UC = sbp("UC", [P, 1024])
            UCS = sbp("UCS", [P, 1024])
            SS = sbp("SS", [P, 2, 4 * SC])
            M1 = sbp("M1", [P, 2, 4 * SC])
            M2 = sbp("M2", [P, 2, 4 * SC])
            TR = sbp("TR", [P, 2, 4, SC])
            DC = sbp("DC", [P, 4, SC])
            H = sbp("H", [P, 8, HC])
            LS = sbp("LS", [P, 8, P])
            Q = sbp("Q", [P, 8, 9 * GC])
            MT = sbp("MT", [P, 8, P])
            KS = sbp("KS", [P, P])
            PJ = sbp("PJ", [P, PKW])
            BD = sbp("BD", [P, 8, 2 * GC])
            FB = sbp("FB", [P, 16])
            FS = sbp("FS", [16, P])
            flat = lambda a: a.rearrange("p a b -> p (a b)")
            GR = flat(M1[:])[:, 0:1024].rearrange("p (a q r c) -> p a q r c", a=2, q=4, r=L)
            GT = flat(SS[:])[:, 0:1024].rearrange("p (a q r c) -> p a q r c", a=2, q=4, r=L)
            Y = flat(SS[:]).rearrange("p (g c) -> p g c", c=SC)
            row = lambda r, n=1: PJ[:, 4 * r:4 * (r + n)].rearrange("p (n q) -> p n q", q=4)
            bc_ = lambda i: PJ[:, NPR * 4 + 64 * i:NPR * 4 + 64 * (i + 1)].rearrange("p (q c) -> p q c", c=GC)
            W = Weights("ssm", w_in_v, XH, XL)
            NPC = 2 * KT // PIECE
            names = ("pj_in", "g_ready", "bd_ready", "q_ready", "t_ready", "ls_mm", "k_mm", "ls_act", "ls_dve", "ks_ready",
                     "kpad_out", "mt_in", "ga", "gd", "st1_mm", "st1_act", "st1_dve", "st2_mm", "st2_act", "st2_dve",
                     "s_mm", "s_act", "m1_done", "m2_done", "g_done", "scan_done", "p1_done", "p2_done",
                     "h_dve", "h_pool", "y_mm", "y_act", "y_dve", "yt_mm", "yt_act", "yt_dve", "z_mm", "z_act", "zg_out", "zs_out",
                     "fb_ready", "fin_mm", "fin_ev", "fin_out", "dec_ready", "zero_done")
            e = {n: sem("ssm_" + n) for n in names}

            with nc.Block() as block:
                @block.sync
                def _(sp):
                    with sp.Fori(0, 8) as j:
                        for s in range(NPC):
                            col = j * P + (0 if s < NPC // 2 else D_SSM)
                            W.load(sp, j * NPC + s, s, col, PIECE * (s % (NPC // 2)))
                            if s == NPC - 1:
                                sp.wait_ge(e["y_mm"], j)
                                sp.wait_ge(e["kpad_out"], 16 * (j + 2))
                                for r in range(L):
                                    sp.dma_start(MT[r * GC:(r + 1) * GC],
                                                  kpad_s[:, GC * r:GC * r + P].rearrange("(g c) n -> c g n", g=8)
                                                  ).then_inc(e["mt_in"], 16)
                    for s in range(SPL):
                        W.load(sp, 8 * NPC + s, s, 0, 0)

                @block.scalar
                def _(act):
                    act.wait_ge(e["zero_done"], 1)
                    act.dma_start(kpad_s[:, 0:112], UC[:, 0:112]).then_inc(e["kpad_out"], 16)
                    for s in range(SPL):
                        W.split_hi(s, s, 1)
                    with act.Fori(0, 8) as j:
                        for s in range(NPC):
                            m = s + SPL
                            if s == 0:
                                act.wait_ge(e["g_ready"], j)
                                act.wait_ge(e["bd_ready"], j)
                                act.wait_ge(e["q_ready"], j)
                                act.wait_ge(e["ks_ready"], j)
                                act.wait_ge(e["dec_ready"], j)
                                act.wait_ge(e["s_act"], 4 * j)
                                act.dma_start(PJ[:], pk_s[:, ds(j * PKW, PKW)]).then_inc(e["pj_in"], 16)
                            if s == 7:
                                act.wait_ge(W.mm, W.multiplied(j * NPC + s))
                                act.wait_ge(e["zg_out"], 16 * j)
                                S.copy(cols(UZ, 0), group(GB, 0)).then_inc(e["ga"], 1)
                                S.copy(cols(UZ, 2), group(GB, 2)).then_inc(e["ga"], 1)
                            if s == NPC - 1:
                                act.wait_ge(W.mm, W.multiplied(j * NPC + s))
                                for src, dst in halves(GB, U):
                                    S.activation(dst, src, ACT.Silu).then_inc(e["ga"], 1)
                            W.split_hi(j * NPC + m, m, j * (NPC // RAW) + m // RAW + 1)
                            if s == 7:
                                act.wait_ge(e["ls_mm"], j + 1)
                                S.copy(LS[:, 0:4], TB[:, 0:512].rearrange("p (a b) -> p a b", a=4)).then_inc(e["ls_act"], 1)
                            if s == 6:
                                act.wait_ge(e["ks_ready"], j + 1)
                                act.dma_start(kpad_s[:, 112:240], KS[:]).then_inc(e["kpad_out"], 16)
                            if s == 8:
                                act.wait_ge(e["st1_mm"], j + 1)
                                S.copy(UC[:].rearrange("p (g r c) -> p r g c", g=8, r=L)[:, 0:4],
                                       TB[:, 3 * 512:4 * 512].rearrange("p (r g c) -> p r g c", r=4, g=8))
                                S.copy(UCS[0:8].rearrange("p (g r c) -> p r g c", g=8, r=L)[:, 0:4],
                                       TB[0:8, 0:512].rearrange("p (r g c) -> p r g c", r=4, g=8)).then_inc(e["st1_act"], 1)
                            if s == 9:
                                act.wait_ge(e["st2_mm"], j + 1)
                                act.wait_ge(e["zs_out"], 16 * j)
                                S.copy(Ug[:, 0:4, 0:NB], TB[:, 2 * 512:3 * 512].rearrange("p (g c) -> p g c", g=4)
                                       ).then_inc(e["st2_act"], 1)
                            if s == 10:
                                act.wait_ge(e["s_mm"], j + 1)
                                for b in range(3):
                                    n = min(3, 8 - 3 * b) * SC
                                    S.copy(flat(SS[:])[:, 3 * b * SC:3 * b * SC + n], TB[:, 512 * b:512 * b + n]
                                           ).then_inc(e["s_act"], 1)
                                act.wait_ge(e["s_act"], 4 * j + 3)
                                S.copy(flat(SS[:]).rearrange("p (a c) -> p a c", c=SC)[:, :, NB],
                                       PJ[:, 4 * H0:4 * H0 + 8]).then_inc(e["s_act"], 1)
                            if s == 13:
                                act.wait_ge(e["y_mm"], j + 1)
                                S.copy(Y[:, 0:3], TB[:, 3 * 512:3 * 512 + 3 * SC].rearrange("p (g c) -> p g c", g=3))
                                S.copy(Y[:, 6:8], TB[:, 0:2 * SC].rearrange("p (g c) -> p g c", g=2)).then_inc(e["y_act"], 1)
                            if s == 14:
                                act.wait_ge(e["yt_mm"], j + 1)
                                S.copy(UC[:].rearrange("p (t g c) -> p g t c", t=L, g=8)[:, 0:4],
                                       TB[:, 512:1024].rearrange("p (g t c) -> p g t c", g=4, t=L))
                                S.copy(UCS[0:8].rearrange("p (t g c) -> p g t c", t=L, g=8)[:, 0:4],
                                       TB[0:8, 3 * 512:4 * 512].rearrange("p (g t c) -> p g t c", g=4, t=L)).then_inc(e["yt_act"], 1)
                            if s == 15:
                                act.wait_ge(e["ga"], 4 * j + 4)
                                act.dma_start(zs_s[ds(j * P, P), :], U[:, 0:TOK]).then_inc(e["zs_out"], 16)
                                act.wait_ge(e["z_mm"], j + 1)
                                zt = lambda a: a.rearrange("p (c t) -> p t c", t=L)
                                for hlf in range(2):
                                    S.activation(zt(UZ[:, 0:SEQ])[:, 4 * hlf:4 * hlf + 4],
                                                 TB[:, 512 * (1 + hlf):512 * (2 + hlf)].rearrange("p (t c) -> p t c", t=4), ACT.Gelu)
                                S.activation(zt(UZ[:, SEQ:TOK]), TB[:, 0:DEC].rearrange("p (t c) -> p t c", t=L),
                                             ACT.Gelu).then_inc(e["z_act"], 1)
                                act.wait_ge(e["z_act"], j + 1)
                                act.dma_start(zg_s[ds(j * P, P), :], UZ[:]).then_inc(e["zg_out"], 16)
                                act.wait_ge(e["fin_ev"], j + 1)
                                for i, dst in enumerate((hre_prompt, him_prompt, hre_sample, him_sample)):
                                    act.dma_start(dst[0, 0, ds(8 * j, 8), :],
                                                  FS[8 * (i // 2):8 * (i // 2) + 8, (i % 2) * NP:(i % 2 + 1) * NP]
                                                  ).then_inc(e["fin_out"], 16)
                    act.wait_ge(e["zs_out"], 16 * 8)
                    act.wait_ge(e["zg_out"], 16 * 8)
                    act.wait_ge(e["fin_out"], 64 * 8)
                    act.wait_ge(W.w_in[0], 16 * (8 * NPC // RAW + 1))
                    act.wait_ge(W.w_in[1], 16 * (8 * NPC // RAW + 1))

                @block.vector
                def _(dve):
                    o = Order(dve, "dve_ssm")
                    V.memset(UC[:, 0:112], 0.0).then_inc(e["zero_done"], 1)
                    V.memset(BD[:], 0.0).then_inc(e["zero_done"], 1)
                    V.memset(H[:, :, 0:1], 0.0).then_inc(e["zero_done"], 1)
                    dve.wait_ge(e["zero_done"], 3)
                    dve.sem_inc(W.lo, RAW)
                    for s in range(SPL):
                        W.split_lo(s, s)
                    with dve.Fori(0, 8) as j:
                        o.enter(j, 4)
                        for s in range(NPC):
                            m = s + SPL
                            if s == 7:
                                dve.wait_ge(W.mm, W.multiplied(j * NPC + s))
                                dve.wait_ge(e["zg_out"], 16 * j)
                                V.tensor_copy(cols(UZ, 1), group(GB, 1)).then_inc(e["gd"], 1)
                            W.split_lo(j * NPC + m, m)
                            if s == 0:
                                dve.wait_ge(e["pj_in"], 16 * (j + 1))
                                dve.wait_ge(e["z_mm"], j)
                                o.then(V.tensor_copy(DC[:], row(MG)[:, 0].unsqueeze(2).to_broadcast([P, 4, SC])))
                                V.memset(DC[:, :, 0:NB + 1:NB], 0.0).then_inc(e["dec_ready"], 1)
                                for i in range(2):
                                    for g in range(2):
                                        ins = V.tensor_copy(BD[i * NP:(i + 1) * NP, g::2, g * GC:(g + 1) * GC],
                                                            bc_(i)[g * NP:(g + 1) * NP])
                                ins.then_inc(e["bd_ready"], 1)
                                qa = lambda base: row(base, 9).rearrange("p r q -> p q r").unsqueeze(3).to_broadcast([P, 4, 9, GC])
                                qc = lambda i: bc_(i).unsqueeze(2).to_broadcast([P, 4, 9, GC])
                                q4 = lambda t: t[:, 0:576].rearrange("p (q r c) -> p q r c", q=4, r=9)
                                q3 = lambda t, g: t[g * NP:(g + 1) * NP, 0:576].rearrange("p (q n) -> p q n", q=4)
                                V.tensor_tensor(q4(UC), qa(AR), qc(2), ALU.mult)
                                o.then(V.tensor_tensor(q4(UCS), qa(AI), qc(3), ALU.mult))
                                for g in range(2):
                                    ins = V.tensor_tensor(Q[0:NP, g::2], q3(UC, g), q3(UCS, g), ALU.subtract)
                                o.then(ins)
                                V.tensor_tensor(q4(UC), qa(AI), qc(2), ALU.mult)
                                o.then(V.tensor_tensor(q4(UCS), qa(AR), qc(3), ALU.mult))
                                for g in range(2):
                                    ins = V.scalar_tensor_tensor(Q[NP:P, g::2], q3(UC, g), -1.0, q3(UCS, g), ALU.mult, ALU.subtract)
                                ins.then_inc(e["q_ready"], 1)
                            if s == 5:
                                dve.wait_ge(e["k_mm"], j + 1)
                                dve.wait_ge(e["kpad_out"], 16 * (j + 1))
                                V.tensor_copy(KS[:, GC:P], TB[:, 2 * 512 + GC:2 * 512 + P])
                                V.scalar_tensor_tensor(KS[:, 0:GC], delta[:], PJ[:, PKW - 1:PKW], TB[:, 2 * 512:2 * 512 + GC],
                                                       ALU.mult, ALU.add).then_inc(e["ks_ready"], 1)
                            if s == 7:
                                dve.wait_ge(e["ls_mm"], j + 1)
                                V.tensor_copy(LS[:, 4:8], TB[:, 512:1024].rearrange("p (a b) -> p a b", a=4)).then_inc(e["ls_dve"], 1)
                            if s == 8:
                                dve.wait_ge(e["st1_mm"], j + 1)
                                V.tensor_copy(UC[:].rearrange("p (g r c) -> p r g c", g=8, r=L)[:, 4:8],
                                              TB[:, 4 * 512:5 * 512].rearrange("p (r g c) -> p r g c", r=4, g=8))
                                V.tensor_copy(UCS[0:8].rearrange("p (g r c) -> p r g c", g=8, r=L)[:, 4:8],
                                              TB[0:8, 512:1024].rearrange("p (r g c) -> p r g c", r=4, g=8)).then_inc(e["st1_dve"], 1)
                            if s == 9:
                                dve.wait_ge(e["st2_mm"], j + 1)
                                dve.wait_ge(e["zs_out"], 16 * j)
                                V.memset(Ug[:, :, NB:NB + 1], 0.0)
                                V.tensor_copy(Ug[:, 4:8, 0:NB], TB[:, 3 * 512:4 * 512].rearrange("p (g c) -> p g c", g=4))
                                V.tensor_copy(Ug[:, :, NB + 1:SC], TB[:, 4 * 512:4 * 512 + DEC].rearrange("p (g c) -> p g c", g=8)
                                              ).then_inc(e["st2_dve"], 1)
                            if s == 10:
                                th = lambda i: TR[:, i].rearrange("p a b -> p (a b)")
                                tr = lambda i: th(i).unsqueeze(1).to_broadcast([P, 2, 4 * SC])
                                dve.wait_ge(e["s_act"], 4 * (j + 1))
                                dve.wait_ge(e["t_ready"], j + 1)
                                V.tensor_tensor(M1[:], SS[:], tr(0), ALU.mult)
                                V.tensor_tensor(M2[:, 0], SS[:, 0], th(1), ALU.mult).then_inc(e["m1_done"], 1)
                                dve.wait_ge(e["m1_done"], j + 1)
                                dve.wait_ge(e["m2_done"], j + 1)
                                V.tensor_tensor(SS[:, 0], M1[:, 0], M2[:, 1], ALU.subtract).then_inc(e["g_done"], 1)
                                V.tensor_tensor(SS[:, 1], M1[:, 1], M2[:, 0], ALU.add).then_inc(e["g_done"], 1)
                                dcf = DC[:].rearrange("p a b -> p (a b)")
                                for i in range(2):
                                    dve.wait_ge(e["g_done"], 2 * j + 2)
                                    V.tensor_tensor_scan(M1[:, i], dcf, SS[:, i], 0.0, ALU.mult, ALU.add).then_inc(e["scan_done"], 1)
                                dve.wait_ge(e["scan_done"], 2 * j + 2)
                                V.tensor_tensor(SS[:], M1[:], tr(0), ALU.mult)
                                V.tensor_tensor(M2[:, 1], M1[:, 1], th(1), ALU.mult).then_inc(e["p1_done"], 1)
                                dve.wait_ge(e["p1_done"], j + 1)
                                dve.wait_ge(e["p2_done"], j + 1)
                                h4 = lambda t, i, g: t[g * NP:(g + 1) * NP, i].rearrange("p (q c) -> p q c", q=4)
                                V.tensor_tensor(H[0:NP, 1::2, 1:HC], h4(SS, 0, 1), h4(M2, 1, 1), ALU.add)
                                V.tensor_tensor(H[NP:P, 1::2, 1:HC], h4(SS, 1, 1), h4(M2, 0, 1), ALU.subtract)
                                V.tensor_tensor(H[NP:P, 0::2, 1:HC], h4(SS, 1, 0), h4(M2, 0, 0), ALU.subtract).then_inc(e["h_dve"], 1)
                            if s == 13:
                                dve.wait_ge(e["h_dve"], j + 1)
                                dve.wait_ge(e["h_pool"], j + 1)
                                V.tensor_copy(FB[:, 0:8], H[:, :, NB])
                                V.tensor_copy(FB[:, 8:16], H[:, :, HC - 1]).then_inc(e["fb_ready"], 1)
                                dve.wait_ge(e["y_mm"], j + 1)
                                V.tensor_copy(Y[:, 3:6], TB[:, 4 * 512:4 * 512 + 3 * SC].rearrange("p (g c) -> p g c", g=3)
                                              ).then_inc(e["y_dve"], 1)
                            if s == 14:
                                dve.wait_ge(e["yt_mm"], j + 1)
                                V.tensor_copy(UC[:].rearrange("p (t g c) -> p g t c", t=L, g=8)[:, 4:8],
                                              TB[:, 1024:1536].rearrange("p (g t c) -> p g t c", g=4, t=L))
                                V.tensor_copy(UCS[0:8].rearrange("p (t g c) -> p g t c", t=L, g=8)[:, 4:8],
                                              TB[0:8, 4 * 512:5 * 512].rearrange("p (g t c) -> p g t c", g=4, t=L)).then_inc(e["yt_dve"], 1)
                            if s == 15:
                                dve.wait_ge(e["fin_mm"], j + 1)
                                dve.wait_ge(e["fin_out"], 64 * j)
                                V.tensor_copy(FS[:], TB[0:16, 4 * 512:4 * 512 + P]).then_inc(e["fin_ev"], 1)
                    o.leave(8)

                @block.gpsimd
                def _(pool):
                    o = Order(pool, "pool_ssm")
                    PO = 32
                    with pool.Fori(0, 8) as j:
                        o.enter(j, PO)
                        pool.wait_ge(e["pj_in"], 16 * (j + 1))
                        pool.wait_ge(e["p1_done"], j)
                        pool.wait_ge(e["z_mm"], j)
                        stand(pool, "pool")
                        a = lambda base: row(base, L).rearrange("p r q -> p q r").unsqueeze(3).to_broadcast([P, 4, L, GC])
                        b = lambda i: bc_(i).unsqueeze(2).to_broadcast([P, 4, L, GC])
                        G.tensor_tensor(GT[:, 0], a(AR), b(0), ALU.mult)
                        o.then(G.tensor_tensor(GT[:, 1], a(AI), b(1), ALU.mult))
                        o.then(G.tensor_tensor(GR[:, 0], GT[:, 0], GT[:, 1], ALU.subtract))
                        G.tensor_tensor(GT[:, 0], a(AR), b(1), ALU.mult)
                        o.then(G.tensor_tensor(GT[:, 1], a(AI), b(0), ALU.mult))
                        G.tensor_tensor(GR[:, 1], GT[:, 0], GT[:, 1], ALU.add).then_inc(e["g_ready"], 1)
                        G.memset(TR[:, 0, :, 0:1], 1.0)
                        o.then(G.memset(TR[:, 1, :, 0:1], 0.0))
                        for lv in range(NLV):
                            n = 1 << lv
                            ta = M2[:, 0, 0:4 * n].rearrange("p (q c) -> p q c", q=4)
                            tb = M2[:, 1, 0:4 * n].rearrange("p (q c) -> p q c", q=4)
                            wr = row(WR + lv)[:, 0].unsqueeze(2).to_broadcast([P, 4, n])
                            wi = row(WI + lv)[:, 0].unsqueeze(2).to_broadcast([P, 4, n])
                            re, im = TR[:, 0, :, 0:n], TR[:, 1, :, 0:n]
                            G.tensor_tensor(ta, re, wr, ALU.mult)
                            o.then(G.tensor_tensor(tb, im, wi, ALU.mult))
                            o.then(G.tensor_tensor(TR[:, 0, :, n:2 * n], ta, tb, ALU.subtract))
                            G.tensor_tensor(ta, re, wi, ALU.mult)
                            o.then(G.tensor_tensor(tb, im, wr, ALU.mult))
                            o.then(G.tensor_tensor(TR[:, 1, :, n:2 * n], ta, tb, ALU.add))
                        stand(pool, "pool")
                        G.tensor_copy(TR[:].rearrange("p a q c -> p (a q) c")[:, :, NB:SC],
                                      TR[:].rearrange("p a q c -> p (a q) c")[:, :, 0:NBS + 1]).then_inc(e["t_ready"], 1)
                        th = TR[:, 1].rearrange("p a b -> p (a b)")
                        pool.wait_ge(e["t_ready"], j + 1)
                        pool.wait_ge(e["s_act"], 4 * (j + 1))
                        G.tensor_tensor(M2[:, 1], SS[:, 1], th, ALU.mult).then_inc(e["m2_done"], 1)
                        pool.wait_ge(e["scan_done"], 2 * j + 1)
                        G.tensor_tensor(M2[:, 0], M1[:, 0], th, ALU.mult).then_inc(e["p2_done"], 1)
                        pool.wait_ge(e["p1_done"], j + 1)
                        h4 = lambda t, i, g: t[g * NP:(g + 1) * NP, i].rearrange("p (q c) -> p q c", q=4)
                        G.tensor_tensor(H[0:NP, 0::2, 1:HC], h4(SS, 0, 0), h4(M2, 1, 0), ALU.add).then_inc(e["h_pool"], 1)
                    o.leave(8)

                @block.tensor
                def _(pe):
                    pe.wait_ge(e["zero_done"], 3)
                    W.credit("pe")
                    gb = (2, 3, 4)
                    with pe.Fori(0, 8) as j:
                        for s in range(NPC):
                            free = None
                            if s == 0:
                                def free(b):
                                    if b == 0:
                                        pe.wait_ge(e["ga"], 4 * j)
                            if s == 8:
                                def free(b):
                                    pe.wait_ge(e["gd"] if b == 1 else e["ga"], j + 1 if b == 1 else 4 * j + 1 + b // 2)
                            k = PIECE * (s % 8)
                            W.multiply(j * NPC + s, s, k, k == 0, k == KT - PIECE, free=free)
                            if s == 5:
                                pe.wait_ge(e["z_act"], j)
                                pe.wait_ge(e["bd_ready"], j + 1)
                                pe.wait_ge(e["q_ready"], j + 1)
                                for g in range(8):
                                    q = g // 2
                                    ins = T.matmul(TB[32 * q:32 * q + 32, 1024:1024 + P], BD[:, g], Q[:, g, 0:P],
                                                   start=g % 2 == 0, stop=g % 2 == 1)
                                ins.then_inc(e["k_mm"], 1)
                            if s == 7:
                                pe.wait_ge(e["g_ready"], j + 1)
                                pe.wait_ge(e["z_act"], j)
                                pe.wait_ge(e["fin_ev"], j)
                                for i in range(8):
                                    ins = T.transpose(TB[:, i * P:(i + 1) * P], GR[:, i // 4, i % 4].rearrange("p r c -> p (r c)"),
                                                      ident[:])
                                ins.then_inc(e["ls_mm"], 1)
                            if s == 8:
                                pe.wait_ge(e["ls_act"], j + 1)
                                pe.wait_ge(e["ls_dve"], j + 1)
                                pe.wait_ge(e["ga"], 4 * j + 2)
                                pe.wait_ge(e["gd"], j + 1)
                                for r in range(L):
                                    i = L - 1 - r
                                    T.transpose(TB[:, 3 * 512 + r * P:3 * 512 + (r + 1) * P], UZ[:, i:SEQ:L], ident[:])
                                    ins = T.transpose(TB[0:NBS, r * P:(r + 1) * P], UZ[:, SEQ + i:TOK:L], ident[:])
                                ins.then_inc(e["st1_mm"], 1)
                            if s == 9:
                                pe.wait_ge(e["st1_act"], j + 1)
                                pe.wait_ge(e["st1_dve"], j + 1)
                                pe.wait_ge(e["ks_ready"], j + 1)
                                for g in range(8):
                                    T.transpose(TB[:, 1024 + g * P:1024 + (g + 1) * P], UC[:, g * P:(g + 1) * P], ident[:])
                                    ins = T.transpose(TB[:, 4 * 512 + g * NBS:4 * 512 + (g + 1) * NBS],
                                                      UCS[0:NBS, g * P:(g + 1) * P], ident[0:NBS, 0:NBS])
                                ins.then_inc(e["st2_mm"], 1)
                            if s == 10:
                                pe.wait_ge(e["st2_act"], j + 1)
                                pe.wait_ge(e["st2_dve"], j + 1)
                                for i in range(8):
                                    for g in range(2):
                                        c = 512 * (i // 3) + (i % 3) * SC
                                        ins = T.matmul(TB[g * NP:(g + 1) * NP, c:c + SC], LS[:, i, g * NP:(g + 1) * NP],
                                                       Ug[:, 2 * (i % 4) + g], start=True, stop=True)
                                ins.then_inc(e["s_mm"], 1)
                            if s == 13:
                                pe.wait_ge(e["h_dve"], j + 1)
                                pe.wait_ge(e["h_pool"], j + 1)
                                pe.wait_ge(e["mt_in"], P * (j + 1))
                                for g in range(8):
                                    c = 512 * (3, 4, 0)[g // 3] + (g % 3) * SC
                                    T.matmul(TB[:, c:c + SC], MT[:, g], Ug[:, g], start=True, stop=False)
                                    ins = T.matmul(TB[:, c:c + SC], Q[:, g, GC:], H[:, g, 0:SC], start=False, stop=True)
                                ins.then_inc(e["y_mm"], 1)
                            if s == 14:
                                pe.wait_ge(e["y_act"], j + 1)
                                pe.wait_ge(e["y_dve"], j + 1)
                                for g in range(8):
                                    T.transpose(TB[:, 512 + g * P:512 + (g + 1) * P], Y[:, g, 0:NB], ident[:])
                                    ins = T.transpose(TB[0:NBS, 3 * 512 + g * P:3 * 512 + (g + 1) * P], Y[:, g, NB + 1:SC], ident[:])
                                ins.then_inc(e["yt_mm"], 1)
                            if s == 15:
                                pe.wait_ge(e["yt_act"], j + 1)
                                pe.wait_ge(e["yt_dve"], j + 1)
                                for t in range(L):
                                    T.transpose(TB[:, 512 + t * P:512 + (t + 1) * P], UC[:, t * P:(t + 1) * P], ident[:])
                                    ins = T.transpose(TB[:, t * NBS:(t + 1) * NBS], UCS[0:NBS, t * P:(t + 1) * P],
                                                      ident[0:NBS, 0:NBS])
                                ins.then_inc(e["z_mm"], 1)
                                pe.wait_ge(e["fb_ready"], j + 1)
                                T.transpose(TB[0:16, 4 * 512:4 * 512 + P], FB[:], ident[:]).then_inc(e["fin_mm"], 1)

        free_semaphores()

        SQ, SQA = sb("SQ", [P, TOK]), sb("SQA", [P, TOK])
        with ExitStack() as st:
            sbp = pool_of(st)
            QR, KR, VR, ZR = (sbp(n, [P, TOK]) for n in ("QR", "KR", "VR", "ZR"))
            QN, KN = sbp("QN", [P, TOK]), sbp("KN", [P, TOK])
            VT = sbp("VT", [P, TT, P])
            KO = sbp("KO", [P, TT, P])
            NCB = sbp("NCB", [P, CT])
            PR = sbp("PR", [P, SEQ])
            PT = sbp("PT", [P, SEQ])
            CK, CV, KPT = sbp("CK", [PAST, P]), sbp("CV", [PAST, P]), sbp("KPT", [P, PAST])
            qg, tabs = sbp("qg", [P, 1]), sbp("tabs", [P, 1])
            mx, nmx, rsum, rrec = (sbp(n, [P, 1]) for n in ("mx", "nmx", "rsum", "rrec"))
            W = Weights("att", w_in_v, XH, XL)
            NPC = 4 * KT // PIECE
            NR = 9
            names = ("ga", "gd", "sq", "ss_mm", "rt", "qn_r", "qn", "kn", "kpt_mm", "kpt", "s_mm", "nmx", "exp", "pn",
                     "pt_mm", "pt_act", "pt_dve", "o_mm", "y", "v_mm", "v_act", "v_dve", "k_mm", "k_act", "k_dve",
                     "in", "zhi", "zlo", "zs_in", "sig", "y1", "yg", "sqg", "sqs", "ys_out", "k_out", "v_out", "y_out", "ysq", "sqa", "init", "qg")
            e = {n: sem("att_" + n) for n in names}
            KG = D_SSM // P
            GP = KG // PIECE
            ZH, ZL = XH[:, 0:KG], XH[:, KG:2 * KG]
            stage = (QR, KR)
            SG, QG, ZG, ZS = QR, KR, VR, KO[:].rearrange("p m d -> p (m d)")[:, 0:TOK]
            SQS = SQ
            zin = (sem("att_zin0"), sem("att_zin1"))
            ROWS = (0, 1, 2, 8, 3, 4, 5, 6, 7)
            S_AT = (0, 3, 5, 7, 10, 13, 16, 21, 24)
            T_AT = (2, 4, 6, 8, 12, 15, 18, 23, 26)
            O_AT = (3, 5, 7, 9, 13, 16, 19, 24, 27)
            KPT_AT = 5
            SQ_AT = {8: (0, QR), 19: (1, KR)}
            SS_AT = {9: (0, 4), 20: (1, 7)}
            RT_AT = {9: 0, 20: 1}
            REC = 8
            REC_AT = ((11, 12, 13, 14, 15, 16, 17, 18), (22, 22, 23, 23, 25, 25, 26, 26))
            QN_AT, KN_AT, YSQ_AT, KT_AT, VT_AT = 18, 27, 29, 29, 31
            RW = TOK // REC

            def keys(i):
                return (P * (i + 1), P) if i < NR - 1 else (PAST + DEC, DEC)

            def row_at(s, at):
                return ROWS[at.index(s)], at.index(s)

            with nc.Block() as block:
                @block.sync
                def _(sp):
                    with sp.Fori(0, NH) as h:
                        for s in range(NPC):
                            col = h * P + 2 * D_SSM + D_ATT * (s // 8)
                            W.load(sp, h * NPC + s, s, col, PIECE * (s % 8))

                    def glu_piece(s):
                        W.load(sp, NH * NPC + s, s, s // GP * P, PIECE * (s % GP), w_glu_v)
                    for s in range(RAW):
                        glu_piece(s)
                    sp.wait_ge(e["qn"], NH)
                    sp.wait_ge(e["kn"], NH)
                    for k in range(KG):
                        if k >= 2:
                            sp.wait_ge(e["zlo"], k - 1)
                        sp.dma_start(stage[k % 2][:], zg_s[k * P:(k + 1) * P, :]).then_inc(zin[k % 2], 16)
                    for s in range(RAW, NPC):
                        glu_piece(s)

                @block.gpsimd
                def _(pool):
                    G.memset(SQA[:], 0.0).then_inc(e["init"], 1)
                    pool.wait_ge(e["init"], 1)

                    def part(h, gemm, att, ha):
                        if att:
                            pool.wait_ge(e["y"], NR * (ha + 1))
                            stand(pool, "pool")
                            pool.dma_start(ya_s[ds(ha * P, P), :], ZR[:]).then_inc(e["y_out"], 16)
                            pool.wait_ge(e["ysq"], ha + 1)
                            G.tensor_tensor(SQA[:], SQA[:], (SQ if gemm else QG)[:], ALU.add).then_inc(e["sqa"], 1)
                            pool.wait_ge(e["sqa"], ha + 1)
                        if gemm:
                            pool.wait_ge(e["qn_r"], h + 1)
                            if att:
                                pool.wait_ge(e["s_mm"], NR * (ha + 1))
                            stand(pool, "pool")
                            G.tensor_copy(QN[:], QR[:]).then_inc(e["qn"], 1)
                            if att:
                                pool.wait_ge(e["o_mm"], NR * (ha + 1))
                                pool.wait_ge(e["nmx"], NR * (ha + 1))
                            stand(pool, "pool")
                            for dst, src in ((CK[:], cache_k[0, 0]), (CV[:], cache_v[0, 0])):
                                pool.dma_start(dst, src.rearrange("t h d -> t (h d)")[:, ds(h * P, P)]).then_inc(e["in"], 16)
                            pool.dma_start(NCB[:], nc_s[ds(h, 1), :].to_broadcast([P, CT])).then_inc(e["in"], 16)
                            for n, src, po, so in (("v", VT, v_prompt, v_sample), ("k", KO, k_prompt, k_sample)):
                                pool.wait_ge(e[n + "_act"], h + 1)
                                pool.wait_ge(e[n + "_dve"], h + 1)
                                stand(pool, "pool")
                                pool.dma_start(po[0, 0].rearrange("(m p) h d -> p m (h d)", p=P)[:, :, ds(h * P, P)],
                                               src[:, 0:TT - 1]).then_inc(e[n + "_out"], 16)
                                pool.dma_start(so[0, 0].rearrange("p h d -> p (h d)")[:, ds(h * P, P)],
                                               src[0:DEC, TT - 1]).then_inc(e[n + "_out"], 16)
                    part(0, True, False, None)
                    with pool.Fori(1, NH) as h:
                        part(h, True, True, h - 1)

                    def finish_glu(n):
                        pool.wait_ge(e["yg"], n + 1)
                        pool.dma_start(ys_s[n * P:(n + 1) * P, :], SG[:]).then_inc(e["ys_out"], 16)
                        pool.wait_ge(e["sqg"], n + 1)
                        if n:
                            G.tensor_tensor(SQS[:], SQS[:], QG[:], ALU.add).then_inc(e["sqs"], 1)
                        else:
                            G.tensor_copy(SQS[:], QG[:]).then_inc(e["sqs"], 1)
                        pool.wait_ge(e["sqs"], n + 1)
                    for n in range(KG):
                        if n == 0:
                            pool.wait_ge(e["v_mm"], NH)
                            pool.wait_ge(e["k_out"], 32 * NH)
                        else:
                            pool.wait_ge(e["yg"], n)
                        pool.dma_start(ZG[:], zg_s[n * P:(n + 1) * P, :]).then_inc(e["zs_in"], 16)
                        pool.dma_start(ZS, zs_s[n * P:(n + 1) * P, :]).then_inc(e["zs_in"], 16)
                        if n:
                            finish_glu(n - 1)
                    part(None, False, True, NH - 1)
                    finish_glu(KG - 1)
                    pool.wait_ge(e["k_out"], 32 * NH)
                    pool.wait_ge(e["v_out"], 32 * NH)

                @block.scalar
                def _(act):
                    for s in range(SPL):
                        W.split_hi(s, s, 1)
                    o = Order(act, "act_tables")

                    def table(func):
                        o.then(S.activation(tabs[:], epsc[:], func))

                    def square_glu(n):
                        act.wait_ge(e["yg"], n + 1)
                        if n:
                            act.wait_ge(e["sqs"], n)
                        if n == KG - 1:
                            act.wait_ge(e["sqa"], NH)
                        S.activation(QG[:], SG[:], ACT.Square).then_inc(e["sqg"], 1)

                    def part(h, gemm, att, ha):
                        for s in range(NPC):
                            if not gemm and s % GP == GP - 1:
                                n = s // GP
                                act.wait_ge(W.mm, W.multiplied(NH * NPC + s))
                                if n:
                                    act.wait_ge(e["ys_out"], 16 * n)
                                else:
                                    act.wait_ge(e["zlo"], KG)
                                for src, dst in halves(GB, SG):
                                    S.activation(dst, src, ACT.Sigmoid, bias=vec[:, 8 + n:9 + n]).then_inc(e["sig"], 1)
                                table(ACT.Exp)
                            if gemm and s in (7, 15, 23):
                                act.wait_ge(W.mm, W.multiplied(h * NPC + s))
                                raw = {7: QR, 15: KR, 23: VR}[s]
                                if s == 7 and att:
                                    act.wait_ge(e["qn"], h)
                                S.copy(cols(raw, 0), group(GB, 0)).then_inc(e["ga"], 1)
                                S.copy(cols(raw, 2), group(GB, 2)).then_inc(e["ga"], 1)
                            if gemm and s == NPC - 1:
                                act.wait_ge(W.mm, W.multiplied(h * NPC + s))
                                if att:
                                    act.wait_ge(e["y_out"], 16 * h)
                                for src, dst in halves(GB, ZR):
                                    S.activation(dst, src, ACT.Silu).then_inc(e["ga"], 1)
                            if gemm:
                                m = s + SPL
                                W.split_hi(h * NPC + m, m, h * (NPC // RAW) + m // RAW + 1)
                            elif s + SPL < NPC:
                                m = NH * NPC + s + SPL
                                W.split_hi(m, m, m // RAW + 1)
                            if gemm and s in RT_AT:
                                w = RT_AT[s]
                                table(ACT.Sqrt)
                                act.wait_ge(e["ss_mm"], 2 * h + w + 1)
                                S.activation(SQ[:, 0:SEQ], TB[:, 0:SEQ], ACT.Sqrt, bias=epsc[:], scale=1.0 / HD)
                                S.activation(SQ[:, SEQ:TOK], TB[:, 4 * 512 + P:4 * 512 + P + DEC], ACT.Sqrt, bias=epsc[:],
                                             scale=1.0 / HD).then_inc(e["rt"], 1)
                                table(ACT.Exp)
                            if att and s in S_AT:
                                i, p = row_at(s, S_AT)
                                w, n = keys(i)
                                act.wait_ge(e["nmx"], NR * ha + p + 1)
                                S.activation(PR[0:n, 0:w], PR[0:n, 0:w], ACT.Exp, bias=nmx[0:n],
                                             accum_out=rsum[0:n]).then_inc(e["exp"], 1)
                            if att and s == KPT_AT:
                                act.wait_ge(e["kpt_mm"], ha + 1)
                                S.copy(KPT[:], TB[:, 1024:1024 + PAST]).then_inc(e["kpt"], 1)
                            if att and s in T_AT:
                                i, p = row_at(s, T_AT)
                                act.wait_ge(e["pt_mm"], NR * ha + p + 1)
                                if i < NR - 1:
                                    b = min(i + 1, 4) * P
                                    S.copy(PT[:, 0:b], TB[:, 1024:1024 + b]).then_inc(e["pt_act"], 1)
                                else:
                                    S.copy(PT[:, 0:DEC], TB[:, 1024:1024 + DEC])
                                    S.copy(PT[0:DEC, P:P + DEC], TB[0:DEC, 1024 + P:1024 + P + DEC]).then_inc(e["pt_act"], 1)
                            if gemm and s in SQ_AT:
                                w, raw = SQ_AT[s]
                                act.wait_ge(e["ga"], 8 * h + 2 * w + 2)
                                act.wait_ge(e["gd"], 3 * h + w + 1)
                                if w:
                                    act.wait_ge(e["qn_r"], h + 1)
                                elif att:
                                    act.wait_ge(e["kn"], h)
                                    act.wait_ge(e["sqa"], ha)
                                S.activation(SQ[:], raw[:], ACT.Square).then_inc(e["sq"], 1)
                            if att and s == YSQ_AT:
                                act.wait_ge(e["y"], NR * (ha + 1))
                                if gemm:
                                    act.wait_ge(e["kn"], h + 1)
                                else:
                                    act.wait_ge(e["sqs"], KG - 1)
                                S.activation((SQ if gemm else QG)[:], ZR[:], ACT.Square).then_inc(e["ysq"], 1)
                            if gemm and s == KT_AT:
                                act.wait_ge(e["k_mm"], h + 1)
                                act.wait_ge(e["k_out"], 32 * h)
                                S.copy(KO[:, 0:4], TB[:, 0:512].rearrange("p (m d) -> p m d", m=4))
                                S.copy(KO[0:DEC, TT - 1], TB[0:DEC, 4 * 512:4 * 512 + P]).then_inc(e["k_act"], 1)
                            if not gemm and s % GP == GP - 2:
                                table(ACT.Sigmoid)
                            if not gemm and s % GP == 0 and s:
                                square_glu(s // GP - 1)
                            if gemm and s == NPC - 2:
                                table(ACT.Silu)
                            if gemm and s == VT_AT:
                                act.wait_ge(e["v_mm"], h + 1)
                                act.wait_ge(e["v_out"], 32 * h)
                                S.copy(VT[:, 0:4], TB[:, 1024:1536].rearrange("p (m d) -> p m d", m=4))
                                S.copy(VT[0:DEC, TT - 1], TB[0:DEC, 4 * 512:4 * 512 + P]).then_inc(e["v_act"], 1)
                                table(ACT.Exp)
                    part(0, True, False, None)
                    with act.Fori(1, NH) as h:
                        o.enter(h - 1, 6)
                        part(h, True, True, h - 1)
                    o.leave(NH - 1)
                    for k in range(KG):
                        act.wait_ge(zin[k % 2], 16 * (k // 2 + 1))
                        if k == 0:
                            act.wait_ge(W.mm, W.multiplied(NH * NPC - 1))
                        S.copy(ZH[:, k], stage[k % 2][:]).then_inc(e["zhi"], 1)
                    part(None, False, True, NH - 1)
                    square_glu(KG - 1)

                @block.vector
                def _(dve):
                    V.tensor_scalar(qg[:], vec[:, 32:33], HD ** -0.5, None, ALU.mult).then_inc(e["qg"], 1)
                    dve.sem_inc(W.lo, RAW)
                    dve.wait_ge(e["qg"], 1)
                    for s in range(SPL):
                        W.split_lo(s, s)
                    o = Order(dve, "dve_att")

                    def gate_glu(n):
                        dve.wait_ge(e["sig"], 2 * n + 2)
                        dve.wait_ge(e["zs_in"], 32 * (n + 1))
                        V.tensor_tensor(SG[:], SG[:], ZG[:], ALU.mult).then_inc(e["y1"], 1)
                        dve.wait_ge(e["y1"], n + 1)
                        V.tensor_tensor(SG[:], SG[:], ZS, ALU.mult).then_inc(e["yg"], 1)

                    def part(h, gemm, att, ha):
                        for s in range(NPC):
                            if gemm and s in (7, 15, 23):
                                dve.wait_ge(W.mm, W.multiplied(h * NPC + s))
                                raw = {7: QR, 15: KR, 23: VR}[s]
                                if s == 7 and att:
                                    dve.wait_ge(e["qn"], h)
                                V.tensor_copy(cols(raw, 1), group(GB, 1)).then_inc(e["gd"], 1)
                            if gemm:
                                m = s + SPL
                                W.split_lo(h * NPC + m, m)
                            elif s + SPL < NPC:
                                W.split_lo(NH * NPC + s + SPL, s + SPL)
                            if not gemm and s % GP == 0 and s:
                                gate_glu(s // GP - 1)
                            if att and s in O_AT:
                                i, p = row_at(s, O_AT)
                                n = keys(i)[1]
                                dve.wait_ge(e["o_mm"], NR * ha + p + 1)
                                V.tensor_tensor(ZR[:, i * P:i * P + n], TB[:, 4 * 512:4 * 512 + n], ZR[:, i * P:i * P + n],
                                                ALU.mult).then_inc(e["y"], 1)
                            if att and s in S_AT:
                                i, p = row_at(s, S_AT)
                                w, n = keys(i)
                                c = 0 if i < NR - 1 else SEQ
                                if p == 0:
                                    dve.wait_ge(e["in"], 48 * (ha + 1))
                                dve.wait_ge(e["s_mm"], NR * ha + p + 1)
                                stand(dve, "dve")
                                o.then(V.tensor_tensor_reduce(out=PR[0:n, 0:w], in0=TB[0:n, 0:w], in1=NCB[0:n, c:c + w], scale=1.0,
                                                              scalar=-3e38, op0=ALU.add, op1=ALU.max, accum_out=mx[0:n]))
                                V.tensor_scalar(nmx[0:n], mx[0:n], -1.0, None, ALU.mult).then_inc(e["nmx"], 1)
                                dve.wait_ge(e["exp"], NR * ha + p + 1)
                                o.then(V.reciprocal(rrec[0:n], rsum[0:n]))
                                V.tensor_scalar(PR[0:n, 0:w], PR[0:n, 0:w], rrec[0:n], None, ALU.mult).then_inc(e["pn"], 1)
                            if att and s in T_AT and 4 <= row_at(s, T_AT)[0] < NR - 1:
                                i, p = row_at(s, T_AT)
                                dve.wait_ge(e["pt_mm"], NR * ha + p + 1)
                                V.tensor_copy(PT[:, 512:P * (i + 1)], TB[:, 1536:1024 + P * (i + 1)]).then_inc(e["pt_dve"], 1)
                            for w in range(2):
                                for x, at in enumerate(REC_AT[w]):
                                    if gemm and at == s:
                                        if x == 0:
                                            dve.wait_ge(e["rt"], 2 * h + w + 1)
                                        a = SQ[:, RW * x:RW * (x + 1)]
                                        o.then(V.reciprocal(a, a))
                            if gemm and s == QN_AT:
                                V.scalar_tensor_tensor(QR[:], QR[:], qg[:], SQ[:], ALU.mult, ALU.mult).then_inc(e["qn_r"], 1)
                            if gemm and s == KN_AT:
                                V.scalar_tensor_tensor(KN[:], KR[:], vec[:, 33:34], SQ[:], ALU.mult, ALU.mult).then_inc(e["kn"], 1)
                            if gemm and s == KT_AT:
                                dve.wait_ge(e["k_mm"], h + 1)
                                dve.wait_ge(e["k_out"], 32 * h)
                                V.tensor_copy(KO[:, 4:8], TB[:, 512:1024].rearrange("p (m d) -> p m d", m=4)).then_inc(e["k_dve"], 1)
                            if gemm and s == VT_AT:
                                dve.wait_ge(e["v_mm"], h + 1)
                                dve.wait_ge(e["v_out"], 32 * h)
                                V.tensor_copy(VT[:, 4:8], TB[:, 1536:2048].rearrange("p (m d) -> p m d", m=4)).then_inc(e["v_dve"], 1)
                    part(0, True, False, None)
                    with dve.Fori(1, NH) as h:
                        o.enter(h - 1, 2 * NR + 2 * REC)
                        part(h, True, True, h - 1)
                    o.leave(NH - 1)
                    for k in range(KG):
                        dve.wait_ge(e["zhi"], k + 1)
                        V.tensor_tensor(ZL[:, k], stage[k % 2][:], ZH[:, k].bitcast(f32), ALU.subtract).then_inc(e["zlo"], 1)
                    part(None, False, True, NH - 1)
                    gate_glu(KG - 1)

                @block.tensor
                def _(pe):
                    W.credit("pe")

                    def part(h, gemm, att, ha):
                        for s in range(NPC):
                            if gemm:
                                def free(b):
                                    if b == 1 and s:
                                        pe.wait_ge(e["gd"], 3 * h + s // 8)
                                    elif b == 2 or s:
                                        pe.wait_ge(e["ga"], 8 * h + s // 4 - (b == 0))
                                    elif b == 0:
                                        if att:
                                            pe.wait_ge(e["ga"], 8 * h - 1)
                                k = PIECE * (s % 8)
                                W.multiply(h * NPC + s, s, k, k == 0, k == KT - PIECE, free=free if k == 0 else None)
                            else:
                                def free(b):
                                    if s == 0:
                                        pe.wait_ge(e["ga"], 8 * NH)
                                    elif b != 1:
                                        pe.wait_ge(e["sig"], s // GP * 2 - (b == 0))
                                if s < GP:
                                    pe.wait_ge(e["zlo"], PIECE * (s + 1))
                                W.multiply(NH * NPC + s, s, PIECE * (s % GP), s % GP == 0, s % GP == GP - 1, ZH, ZL,
                                           free=free if s % GP == 0 else None)
                            if gemm and s - 1 in RT_AT:
                                pe.wait_ge(e["rt"], 2 * h + RT_AT[s - 1] + 1)
                            if att and s in O_AT:
                                i, p = row_at(s, O_AT)
                                w, n = keys(i)
                                pe.wait_ge(e["pt_act"], NR * ha + p + 1)
                                if 4 <= i < NR - 1:
                                    pe.wait_ge(e["pt_dve"], 4 * ha + i - 3)
                                if p:
                                    pe.wait_ge(e["y"], NR * ha + p)
                                O = TB[:, 4 * 512:4 * 512 + n]
                                if i < NR - 1:
                                    for b in range(i + 1):
                                        ins = T.matmul(O, VT[:, b], PT[:, b * P:(b + 1) * P], start=b == 0, stop=b == i)
                                else:
                                    T.matmul(O, CV[:], PT[:, 0:DEC], start=True, stop=False)
                                    ins = T.matmul(O, VT[0:DEC, TT - 1], PT[0:DEC, P:P + DEC], start=False, stop=True)
                                ins.then_inc(e["o_mm"], 1)
                            if att and s in S_AT:
                                i, p = row_at(s, S_AT)
                                w, n = keys(i)
                                if p == 0:
                                    pe.wait_ge(e["qn"], ha + 1)
                                    pe.wait_ge(e["kn"], ha + 1)
                                    pe.wait_ge(e["k_act"], ha + 1)
                                    pe.wait_ge(e["k_dve"], ha + 1)
                                    pe.wait_ge(e["v_act"], ha + 1)
                                    pe.wait_ge(e["v_dve"], ha + 1)
                                else:
                                    pe.wait_ge(e["nmx"], NR * ha + p)
                                if i < NR - 1:
                                    q = QN[:, i * P:(i + 1) * P]
                                    for c in range(0, w, 512):
                                        cw = min(512, w - c)
                                        T.matmul(TB[:, c:c + cw], q, KN[:, c:c + cw], start=True, stop=c + cw < w)
                                    ins = T.matmul(TB[:, w - P:w], identb[:], maskb[:], start=False, stop=True)
                                else:
                                    pe.wait_ge(e["kpt"], ha + 1)
                                    q = QN[:, SEQ:TOK]
                                    T.matmul(TB[0:DEC, 0:PAST], q, KPT[:], start=True, stop=True)
                                    T.matmul(TB[0:DEC, PAST:w], q, KN[:, SEQ:TOK], start=True, stop=False)
                                    ins = T.matmul(TB[0:DEC, PAST:w], identb[0:DEC, 0:DEC], maskb[0:DEC, 0:DEC],
                                                   start=False, stop=True)
                                ins.then_inc(e["s_mm"], 1)
                            if att and s == KPT_AT:
                                pe.wait_ge(e["in"], 48 * (ha + 1))
                                pe.wait_ge(e["pt_act"], NR * ha + sum(t < s for t in T_AT))
                                T.transpose(TB[:, 1024:1024 + PAST], CK[:], ident[:]).then_inc(e["kpt_mm"], 1)
                            if att and s in T_AT:
                                i, p = row_at(s, T_AT)
                                w, n = keys(i)
                                pe.wait_ge(e["pn"], NR * ha + p + 1)
                                if s > KPT_AT:
                                    pe.wait_ge(e["kpt"], ha + 1)
                                if p:
                                    pe.wait_ge(e["pt_act"], NR * ha + p)
                                if i < NR - 1:
                                    for b in range(i + 1):
                                        ins = T.transpose(TB[:, 1024 + b * P:1024 + (b + 1) * P], PR[:, b * P:(b + 1) * P], ident[:])
                                else:
                                    stand(pe, "pe")
                                    T.transpose(TB[:, 1024:1024 + DEC], PR[0:DEC, 0:PAST], ident[0:DEC, 0:DEC])
                                    ins = T.transpose(TB[0:DEC, 1024 + P:1024 + P + DEC], PR[0:DEC, PAST:w], ident[0:DEC, 0:DEC])
                                ins.then_inc(e["pt_mm"], 1)
                            if gemm and s in SS_AT:
                                w, p = SS_AT[s]
                                pe.wait_ge(e["sq"], 2 * h + w + 1)
                                if att:
                                    pe.wait_ge(e["nmx"], NR * ha + p)
                                    pe.wait_ge(e["y"], NR * ha + p)
                                for c, d, n in ((0, 0, 512), (512, 512, 512), (SEQ, 4 * 512 + P, DEC)):
                                    ins = T.matmul(TB[:, d:d + n], ones[:], SQ[:, c:c + n], start=True, stop=True)
                                ins.then_inc(e["ss_mm"], 1)
                            if gemm and s in (KT_AT, VT_AT):
                                src, base, name = (KN, 0, "k") if s == KT_AT else (VR, 1024, "v")
                                if s == KT_AT:
                                    pe.wait_ge(e["kn"], h + 1)
                                    if att:
                                        pe.wait_ge(e["y"], NR * (ha + 1))
                                else:
                                    pe.wait_ge(e["ga"], 8 * h + 6)
                                    pe.wait_ge(e["gd"], 3 * h + 3)
                                    pe.wait_ge(e["k_act"], h + 1)
                                for m in range(TT):
                                    n = min(P, TOK - m * P)
                                    d = base + m * P if m < TT - 1 else 4 * 512
                                    ins = T.transpose(TB[0:n, d:d + P], src[:, m * P:m * P + n], ident[:])
                                ins.then_inc(e[name + "_mm"], 1)
                    part(0, True, False, None)
                    with pe.Fori(1, NH) as h:
                        part(h, True, True, h - 1)
                    part(None, False, True, NH - 1)

        with ExitStack() as st:
            sbp = pool_of(st)
            YH, YL = XH, XL
            RB = (SQS, SQA)
            yf = sbp("yf", [P, YB, TOK])
            rm = sbp("rm", [P, 4, 2, TT])
            OT = sbp("OT", [P, 2, TOK])
            XO = sbp("XO", [P, 2, TT, P])
            DG = OT
            done_y, done_ys = e["y_out"], e["ys_out"]
            W = Weights("out", w_out_v, YH, YL)
            NPC = KT // PIECE
            NCH = D_MODEL // P
            names = ("ss", "ms", "rt", "dg", "bc_mm", "bc", "sc_dve", "sc_pool", "yhi", "ylo", "ga", "gd", "t_mm", "add", "x_in0", "x_in1", "o_out0", "o_out1")
            e = {n: sem("out_" + n) for n in names}
            yin = [sem(f"out_yin{x}") for x in range(YB)]

            def kt(x):
                return (x + KG) % KT

            def scale(x, eng, wait):
                wait.wait_ge(yin[x % YB], 16 * (x // YB + 1))
                return eng.tensor_tensor(yf[:, x % YB], yf[:, x % YB], RB[x < KG][:], ALU.mult)

            with nc.Block() as block:
                @block.sync
                def _(sp):
                    sp.wait_ge(done_y, 16 * NH)
                    for x in range(KT):
                        if x < RAW:
                            W.load(sp, x, x, 0, kt(PIECE * x))
                        if x == RAW:
                            for m in range(RAW, NPC):
                                W.load(sp, m, m, 0, kt(PIECE * m))
                        if x == KG:
                            sp.wait_ge(done_ys, 16 * KG)
                        if x >= YB:
                            sp.wait_ge(e["ylo"], x - YB + 1)
                        src = (ya_s if x < KG else ys_s)[(x % KG) * P:(x % KG + 1) * P, :]
                        sp.dma_start(yf[:, x % YB], src).then_inc(yin[x % YB], 16)
                    with sp.Fori(1, D_MODEL // P) as n:
                        for s in range(NPC):
                            W.load(sp, n * NPC + s, s, n * P, kt(PIECE * s), apart=kt(PIECE * s) == 0)
                    for s in range(SPL):
                        W.load(sp, (D_MODEL // P) * NPC + s, s, 0, 0)

                @block.gpsimd
                def _(pool):
                    def residual(n, b, first, turn):
                        if not first:
                            pool.wait_ge(e[f"o_out{b}"], 32 * turn)
                            stand(pool, "pool")
                        pool.dma_start(XO[:, b, 0:TT - 1], x_prompt[0].rearrange("(m p) n -> p m n", p=P)[:, :, ds(n * P, P)]
                                       ).then_inc(e[f"x_in{b}"], 16)
                        pool.dma_start(XO[0:DEC, b, TT - 1], x_sample[0][:, ds(n * P, P)]).then_inc(e[f"x_in{b}"], 16)

                    def store(n, b):
                        pool.wait_ge(e["add"], 2 * n + 2)
                        stand(pool, "pool")
                        pool.dma_start(y_prompt[0].rearrange("(m p) n -> p m n", p=P)[:, :, ds(n * P, P)], XO[:, b, 0:TT - 1]
                                       ).then_inc(e[f"o_out{b}"], 16)
                        pool.dma_start(y_sample[0][:, ds(n * P, P)], XO[0:DEC, b, TT - 1]).then_inc(e[f"o_out{b}"], 16)
                    residual(0, 0, True, 0)
                    residual(1, 1, True, 0)
                    pool.wait_ge(e["bc"], 3)
                    for x in range(1, KT, 2):
                        if x > KG:
                            pool.wait_ge(e["bc"], 6)
                        scale(x, G, pool).then_inc(e["sc_pool"], 1)
                    with pool.Fori(0, NCH // 2 - 1) as i:
                        for b in range(2):
                            store(2 * i + b, b)
                            residual(2 * i + b + 2, b, False, i + 1)
                    for b in range(2):
                        store(NCH - 2 + b, b)
                    for b in range(2):
                        pool.wait_ge(e[f"o_out{b}"], 32 * (NCH // 2))

                @block.scalar
                def _(act):
                    act.wait_ge(e["ms"], 1)
                    S.activation(rm[:, 1, :, 0:TT - 1], rm[:, 0, :, 0:TT - 1], ACT.Sqrt)
                    S.activation(rm[0:DEC, 1, :, TT - 1], rm[0:DEC, 0, :, TT - 1], ACT.Sqrt).then_inc(e["rt"], 1)
                    for s in range(SPL):
                        W.split_hi(s, s, 1)
                    for w in (1, 0):
                        act.wait_ge(e["bc_mm"], 2 - w)
                        for b in range(3):
                            S.copy(cols(RB[w], b), group((GB, TB)[w], b)).then_inc(e["bc"], 1)
                    for x in range(KT):
                        act.wait_ge(e["sc_pool" if x % 2 else "sc_dve"], x // 2 + 1)
                        S.activation(YH[:, kt(x)], yf[:, x % YB], ACT.Copy, scale=vec[:, 16 + kt(x):17 + kt(x)]
                                     ).then_inc(e["yhi"], 1)
                        if x % PIECE == 1 and x // PIECE >= 3:
                            m = SPL + x // PIECE - 3
                            W.split_hi(m, m, m // RAW + 1)

                    def chunk(n, b):
                        for s in range(NPC):
                            if s == NPC - 1:
                                act.wait_ge(W.mm, W.multiplied(n * NPC + s))
                                if not isinstance(n, int):
                                    act.wait_ge(e["t_mm"], n - 1)
                                S.copy(cols(OT[:, b], 0), group(GB, 0)).then_inc(e["ga"], 1)
                                S.copy(cols(OT[:, b], 2), group(GB, 2)).then_inc(e["ga"], 1)
                            m = s + SPL
                            if not isinstance(n, int) or n or s >= NPC - 3:
                                W.split_hi(n * NPC + m, m, n * (NPC // RAW) + m // RAW + 1)
                    chunk(0, 0)
                    chunk(1, 1)
                    with act.Fori(1, NCH // 2) as i:
                        chunk(2 * i, 0)
                        chunk(2 * i + 1, 1)

                @block.vector
                def _(dve):
                    dve.sem_inc(W.lo, RAW)
                    o = Order(dve, "out_dve")
                    dve.wait_ge(e["ss"], 1)
                    sums = TB[:, 2048:2048 + 2 * TT].rearrange("p (w m) -> p w m", w=2)
                    tiles = ((slice(0, P), slice(0, TT - 1)), (slice(0, DEC), slice(TT - 1, TT)))
                    ms, rt, rr, tmp = (lambda p, m, i=i: rm[p, i, :, m] for i in range(4))
                    for p, m in tiles:
                        ins = V.tensor_scalar(ms(p, m), sums[p, :, m], 1.0 / D_SSM, EPS, ALU.mult, ALU.add)
                    ins.then_inc(e["ms"], 1)
                    dve.wait_ge(e["rt"], 1)
                    for p, m in tiles:
                        o.then(V.reciprocal(rr(p, m), rt(p, m)))
                        o.then(V.tensor_tensor(tmp(p, m), rr(p, m), rr(p, m), ALU.mult))
                        o.then(V.scalar_tensor_tensor(tmp(p, m), tmp(p, m), -0.5, ms(p, m), ALU.mult, ALU.mult))
                        o.then(V.scalar_tensor_tensor(rr(p, m), tmp(p, m), 1.5, rr(p, m), ALU.add, ALU.mult))
                    for w in (1, 0):
                        V.tensor_tensor(DG[:, w, 0:SEQ].rearrange("p (m t) -> p m t", t=P),
                                        ident[:].unsqueeze(1).to_broadcast([P, TT - 1, P]),
                                        rm[:, 2, w, 0:TT - 1].unsqueeze(2).to_broadcast([P, TT - 1, P]), ALU.mult)
                        V.tensor_scalar(DG[0:DEC, w, SEQ:], ident[0:DEC, 0:DEC], rm[0:DEC, 2, w, TT - 1:TT], None, ALU.mult
                                        ).then_inc(e["dg"], 1)
                    for s in range(SPL):
                        W.split_lo(s, s)

                    def scale_dve(x):
                        dve.wait_ge(e["bc"], 3 if x < KG else 6)
                        scale(x, V, dve).then_inc(e["sc_dve"], 1)
                    scale_dve(0)
                    for x in range(KT):
                        if x % 2 and x + 1 < KT:
                            scale_dve(x + 1)
                        dve.wait_ge(e["yhi"], x + 1)
                        V.scalar_tensor_tensor(YL[:, kt(x)], yf[:, x % YB], vec[:, 16 + kt(x):17 + kt(x)],
                                               YH[:, kt(x)].bitcast(f32), ALU.mult, ALU.subtract).then_inc(e["ylo"], 1)
                        if x % PIECE == 1 and x // PIECE >= 3:
                            m = SPL + x // PIECE - 3
                            W.split_lo(m, m)

                    def part(n, gemm, tr, b, turn):
                        for s in range(NPC):
                            if gemm and s == NPC - 1:
                                dve.wait_ge(W.mm, W.multiplied(n * NPC + s))
                                if not isinstance(n, int):
                                    dve.wait_ge(e["t_mm"], n - 1)
                                V.tensor_copy(cols(OT[:, 1 - b], 1), group(GB, 1)).then_inc(e["gd"], 1)
                            if gemm:
                                m = s + SPL
                                if not isinstance(n, int) or n or s >= NPC - 3:
                                    W.split_lo(n * NPC + m, m)
                            if tr and s == NPC - 1:
                                dve.wait_ge(e["t_mm"], n)
                                dve.wait_ge(e[f"x_in{b}"], 32 * turn)
                                V.tensor_tensor(XO[:, b, 0:TT - 1], XO[:, b, 0:TT - 1],
                                                TB[:, 0:SEQ].rearrange("p (m n) -> p m n", n=P), ALU.add).then_inc(e["add"], 1)
                                V.tensor_tensor(XO[0:DEC, b, TT - 1], XO[0:DEC, b, TT - 1], TB[0:DEC, SEQ:SEQ + P],
                                                ALU.add).then_inc(e["add"], 1)
                    part(0, True, False, 1, 0)
                    part(1, True, True, 0, 1)
                    with dve.Fori(0, NCH // 2 - 1) as i:
                        part(2 * i + 2, True, True, 1, i + 1)
                        part(2 * i + 3, True, True, 0, i + 2)
                    part(NCH, False, True, 1, NCH // 2)

                @block.tensor
                def _(pe):
                    W.credit("pe")
                    for m in range(TT):
                        w = min(P, TOK - m * P)
                        for x in range(2):
                            ins = T.matmul(TB[0:w, 2048 + TT * x + m:2049 + TT * x + m], RB[x][:, m * P:m * P + w], ones[:, 0:1],
                                           start=True, stop=True)
                    ins.then_inc(e["ss"], 1)
                    for x in (1, 0):
                        pe.wait_ge(e["dg"], 2 - x)
                        for b, (c, n) in enumerate(COLS):
                            full = min(n, SEQ - c)
                            ins = T.matmul((GB, TB)[x][:, 512 * b:512 * b + full], ones[:], DG[:, x, c:c + full], start=True, stop=True)
                            if full < n:
                                ins = T.matmul((GB, TB)[x][:, 512 * b + full:512 * b + n], ones[0:DEC], DG[0:DEC, x, SEQ:],
                                               start=True, stop=True)
                        ins.then_inc(e["bc_mm"], 1)

                    def chunk(n, first):
                        for s in range(NPC):
                            def free(b):
                                if first:
                                    if b == 0:
                                        pe.wait_ge(e["bc"], 6)
                                elif b == 1:
                                    pe.wait_ge(e["gd"], n)
                                else:
                                    pe.wait_ge(e["ga"], 2 * n - (b == 0))
                            if first:
                                pe.wait_ge(e["ylo"], PIECE * (s + 1))
                            W.multiply(n * NPC + s, s, kt(PIECE * s), s == 0, s == NPC - 1, free=free if s == 0 else None)

                    def transposes(n, b):
                        pe.wait_ge(e["ga"], 2 * n + 2)
                        pe.wait_ge(e["gd"], n + 1)
                        if not isinstance(n, int) or n:
                            pe.wait_ge(e["add"], 2 * n)
                        for m in range(TT):
                            w = min(P, TOK - m * P)
                            ins = T.transpose(TB[0:w, m * P:(m + 1) * P], OT[:, b, m * P:m * P + w], ident[:])
                        ins.then_inc(e["t_mm"], 1)
                    chunk(0, True)
                    with pe.Fori(0, NCH // 2 - 1) as i:
                        chunk(2 * i + 1, False)
                        transposes(2 * i, 0)
                        chunk(2 * i + 2, False)
                        transposes(2 * i + 1, 1)
                    chunk(NCH - 1, False)
                    transposes(NCH - 2, 0)
                    transposes(NCH - 1, 1)


_INS = ["x_prompt", "x_sample", "cache_k", "cache_v", "cache_logf", "state_ssm_re", "state_ssm_im",
        "norm_gain", "w_in", "b_f", "q_norm_gain", "k_norm_gain", "ssm_log_dt", "ssm_a_re", "ssm_a_im",
        "ssm_b_re", "ssm_b_im", "ssm_c_re", "ssm_c_im", "ssm_d", "w_glu", "b_glu",
        "ssm_out_norm", "att_out_norm", "w_out"]
_OUTS = [("y_prompt", (1, SEQ, D_MODEL)), ("y_sample", (1, DEC, D_MODEL)),
         ("k_prompt", (1, 1, SEQ, NH, HD)), ("v_prompt", (1, 1, SEQ, NH, HD)), ("logf_prompt", (1, 1, SEQ, NH)),
         ("hre_prompt", (1, 1, NG, NP)), ("him_prompt", (1, 1, NG, NP)),
         ("k_sample", (1, 1, DEC, NH, HD)), ("v_sample", (1, 1, DEC, NH, HD)), ("logf_sample", (1, 1, DEC, NH)),
         ("hre_sample", (1, 1, NG, NP)), ("him_sample", (1, 1, NG, NP))]


def kernel(**inputs):
    import numpy as _np
    import concourse.bacc as _bacc
    from concourse import mybir as _mybir
    from concourse.bass_utils import run_bass_kernel_spmd as _run

    nc = _bacc.Bacc("TRN2", target_bir_lowering=False, num_devices=1)
    arrays, args = {}, []
    for name in _INS:
        a = _np.ascontiguousarray(inputs[name])
        arrays[f"in_{name}"] = a
        args.append(nc.dram_tensor(f"in_{name}", a.shape, _mybir.dt.from_np(a.dtype), kind="ExternalInput").ap())
    for name, shape in _OUTS:
        args.append(nc.dram_tensor(f"out_{name}", shape, _mybir.dt.float32, kind="ExternalOutput").ap())
    build_kernel(nc, *args)
    r = _run(nc, [arrays], core_ids=[0])
    return tuple(r.results[0][f"out_{name}"] for name, _ in _OUTS)
```
